# Optimizing a Trainium2 kernel written in Bass

```python
import jax, jax.numpy as jnp
from jax import lax
import numpy as np

D_MODEL = 1024
BATCH = 1
SEQ = 1024
DEPTH = 1

CHUNK = 64
HEAD_DIM = 64
D_MIX = D_MODEL
DA = 3 * D_MIX // 8
DC = D_MIX // 4
DB = D_MIX - DA - DC
HA = DA // HEAD_DIM
HB = DB // HEAD_DIM
CONV_K = 4
LORA_W = 64
LORA_A = 64
LORA_G = 128
LORA_V = 32
RWKV_SIZES = (DB, DB, DB, LORA_W, LORA_A, LORA_G)
RWKV_COLS = sum(RWKV_SIZES)
S5_GC = 16
S5_G = DC // S5_GC
S5_P = 64
IN_SIZES = (DA, DA, DA, HA, HA, RWKV_COLS, DC)
IN_COLS = sum(IN_SIZES)
N_GROUPS = 4
EXPERTS_PER_GROUP = 8
N_EXPERTS = N_GROUPS * EXPERTS_PER_GROUP
TOP_K = 2
D_EXPERT = D_MODEL // 2
ROW_BLOCK = 128
NORM_EPS = 1e-6
HEAD_NORM_EPS = 1e-5
RWKV_GN_EPS = 64e-5
L2_EPS = 1e-12

IN_SPLITS = [int(s) for s in np.cumsum(IN_SIZES)[:-1]]
RWKV_SPLITS = [int(s) for s in np.cumsum(RWKV_SIZES)[:-1]]

kernel_name = 'hybrid_mlstm_rwkv7_s5_hmoe_adaln'

def rmsnorm(x, g):
    x32 = x.astype(jnp.float32)
    y = x32 * lax.rsqrt(jnp.mean(x32 * x32, axis=-1, keepdims=True) + NORM_EPS)
    return (y * g.astype(jnp.float32)).astype(x.dtype)

def head_layernorm(h, eps):
    mu = jnp.mean(h, axis=-1, keepdims=True)
    var = jnp.mean(jnp.square(h - mu), axis=-1, keepdims=True)
    return (h - mu) * lax.rsqrt(var + eps)

def causal_conv(x, w, b):
    k_len = w.shape[0]
    s_len = x.shape[1]
    xp = jnp.pad(x, ((0, 0), (k_len - 1, 0), (0, 0)))
    return sum(xp[:, j:j + s_len] * w[j] for j in range(k_len)) + b

def mlstm_mixer(qk_pre, v_pre, o_pre, i_pre, f_pre, conv_w, conv_b, w_q, w_k, b_i, b_f, norm_w):
    f32 = jnp.float32
    bsz, s_len, _ = v_pre.shape
    nc = s_len // CHUNK
    cx = jax.nn.silu(causal_conv(qk_pre, conv_w, conv_b)).reshape(bsz, s_len, HA, HEAD_DIM)
    q = jnp.einsum('bshd,hde->bshe', cx, w_q)
    k = jnp.einsum('bshd,hde->bshe', cx, w_k) * (HEAD_DIM ** -0.5)
    v = v_pre.reshape(bsz, s_len, HA, HEAD_DIM)

    def to_chunks(t):
        return t.astype(f32).reshape(bsz, nc, CHUNK, HA, HEAD_DIM).transpose(0, 3, 1, 2, 4)

    def gate_chunks(t):
        return t.astype(f32).reshape(bsz, nc, CHUNK, HA).transpose(0, 3, 1, 2)

    qc, kc, vc = to_chunks(q), to_chunks(k), to_chunks(v)
    ig = gate_chunks(i_pre + b_i)
    flog = jax.nn.log_sigmoid(gate_chunks(f_pre + b_f))
    bcum = jnp.cumsum(flog, axis=-1)
    gtot = bcum[..., -1]

    lw = gtot[..., None] - bcum + ig
    m_loc = jnp.max(lw, axis=-1)
    wloc = jnp.exp(lw - m_loc[..., None])
    c_loc = jnp.einsum('bhcsk,bhcsv->bhckv', kc * wloc[..., None], vc)
    n_loc = jnp.einsum('bhcs,bhcsk->bhck', wloc, kc)

    def step(carry, inp):
        c_prev, n_prev, m_prev = carry
        g_c, ml_c, cl_c, nl_c = inp
        m_new = jnp.maximum(g_c + m_prev, ml_c)
        a_old = jnp.exp(g_c + m_prev - m_new)
        a_loc = jnp.exp(ml_c - m_new)
        c_new = a_old[..., None, None] * c_prev + a_loc[..., None, None] * cl_c
        n_new = a_old[..., None] * n_prev + a_loc[..., None] * nl_c
        return (c_new, n_new, m_new), (c_prev, n_prev, m_prev)

    init = (jnp.zeros((bsz, HA, HEAD_DIM, HEAD_DIM), f32),
            jnp.zeros((bsz, HA, HEAD_DIM), f32),
            jnp.zeros((bsz, HA), f32))
    xs = tuple(jnp.moveaxis(t, 2, 0) for t in (gtot, m_loc, c_loc, n_loc))
    _, (c_st, n_st, m_st) = lax.scan(step, init, xs)
    c_st, n_st, m_st = (jnp.moveaxis(t, 0, 2) for t in (c_st, n_st, m_st))

    causal = jnp.tril(jnp.ones((CHUNK, CHUNK), dtype=bool))
    dmat = jnp.where(causal, bcum[..., :, None] - bcum[..., None, :] + ig[..., None, :], -jnp.inf)
    inter = bcum + m_st[..., None]
    m_t = jnp.maximum(inter, jnp.max(dmat, axis=-1))
    s_qk = jnp.einsum('bhctd,bhcsd->bhcts', qc, kc) * jnp.exp(dmat - m_t[..., None])
    w_inter = jnp.exp(inter - m_t)
    num = (w_inter[..., None] * jnp.einsum('bhctk,bhckv->bhctv', qc, c_st)
           + jnp.einsum('bhcts,bhcsv->bhctv', s_qk, vc))
    den = w_inter * jnp.einsum('bhctk,bhck->bhct', qc, n_st) + jnp.sum(s_qk, axis=-1)
    h = num / jnp.maximum(jnp.abs(den), jnp.exp(-m_t))[..., None]
    h = h.transpose(0, 2, 3, 1, 4).reshape(bsz, s_len, HA, HEAD_DIM)
    h = head_layernorm(h, HEAD_NORM_EPS).reshape(bsz, s_len, DA) * norm_w.astype(f32)
    return h * jax.nn.sigmoid(o_pre.astype(f32))

def rwkv7_mixer(p, mu, w0, w_up, a0, a_up, g_up, k_k, k_a, r_k, ln_w, ln_b,
                v_first=None, v0=None, v_dn=None, v_up=None):
    f32 = jnp.float32
    bsz, s_len, _ = p.shape
    prev = jnp.pad(p, ((0, 0), (1, 0), (0, 0)))[:, :s_len]
    p = p + mu * (prev - p)
    r, k, v, wd, ad, gd = jnp.split(p, RWKV_SPLITS, axis=-1)
    wlog = -jax.nn.softplus(-(w0 + jnp.tanh(wd) @ w_up).astype(f32)) - 0.5
    decay = jnp.exp(-jnp.exp(wlog))
    a = jax.nn.sigmoid((a0 + ad @ a_up).astype(f32))
    g = jax.nn.sigmoid(gd) @ g_up
    if v_first is None:
        v_first = v
    else:
        v = v + (v_first - v) * jax.nn.sigmoid(v0 + (v @ v_dn) @ v_up)

    def heads(t):
        return t.astype(f32).reshape(bsz, s_len, HB, HEAD_DIM)

    r_h, k_h, v_h, a_h, w_h = heads(r), heads(k), heads(v), heads(a), heads(decay)
    kk = k_h * k_k.astype(f32).reshape(HB, HEAD_DIM)
    kk = kk / jnp.maximum(jnp.sqrt(jnp.sum(kk * kk, axis=-1, keepdims=True)), L2_EPS)
    k_h = k_h * (1.0 + (a_h - 1.0) * k_a.astype(f32).reshape(HB, HEAD_DIM))

    def tm(t):
        return jnp.moveaxis(t, 1, 0)

    xs = (tm(r_h), tm(w_h), tm(k_h), tm(v_h), tm(-kk), tm(kk * a_h))

    def step(state, inp):
        r_t, w_t, k_t, v_t, a_t, b_t = inp
        sa = jnp.einsum('bhvk,bhk->bhv', state, a_t)
        state = (state * w_t[:, :, None, :] + sa[..., None] * b_t[:, :, None, :]
                 + v_t[..., None] * k_t[:, :, None, :])
        return state, jnp.einsum('bhvk,bhk->bhv', state, r_t)

    _, y = lax.scan(step, jnp.zeros((bsz, HB, HEAD_DIM, HEAD_DIM), f32), xs)
    y = jnp.moveaxis(y, 0, 1)
    y = head_layernorm(y, RWKV_GN_EPS).reshape(bsz, s_len, DB) * ln_w.astype(f32) + ln_b.astype(f32)
    bonus = jnp.sum(r_h * k_h * r_k.astype(f32), axis=-1, keepdims=True) * v_h
    y = (y + bonus.reshape(bsz, s_len, DB)) * g.astype(f32)
    return y, v_first

def _complex_affine_combine(e1, e2):
    a1r, a1i, b1r, b1i = e1
    a2r, a2i, b2r, b2i = e2
    return (a2r * a1r - a2i * a1i,
            a2r * a1i + a2i * a1r,
            a2r * b1r - a2i * b1i + b2r,
            a2r * b1i + a2i * b1r + b2i)

def s5_mixer(u, a_re, a_im, log_dt, b_re, b_im, c_re, c_im, d, glu_w, glu_b):
    f32 = jnp.float32
    bsz, s_len, _ = u.shape
    uf = u.astype(f32).reshape(bsz, s_len, S5_G, S5_GC)
    a_re = a_re.astype(f32)
    a_im = a_im.astype(f32)
    dt = jnp.exp(log_dt.astype(f32))[:, None]
    mag = jnp.exp(a_re * dt)
    ang = a_im * dt
    ab_re = mag * jnp.cos(ang)
    ab_im = mag * jnp.sin(ang)
    inv = 1.0 / (a_re * a_re + a_im * a_im)
    co_re = ((ab_re - 1.0) * a_re + ab_im * a_im) * inv
    co_im = (ab_im * a_re - (ab_re - 1.0) * a_im) * inv
    b_re = b_re.astype(f32)
    b_im = b_im.astype(f32)
    bb_re = co_re[..., None] * b_re - co_im[..., None] * b_im
    bb_im = co_re[..., None] * b_im + co_im[..., None] * b_re
    bu_re = jnp.einsum('gpc,bsgc->bsgp', bb_re, uf)
    bu_im = jnp.einsum('gpc,bsgc->bsgp', bb_im, uf)
    shape_a = (1, s_len, S5_G, S5_P)
    elems = (jnp.broadcast_to(ab_re, shape_a), jnp.broadcast_to(ab_im, shape_a), bu_re, bu_im)
    _, _, x_re, x_im = lax.associative_scan(_complex_affine_combine, elems, axis=1)
    y = (jnp.einsum('gcp,bsgp->bsgc', c_re.astype(f32), x_re)
         - jnp.einsum('gcp,bsgp->bsgc', c_im.astype(f32), x_im)
         + d.astype(f32).reshape(S5_G, S5_GC) * uf)
    y = jax.nn.gelu(y.reshape(bsz, s_len, DC))
    return y * jax.nn.sigmoid(y @ glu_w.astype(f32) + glu_b.astype(f32))

def hier_moe(h, w_rg, b_rg, w_re, b_re, w1, w3, w2):
    f32 = jnp.float32
    bsz, s_len, d = h.shape
    n_tok = bsz * s_len
    ht = h.reshape(n_tok, d)
    p_group = jax.nn.softmax((ht @ w_rg + b_rg).astype(f32), axis=-1)
    gp, gi = lax.top_k(p_group, 1)
    e_logits = (ht @ w_re + b_re).astype(f32).reshape(n_tok, N_GROUPS, EXPERTS_PER_GROUP)
    sel = jnp.take_along_axis(e_logits, gi[:, :, None], axis=1)[:, 0]
    ev, ei = lax.top_k(sel, TOP_K)
    wts = gp * jax.nn.softmax(ev, axis=-1)

    n_assign = n_tok * TOP_K
    eid = (gi * EXPERTS_PER_GROUP + ei).reshape(n_assign)
    tok = jnp.repeat(jnp.arange(n_tok, dtype=jnp.int32), TOP_K)
    wflat = wts.reshape(n_assign)
    order = jnp.argsort(eid)
    e_s, tok_s, w_s = eid[order], tok[order], wflat[order]
    counts = jnp.zeros((N_EXPERTS,), jnp.int32).at[eid].add(1)
    starts = jnp.cumsum(counts) - counts
    pcounts = (counts + ROW_BLOCK - 1) // ROW_BLOCK * ROW_BLOCK
    pends = jnp.cumsum(pcounts)
    pstarts = pends - pcounts
    dest = pstarts[e_s] + jnp.arange(n_assign, dtype=jnp.int32) - starts[e_s]
    n_rows = n_assign + N_EXPERTS * ROW_BLOCK
    n_blocks = n_rows // ROW_BLOCK
    row_tok = jnp.full((n_rows,), n_tok, jnp.int32).at[dest].set(tok_s)
    row_w = jnp.zeros((n_rows,), f32).at[dest].set(w_s)
    blk_e = jnp.minimum(jnp.searchsorted(pends, jnp.arange(n_blocks, dtype=jnp.int32) * ROW_BLOCK,
                                         side='right'), N_EXPERTS - 1).astype(jnp.int32)
    x_pad = jnp.concatenate([ht, jnp.zeros((1, d), ht.dtype)], axis=0)
    xr = x_pad[row_tok].reshape(n_blocks, ROW_BLOCK, d)

    def expert_block(args):
        xb, e = args
        return (jax.nn.silu(xb @ w1[e]) * (xb @ w3[e])) @ w2[e]

    yr = lax.map(expert_block, (xr, blk_e)).reshape(n_rows, d)
    out = jnp.zeros((n_tok + 1, d), yr.dtype).at[row_tok].add(yr * row_w[:, None].astype(yr.dtype))
    return out[:n_tok].reshape(bsz, s_len, d)

def setup_inputs(seed: int = 0) -> dict:
    key = jax.random.key(seed)
    ks = iter(jax.random.split(key, 64))
    f32 = jnp.float32

    def nrm(shape, scale):
        return scale * jax.random.normal(next(ks), shape, f32)

    def unif(shape, lo, hi):
        return jax.random.uniform(next(ks), shape, f32, lo, hi)

    L = DEPTH
    LV = DEPTH - 1
    return {
        'x': nrm((BATCH, SEQ, D_MODEL), 1.0),
        'c': nrm((BATCH, D_MODEL), 1.0),
        'ada_w': nrm((L, D_MODEL, 6 * D_MODEL), 0.1 * D_MODEL ** -0.5),
        'ada_b': nrm((L, 6 * D_MODEL), 0.02),
        'norm_mix': 1.0 + nrm((L, D_MODEL), 0.02),
        'norm_ffn': 1.0 + nrm((L, D_MODEL), 0.02),
        'norm_final': 1.0 + nrm((D_MODEL,), 0.02),
        'w_in': nrm((L, D_MODEL, IN_COLS), D_MODEL ** -0.5),
        'w_out': nrm((L, D_MIX, D_MODEL), D_MIX ** -0.5),
        'mlstm_conv_w': nrm((L, CONV_K, DA), CONV_K ** -0.5),
        'mlstm_conv_b': nrm((L, DA), 0.02),
        'mlstm_w_q': nrm((L, HA, HEAD_DIM, HEAD_DIM), HEAD_DIM ** -0.5),
        'mlstm_w_k': nrm((L, HA, HEAD_DIM, HEAD_DIM), HEAD_DIM ** -0.5),
        'mlstm_b_i': nrm((L, HA), 0.1),
        'mlstm_b_f': jnp.linspace(3.0, 6.0, HA, dtype=f32)[None, :] + nrm((L, HA), 0.1),
        'mlstm_norm_w': 1.0 + nrm((L, DA), 0.02),
        'rwkv_mu': unif((L, RWKV_COLS), 0.0, 1.0),
        'rwkv_w0': jnp.linspace(-6.0, 1.0, DB, dtype=f32)[None, :] + nrm((L, DB), 0.1),
        'rwkv_w_up': nrm((L, LORA_W, DB), 0.1),
        'rwkv_a0': nrm((L, DB), 0.1),
        'rwkv_a_up': nrm((L, LORA_A, DB), 0.5 * LORA_A ** -0.5),
        'rwkv_g_up': nrm((L, LORA_G, DB), LORA_G ** -0.5),
        'rwkv_k_k': 0.85 + nrm((L, DB), 0.02),
        'rwkv_k_a': 1.0 + nrm((L, DB), 0.02),
        'rwkv_r_k': nrm((L, HB, HEAD_DIM), 0.1),
        'rwkv_ln_w': 1.0 + nrm((L, DB), 0.02),
        'rwkv_ln_b': nrm((L, DB), 0.02),
        'rwkv_v0': 1.0 + nrm((LV, DB), 0.1),
        'rwkv_v_dn': nrm((LV, DB, LORA_V), DB ** -0.5),
        'rwkv_v_up': nrm((LV, LORA_V, DB), 0.1 * LORA_V ** -0.5),
        's5_a_re': -0.5 + nrm((L, S5_G, S5_P), 0.01),
        's5_a_im': jnp.pi * jnp.arange(S5_P, dtype=f32) + nrm((L, S5_G, S5_P), 0.01),
        's5_log_dt': unif((L, S5_G), float(np.log(1e-3)), float(np.log(1e-1))),
        's5_b_re': nrm((L, S5_G, S5_P, S5_GC), (2 * S5_GC) ** -0.5),
        's5_b_im': nrm((L, S5_G, S5_P, S5_GC), (2 * S5_GC) ** -0.5),
        's5_c_re': nrm((L, S5_G, S5_GC, S5_P), S5_P ** -0.5),
        's5_c_im': nrm((L, S5_G, S5_GC, S5_P), S5_P ** -0.5),
        's5_d': nrm((L, DC), 1.0),
        's5_glu_w': nrm((L, DC, DC), DC ** -0.5),
        's5_glu_b': nrm((L, DC), 0.02),
        'moe_w_rg': nrm((L, D_MODEL, N_GROUPS), D_MODEL ** -0.5),
        'moe_b_rg': nrm((L, N_GROUPS), 0.01),
        'moe_w_re': nrm((L, D_MODEL, N_EXPERTS), D_MODEL ** -0.5),
        'moe_b_re': nrm((L, N_EXPERTS), 0.01),
        'moe_w1': nrm((L, N_EXPERTS, D_MODEL, D_EXPERT), D_MODEL ** -0.5),
        'moe_w3': nrm((L, N_EXPERTS, D_MODEL, D_EXPERT), D_MODEL ** -0.5),
        'moe_w2': nrm((L, N_EXPERTS, D_EXPERT, D_MODEL), D_EXPERT ** -0.5),
    }

def reference(x, c, ada_w, ada_b, norm_mix, norm_ffn, norm_final, w_in, w_out,
              mlstm_conv_w, mlstm_conv_b, mlstm_w_q, mlstm_w_k, mlstm_b_i, mlstm_b_f, mlstm_norm_w,
              rwkv_mu, rwkv_w0, rwkv_w_up, rwkv_a0, rwkv_a_up, rwkv_g_up, rwkv_k_k, rwkv_k_a,
              rwkv_r_k, rwkv_ln_w, rwkv_ln_b, rwkv_v0, rwkv_v_dn, rwkv_v_up,
              s5_a_re, s5_a_im, s5_log_dt, s5_b_re, s5_b_im, s5_c_re, s5_c_im, s5_d,
              s5_glu_w, s5_glu_b,
              moe_w_rg, moe_b_rg, moe_w_re, moe_b_re, moe_w1, moe_w3, moe_w2):
    out_dtype = x.dtype
    cond = jax.nn.silu(c)
    v_first = None
    for l in range(DEPTH):
        mod = (cond @ ada_w[l] + ada_b[l])[:, None, :]
        sh1, sc1, gt1, sh2, sc2, gt2 = jnp.split(mod, 6, axis=-1)

        h = rmsnorm(x, norm_mix[l]) * (1.0 + sc1) + sh1
        proj = h @ w_in[l]
        a_qk, a_v, a_o, a_i, a_f, b_cols, c_u = jnp.split(proj, IN_SPLITS, axis=-1)
        y_a = mlstm_mixer(a_qk, a_v, a_o, a_i, a_f, mlstm_conv_w[l], mlstm_conv_b[l],
                          mlstm_w_q[l], mlstm_w_k[l], mlstm_b_i[l], mlstm_b_f[l], mlstm_norm_w[l])
        if l == 0:
            y_b, v_first = rwkv7_mixer(b_cols, rwkv_mu[l], rwkv_w0[l], rwkv_w_up[l], rwkv_a0[l],
                                       rwkv_a_up[l], rwkv_g_up[l], rwkv_k_k[l], rwkv_k_a[l],
                                       rwkv_r_k[l], rwkv_ln_w[l], rwkv_ln_b[l])
        else:
            y_b, _ = rwkv7_mixer(b_cols, rwkv_mu[l], rwkv_w0[l], rwkv_w_up[l], rwkv_a0[l],
                                 rwkv_a_up[l], rwkv_g_up[l], rwkv_k_k[l], rwkv_k_a[l],
                                 rwkv_r_k[l], rwkv_ln_w[l], rwkv_ln_b[l],
                                 v_first, rwkv_v0[l - 1], rwkv_v_dn[l - 1], rwkv_v_up[l - 1])
        y_c = s5_mixer(c_u, s5_a_re[l], s5_a_im[l], s5_log_dt[l], s5_b_re[l], s5_b_im[l],
                       s5_c_re[l], s5_c_im[l], s5_d[l], s5_glu_w[l], s5_glu_b[l])
        mixed = jnp.concatenate([y_a.astype(h.dtype), y_b.astype(h.dtype), y_c.astype(h.dtype)],
                                axis=-1) @ w_out[l]
        x = x + (1.0 + gt1) * mixed

        h = rmsnorm(x, norm_ffn[l]) * (1.0 + sc2) + sh2
        x = x + (1.0 + gt2) * hier_moe(h, moe_w_rg[l], moe_b_rg[l], moe_w_re[l], moe_b_re[l],
                                       moe_w1[l], moe_w3[l], moe_w2[l])
    return rmsnorm(x, norm_final).astype(out_dtype)


_drawn_inputs = setup_inputs


def setup_inputs(seed=0):
    import zlib

    import numpy as np

    out = dict(_drawn_inputs(seed))
    spreads = {}
    factors = {'norm_final': 7.474,
     'mlstm_conv_b': 3.012,
     'mlstm_b_i': 64.0,
     'mlstm_norm_w': 9.738,
     'rwkv_k_k': 15.83,
     'rwkv_k_a': 3.439,
     'rwkv_ln_w': 10.182,
     'rwkv_ln_b': 10.999,
     's5_a_re': 64.0,
     's5_b_re': 2.845,
     's5_c_re': 8.599,
     's5_c_im': 8.469,
     's5_glu_b': 37.64,
     'moe_b_rg': 15.781,
     'moe_b_re': 12.219,
     'norm_ffn': 3.209,
     's5_b_im': 6.227}
    for name, (base, spread) in spreads.items():
        noise = np.random.default_rng([zlib.crc32(name.encode()), seed]).standard_normal(out[name].shape)
        drawn = base * np.exp(spread * noise) if base else spread * noise
        out[name] = __import__('jax').numpy.asarray(drawn.astype(out[name].dtype))
    for name, factor in factors.items():
        out[name] = (out[name] * factor).astype(out[name].dtype)
    return out
```

```python
from contextlib import ExitStack, contextmanager

import numpy as np

import concourse.bass as bass
from concourse import mybir

F32 = mybir.dt.float32
I32 = mybir.dt.int32
ALU = mybir.AluOpType
ACT = mybir.ActivationFunctionType
AX = mybir.AxisListType

P = 128
D = 1024
S = 1024
KT = D // P
NT = S // P
HD = 64
DA, DB, DC = 384, 384, 256
HA, HB = DA // HD, DB // HD
QA = DA // P
QB = DB // P
CONV_K = 4
C_QK, C_VO, C_R, C_LORA, C_U = 0, DA, 3 * DA + 2 * HA, 3 * DA + 2 * HA + 3 * DB, 3 * DA + 2 * HA + 3 * DB + 256
VO = 2 * DA + 2 * HA
IN_COLS = C_U + DC
G5, P5, GC = 16, 64, 16
QS = G5 // 2
J5, M5 = 16, S // 16
NG, EPG, NE = 4, 8, 32
DE = 512
MAXBLK = 48
SLOTS = MAXBLK * P
BIG = 1.0e30
NORM_EPS, HEAD_EPS, GN_EPS = 1e-6, 1e-5, 64e-5
RWKV_DECAY = -0.5 * float(np.exp(-0.5))

COLS = {}
_n = 0
for _name, _w in (("c", KT), ("conv_w", QA * CONV_K), ("conv_b", QA), ("mu", 11), ("w0", QB), ("a0", QB),
                  ("k_k", QB), ("k_a", QB), ("r_k", QB), ("a_re", QS), ("a_im", QS), ("log_dt", QS),
                  ("d5", 2), ("glu_b", 2), ("b_i", 1), ("b_f", 1)):
    COLS[_name] = (_n, _n + _w)
    _n += _w
NCOLS = _n


class Chain:

    def __init__(self, eng, sem):
        self.eng, self.sem, self.n = eng, sem, 0

    def add(self, ins):
        ins.then_inc(self.sem, 1)
        self.n += 1

    def sync(self):
        if self.n:
            self.eng.wait_ge(self.sem, self.n)

    def link(self, ins):
        self.add(ins)
        self.sync()


@contextmanager
def phase_semaphores(nc):
    taken = []

    def sem(name):
        taken.append(nc.alloc_semaphore(name))
        return taken[-1]

    yield sem
    nc.clear_and_free_semaphores(taken)
    nc.all_engine_barrier()


def col(t, name, i=0, n=1):
    a = COLS[name][0] + i
    return t["cols"][:, a:a + n]


def phase_norm1(nc, t, io):
    ps = t["ps"]
    with ExitStack() as ctx:
        sb = lambda n, s, d=F32: ctx.enter_context(nc.sbuf_tensor(n, s, d))
        sem = ctx.enter_context(phase_semaphores(nc))
        ring = sb("ada_ring", [P, 3, KT * 512])
        xs = sb("n1_x", [P, NT, D])
        h = sb("n1_h", [P, 2, D])
        junk = sb("n1_junk", [P, D])
        mod = sb("n1_mod", [P, 2, D])
        scale = sb("n1_scale", [P, D])
        ss = sb("n1_ss", [P, NT])
        rstd = sb("n1_rstd", [P, NT])
        const_in, x_in = sem("n1_const_in"), [sem(f"n1_x_in{i}") for i in range(4)]
        w_in = [sem(f"n1_ada_in{i}") for i in range(3)]
        cond_tanh, cond_ready = sem("n1_cond_tanh"), sem("n1_cond_ready")
        mod_done, mod_taken = sem("n1_mod_done"), sem("n1_mod_taken")
        sums_ready, var_ready, root_ready = sem("n1_sums"), sem("n1_var"), sem("n1_root")
        h_ready, tr_done, tr_taken = sem("n1_h_ready"), sem("n1_tr_done"), sem("n1_tr_taken")
        dve_c, = [sem("n1_dve")]
        ada = io["ada_w"].rearrange("o (k p) n -> p (o k) n", p=P)
        x = io["x"].rearrange("b (i p) d -> p (b i) d", p=P)
        with nc.Block() as block:
            @block.sync
            def _(sp):
                sp.dma_start(t["cols"][:, :], io["cols"]).then_inc(const_in, 16)
                sp.dma_start(t["ident"][:, :], io["ident"]).then_inc(const_in, 16)
                sp.dma_start(mod[:, :, :], io["rows_mod"][:, 0:2 * D].rearrange("p (a d) -> p a d", a=2)
                             ).then_inc(const_in, 16)
                sp.dma_start(scale[:, :], io["rows_norm"][:, 0:D]).then_inc(const_in, 16)
                for n in range(4):
                    if n >= 3:
                        sp.wait_ge(mod_done, n - 2)
                    sp.dma_start(ring[:, n % 3, :].rearrange("p (k n) -> p k n", k=KT),
                                 ada[:, :, n * 512:(n + 1) * 512]).then_inc(w_in[n % 3], 16)
                    sp.dma_start(xs[:, 2 * n:2 * n + 2, :], x[:, 2 * n:2 * n + 2, :]).then_inc(x_in[n], 16)

            @block.scalar
            def _(act):
                act.wait_ge(const_in, 64)
                nc.scalar.activation(t["cond"][:, :], col(t, "c", 0, KT), ACT.Tanh, scale=0.5).then_inc(cond_tanh, 1)
                for i in range(NT):
                    act.wait_ge(x_in[i // 2], 16)
                    if i:
                        act.wait_ge(sums_ready, i)
                    nc.scalar.activation(junk[:, :], xs[:, i, :], ACT.Square,
                                         accum_out=ss[:, i:i + 1]).then_inc(sums_ready, 1)
                act.wait_ge(var_ready, 1)
                nc.scalar.activation(rstd[:, :], ss[:, :], ACT.Sqrt).then_inc(root_ready, 1)
                for g in range(2 * NT):
                    i, half = divmod(g, 2)
                    act.wait_ge(tr_done, g + 1)
                    nc.scalar.activation(t["hT"][:, 4 * half:4 * half + 4, i * P:(i + 1) * P],
                                         ps[4 + g % 4][:, :].rearrange("p (k n) -> p k n", k=4),
                                         ACT.Copy).then_inc(tr_taken, 1)

            @block.vector
            def _(dve):
                ch = Chain(dve, dve_c)
                dve.wait_ge(cond_tanh, 1)
                ch.link(dve.scalar_tensor_tensor(t["cond"][:, :], t["cond"][:, :], 1.0, col(t, "c", 0, KT),
                                                 ALU.add, ALU.mult))
                ch.link(dve.memset(t["cond_bc"][:, :, :], 0.5))
                for k in range(KT):
                    last = dve.tensor_scalar(t["cond_bc"][:, k, :], t["cond_bc"][:, k, :], t["cond"][:, k:k + 1], None,
                                             ALU.mult)
                    ch.add(last)
                ch.sync()
                dve.sem_inc(cond_ready, 1)
                for n in range(4):
                    dve.wait_ge(mod_done, n + 1)
                    part = mod[:, n // 2, (n % 2) * 512:(n % 2) * 512 + 512]
                    ins = dve.tensor_tensor(part, ps[n % 2][:, :], part, ALU.add)
                    ins.then_inc(mod_taken, 1)
                dve.wait_ge(mod_taken, 4)
                ch.link(dve.scalar_tensor_tensor(scale[:, :], mod[:, 1, :], 1.0, scale[:, :], ALU.add, ALU.mult))
                dve.wait_ge(sums_ready, NT)
                dve.tensor_scalar(ss[:, :], ss[:, :], 1.0 / D, NORM_EPS, ALU.mult, ALU.add).then_inc(var_ready, 1)
                dve.wait_ge(root_ready, 1)
                ch.link(dve.reciprocal(rstd[:, :], rstd[:, :]))
                for i in range(NT):
                    if i >= 2:
                        dve.wait_ge(tr_done, 2 * (i - 1))
                    ch.link(dve.scalar_tensor_tensor(h[:, i % 2, :], xs[:, i, :], rstd[:, i:i + 1], scale[:, :],
                                                     ALU.mult, ALU.mult))
                    dve.tensor_tensor(h[:, i % 2, :], h[:, i % 2, :], mod[:, 0, :], ALU.add).then_inc(h_ready, 1)

            @block.tensor
            def _(pe):
                pe.wait_ge(cond_ready, 1)
                for n in range(4):
                    pe.wait_ge(w_in[n % 3], 16 * (n // 3 + 1))
                    if n >= 2:
                        pe.wait_ge(mod_taken, n - 1)
                    w = ring[:, n % 3, :].rearrange("p (k n) -> p k n", k=KT)
                    for k in range(KT):
                        last = nc.tensor.matmul(ps[n % 2][:, :], t["cond_bc"][:, k, :], w[:, k, :],
                                                start=(k == 0), stop=(k == KT - 1))
                    last.then_inc(mod_done, 1)
                for g in range(2 * NT):
                    i, half = divmod(g, 2)
                    pe.wait_ge(h_ready, i + 1)
                    if g >= 4:
                        pe.wait_ge(tr_taken, g - 3)
                    for k in range(4):
                        a = (4 * half + k) * P
                        last = nc.tensor.transpose(ps[4 + g % 4][:, k * P:(k + 1) * P], h[:, i % 2, a:a + P],
                                                   t["ident"][:, :])
                    last.then_inc(tr_done, 1)


def phase_a(nc, t, io):
    ps = t["ps"]
    with ExitStack() as ctx:
        sb = lambda n, s, d=F32: ctx.enter_context(nc.sbuf_tensor(n, s, d))
        sem = ctx.enter_context(phase_semaphores(nc))
        ring = sb("pa_ring", [P, 2, KT, 384])
        uT = sb("pa_u", [P, 2, S])
        braw = sb("pa_b", [P, 4, QS * 32])
        bb = sb("pa_bb", [P, 2, QS * 32])
        bbT = sb("pa_bbT", [P, 2, 2, P])
        co = sb("pa_co", [P, 16, QS])
        coi = sb("pa_coi", [P, QS], I32)
        pw = sb("pa_pw", [P, 3, QS, J5])
        kp = sb("pa_kp", [P, 3, 6, QS])
        tq = sb("pa_tq", [P, 2, QS, 8])
        tb = sb("pa_tb", [P, 2, QS * 32])
        xs = sb("pa_x", [P, 2, 2, S])
        ebuf = sb("pa_e", [P, 2, 2, 32 + M5])
        etmp = sb("pa_et", [P, 2, M5])
        w_in = [sem(f"pa_w_in{i}") for i in range(2)]
        small_in = sem("pa_small_in")
        proj_done, proj_taken = sem("pa_proj_done"), sem("pa_proj_taken")
        dt_ready, act_dt, ang_ready, act_sin = sem("pa_dt"), sem("pa_actdt"), sem("pa_ang"), sem("pa_sin")
        bb_ready, bbt_done, bbt_taken = sem("pa_bb_ready"), sem("pa_bbt_done"), sem("pa_bbt_taken")
        bu_done, bu_taken = sem("pa_bu_done"), sem("pa_bu_taken")
        x_ready, y_done, y_taken = sem("pa_x_ready"), sem("pa_y_done"), sem("pa_y_taken")
        dve_c, act_c, pads = sem("pa_dve"), sem("pa_act"), sem("pa_pads")
        w = io["w_in"].rearrange("o (k p) n -> p (o k) n", p=P)
        blocks = [(C_U, 2), (C_R, 3), (C_R + DB, 3), (C_R + 2 * DB, 3), (C_LORA, 2)]
        tiles = [(b, m) for b, (_, n) in enumerate(blocks) for m in range(n)]
        prev_tiles = [sum(n for _, n in blocks[:b]) for b in range(len(blocks))]

        def dest(mt, half):
            if mt < 2:
                return uT[:, mt, half * 512:(half + 1) * 512]
            return t["pB"][:, mt - 2, 1 + half * 512:1 + (half + 1) * 512]

        bu_after = {2: 0, 3: 1}
        y_after = {5: [0], 6: [1], 8: [2], 9: [3], 11: [4], 12: [5, 6, 7]}

        def take_y(dve, ch, q):
            r = slice(32 * (q % 4), 32 * (q % 4) + 32)
            dve.wait_ge(y_done, q + 1)
            for half in range(2):
                n = slice(half * 512, half * 512 + 512)
                ins = nc.vector.scalar_tensor_tensor(t["ycT"][r, q // 4, n], uT[r, q // 4, n],
                                                     col(t, "d5", q // 4)[r, :],
                                                     ps[2 + half][r, :], ALU.mult, ALU.add)
            ins.then_inc(y_taken, 1)

        with nc.Block() as block:
            @block.sync
            def _(sp):
                sp.dma_start(braw[:, :, :], io["s5_bc"]).then_inc(small_in, 16)
                for b, (c0, n) in enumerate(blocks):
                    if b >= 2:
                        sp.wait_ge(proj_done, 2 * prev_tiles[b - 1])
                    sp.dma_start(ring[:, b % 2, :, 0:n * P], w[:, :, c0:c0 + n * P]).then_inc(w_in[b % 2], 16)

            @block.gpsimd
            def _(pool):
                nc.gpsimd.memset(t["pB"][:, :, 0:1], 0.0).then_inc(pads, 1)
                nc.gpsimd.memset(ebuf[:, :, :, :], 0.0).then_inc(pads, 1)

            @block.scalar
            def _(act):
                nc.scalar.activation(co[:, 0, :], col(t, "log_dt", 0, QS), ACT.Exp).then_inc(act_dt, 1)
                act.wait_ge(dt_ready, 1)
                nc.scalar.activation(co[:, 2, :], co[:, 1, :], ACT.Exp).then_inc(act_dt, 1)
                act.wait_ge(ang_ready, 1)
                nc.scalar.activation(co[:, 5, :], co[:, 5, :], ACT.Sin).then_inc(act_sin, 1)
                nc.scalar.activation(co[:, 6, :], co[:, 6, :], ACT.Sin).then_inc(act_sin, 1)

                def take_bu(q):
                    for part in range(4):
                        act.wait_ge(bu_done, 4 * q + part + 1)
                        if q >= 2 and part == 0:
                            act.wait_ge(y_done, q - 1)
                        nc.scalar.activation(xs[:, q % 2, part // 2, (part % 2) * 512:(part % 2) * 512 + 512],
                                             ps[4 + part][:, :], ACT.Copy).then_inc(bu_taken, 1)

                for mt in range(len(tiles)):
                    for half in range(2):
                        g = 2 * mt + half
                        act.wait_ge(proj_done, g + 1)
                        nc.scalar.activation(dest(mt, half), ps[g % 2][:, :], ACT.Copy).then_inc(proj_taken, 1)
                    if mt == 1:
                        act.wait_ge(bbt_done, 1)
                        nc.scalar.activation(bbT[:, :, :, :].rearrange("p a b n -> p (a b n)"), ps[4][:, :],
                                             ACT.Copy).then_inc(bbt_taken, 1)
                    if mt in bu_after:
                        take_bu(bu_after[mt])
                    for q in y_after.get(mt, []):
                        if q + 2 < QS:
                            take_bu(q + 2)

            @block.vector
            def _(dve):
                ch = Chain(dve, dve_c)
                V = nc.vector
                tt = lambda o, a, b, op: ch.add(V.tensor_tensor(o, a, b, op))
                LT = lambda o, a, b, op: ch.link(V.tensor_tensor(o, a, b, op))
                are, aim = col(t, "a_re", 0, QS), col(t, "a_im", 0, QS)
                dve.wait_ge(act_dt, 1)
                V.tensor_tensor(co[:, 1, :], are, co[:, 0, :], ALU.mult).then_inc(dt_ready, 1)
                LT(co[:, 3, :], aim, co[:, 0, :], ALU.mult)
                ch.link(V.tensor_scalar(co[:, 4, :], co[:, 3, :], float(1 / (2 * np.pi)), None, ALU.mult))
                ch.link(V.tensor_copy(coi[:, :], co[:, 4, :]))
                ch.link(V.tensor_copy(co[:, 4, :], coi[:, :]))
                ch.link(V.scalar_tensor_tensor(co[:, 3, :], co[:, 4, :], -6.28125, co[:, 3, :], ALU.mult, ALU.add))
                ch.link(V.scalar_tensor_tensor(co[:, 3, :], co[:, 4, :], -float(2 * np.pi - 6.28125), co[:, 3, :],
                                               ALU.mult, ALU.add))

                def wrap(x, tmp):
                    ch.link(V.tensor_scalar(tmp, x, float(np.pi), -float(2 * np.pi), ALU.is_gt, ALU.mult))
                    LT(x, x, tmp, ALU.add)
                    ch.link(V.tensor_scalar(tmp, x, -float(np.pi), float(2 * np.pi), ALU.is_lt, ALU.mult))
                    LT(x, x, tmp, ALU.add)

                wrap(co[:, 3, :], co[:, 4, :])
                ch.link(V.tensor_scalar(co[:, 6, :], co[:, 3, :], float(np.pi / 2), None, ALU.add))
                wrap(co[:, 6, :], co[:, 4, :])
                lim = 3.1415925
                ch.link(V.tensor_scalar(co[:, 5, :], co[:, 3, :], lim, -lim, ALU.min, ALU.max))
                V.tensor_scalar(co[:, 6, :], co[:, 6, :], lim, -lim, ALU.min, ALU.max).then_inc(ang_ready, 1)
                dve.wait_ge(act_dt, 2)
                dve.wait_ge(act_sin, 2)
                tt(pw[:, 0, :, 0], co[:, 2, :], co[:, 6, :], ALU.mult)
                LT(pw[:, 1, :, 0], co[:, 2, :], co[:, 5, :], ALU.mult)
                tt(co[:, 7, :], are, are, ALU.mult)
                LT(co[:, 8, :], aim, aim, ALU.mult)
                LT(co[:, 7, :], co[:, 7, :], co[:, 8, :], ALU.add)
                ch.link(V.reciprocal(co[:, 7, :], co[:, 7, :]))
                ch.link(V.tensor_scalar(co[:, 8, :], pw[:, 0, :, 0], -1.0, None, ALU.add))
                tt(co[:, 9, :], co[:, 8, :], are, ALU.mult)
                tt(co[:, 10, :], pw[:, 1, :, 0], aim, ALU.mult)
                tt(co[:, 11, :], pw[:, 1, :, 0], are, ALU.mult)
                LT(co[:, 12, :], co[:, 8, :], aim, ALU.mult)
                tt(co[:, 9, :], co[:, 9, :], co[:, 10, :], ALU.add)
                LT(co[:, 11, :], co[:, 11, :], co[:, 12, :], ALU.subtract)
                tt(co[:, 9, :], co[:, 9, :], co[:, 7, :], ALU.mult)
                LT(co[:, 11, :], co[:, 11, :], co[:, 7, :], ALU.mult)
                dve.wait_ge(small_in, 16)

                def cmul(ore, oim, xre, xim, yre, yim, t0, t1):
                    tt(t0, xim, yim, ALU.mult)
                    LT(t1, xre, yim, ALU.mult)
                    tt(ore, xre, yre, ALU.mult)
                    LT(oim, xim, yre, ALU.mult)
                    tt(ore, ore, t0, ALU.subtract)
                    LT(oim, oim, t1, ALU.add)

                B3 = lambda a: a.rearrange("p (q c) -> p q c", q=QS)
                bc = lambda a, n: a.unsqueeze(2).broadcast_to([P, QS, n])
                cmul(B3(bb[:, 0, :]), B3(bb[:, 1, :]), B3(braw[:, 0, :]), B3(braw[:, 1, :]),
                     bc(co[:, 9, :], 32), bc(co[:, 11, :], 32), B3(tb[:, 0, :]), B3(tb[:, 1, :]))
                V.tensor_scalar(braw[:, 3, :], braw[:, 3, :], -1.0, None, ALU.mult).then_inc(bb_ready, 1)
                for n in (1, 2, 4, 8):
                    cmul(pw[:, 0, :, n:2 * n], pw[:, 1, :, n:2 * n], pw[:, 0, :, 0:n], pw[:, 1, :, 0:n],
                         bc(pw[:, 0, :, n - 1], n), bc(pw[:, 1, :, n - 1], n), tq[:, 0, :, 0:n], tq[:, 1, :, 0:n])
                ch.link(V.tensor_scalar(pw[:, 2, :, :], pw[:, 1, :, :], -1.0, None, ALU.mult))
                ch.add(V.tensor_copy(kp[:, 0, 0, :], pw[:, 0, :, J5 - 1]))
                ch.link(V.tensor_copy(kp[:, 1, 0, :], pw[:, 1, :, J5 - 1]))
                for l in range(1, 6):
                    a, b = kp[:, 0, l - 1, :], kp[:, 1, l - 1, :]
                    cmul(kp[:, 0, l, :], kp[:, 1, l, :], a, b, a, b, co[:, 14, :], co[:, 15, :])
                ch.link(V.tensor_scalar(kp[:, 2, :, :], kp[:, 1, :, :], -1.0, None, ALU.mult))

                def stt(o, a, s, b):
                    ch.add(V.scalar_tensor_tensor(o, a, s, b, ALU.mult, ALU.add))

                dve.wait_ge(pads, 2)
                for q in range(QS):
                    dve.wait_ge(bu_taken, 4 * (q + 1))
                    re = xs[:, q % 2, 0, :].rearrange("p (m j) -> p j m", j=J5)
                    im = xs[:, q % 2, 1, :].rearrange("p (m j) -> p j m", j=J5)
                    A = lambda k: pw[:, k, q, 0:1]
                    for j in range(1, J5):
                        stt(re[:, j, :], re[:, j - 1, :], A(0), re[:, j, :])
                        stt(im[:, j, :], im[:, j - 1, :], A(0), im[:, j, :])
                        ch.sync()
                        stt(re[:, j, :], im[:, j - 1, :], A(2), re[:, j, :])
                        stt(im[:, j, :], re[:, j - 1, :], A(1), im[:, j, :])
                        ch.sync()
                    E = lambda s, c, off: ebuf[:, s, c, 32 - off:32 - off + M5]
                    ch.add(V.tensor_copy(E(0, 0, 0), re[:, J5 - 1, :]))
                    ch.link(V.tensor_copy(E(0, 1, 0), im[:, J5 - 1, :]))
                    for l in range(6):
                        a, b, d = l % 2, 1 - l % 2, 1 << l
                        K = lambda k: kp[:, k, l, q:q + 1]
                        stt(etmp[:, 0, :], E(a, 0, d), K(0), E(a, 0, 0))
                        stt(etmp[:, 1, :], E(a, 1, d), K(0), E(a, 1, 0))
                        ch.sync()
                        stt(E(b, 0, 0), E(a, 1, d), K(2), etmp[:, 0, :])
                        stt(E(b, 1, 0), E(a, 0, d), K(1), etmp[:, 1, :])
                        ch.sync()
                    for j in range(J5):
                        stt(re[:, j, :], E(0, 0, 1), pw[:, 0, q, j:j + 1], re[:, j, :])
                        stt(im[:, j, :], E(0, 1, 1), pw[:, 0, q, j:j + 1], im[:, j, :])
                    ch.sync()
                    for j in range(J5):
                        stt(re[:, j, :], E(0, 1, 1), pw[:, 2, q, j:j + 1], re[:, j, :])
                        stt(im[:, j, :], E(0, 0, 1), pw[:, 1, q, j:j + 1], im[:, j, :])
                    ch.sync()
                    dve.sem_inc(x_ready, 1)
                    if q >= 1:
                        take_y(dve, ch, q - 1)
                take_y(dve, ch, QS - 1)

            @block.tensor
            def _(pe):
                def bu(q):
                    r = slice(32 * (q % 4), 32 * (q % 4) + 32)
                    for part in range(4):
                        c, half = divmod(part, 2)
                        if q == 0 and part == 0:
                            pe.wait_ge(bbt_taken, 1)
                            pe.wait_ge(proj_taken, 4)
                        if q:
                            pe.wait_ge(bu_taken, 4 * (q - 1) + part + 1)
                        nc.tensor.matmul(ps[4 + part][:, :], bbT[r, q // 4, c, :],
                                         uT[r, q // 4, half * 512:half * 512 + 512], start=True, stop=True
                                         ).then_inc(bu_done, 1)

                def y(q):
                    r = slice(32 * (q % 4), 32 * (q % 4) + 32)
                    pe.wait_ge(x_ready, q + 1)
                    if q:
                        pe.wait_ge(y_taken, q)
                    for half in range(2):
                        for c in range(2):
                            last = nc.tensor.matmul(ps[2 + half][r, :], braw[:, 2 + c, 32 * q:32 * q + 32],
                                                    xs[:, q % 2, c, half * 512:half * 512 + 512],
                                                    start=(c == 0), stop=(c == 1))
                    last.then_inc(y_done, 1)

                for mt, (b, m) in enumerate(tiles):
                    if m == 0:
                        pe.wait_ge(w_in[b % 2], 16 * (b // 2 + 1))
                    for half in range(2):
                        g = 2 * mt + half
                        if g >= 2:
                            pe.wait_ge(proj_taken, g - 1)
                        for k in range(KT):
                            last = nc.tensor.matmul(ps[g % 2][:, :], ring[:, b % 2, k, m * P:(m + 1) * P],
                                                    t["hT"][:, k, half * 512:half * 512 + 512],
                                                    start=(k == 0), stop=(k == KT - 1))
                        last.then_inc(proj_done, 1)
                    if mt == 1:
                        pe.wait_ge(bb_ready, 1)
                        for a in range(2):
                            for c in range(2):
                                last = nc.tensor.transpose(ps[4][:, (2 * a + c) * P:(2 * a + c + 1) * P],
                                                           bb[:, c, a * P:(a + 1) * P], t["ident"][:, :])
                        last.then_inc(bbt_done, 1)
                    if mt in bu_after:
                        bu(bu_after[mt])
                    for q in y_after.get(mt, []):
                        y(q)
                        if q + 2 < QS:
                            bu(q + 2)


def phase_b(nc, t, io):
    ps = t["ps"]
    pB, at, bt, bonus, ec = t["pB"], t["a_til"], t["b_hat"], t["bonus"], t["chunk_decay"]
    with ExitStack() as ctx:
        sb = lambda n, s, d=F32: ctx.enter_context(nc.sbuf_tensor(n, s, d, side="right"))
        sem = ctx.enter_context(phase_semaphores(nc))
        ring = sb("pb_ring", [P, 2, KT, VO // 2])
        lora = sb("pb_lora", [P, DB])
        gluw = sb("pb_glu", [P, 2, DC])
        cst = sb("pb_cst", [P, P + 2])
        hcol = sb("pb_hcol", [P, 3, QB])
        T = sb("pb_t", [P, 5, S])
        w_in_s = [sem(f"pb_w_in{i}") for i in range(2)]
        small_in = sem("pb_small_in")
        proj_done, proj_taken = sem("pb_proj_done"), sem("pb_proj_taken")
        seg_ready, lora_ready, lora_tanh = sem("pb_seg"), sem("pb_lora_ready"), sem("pb_lora_tanh")
        z_done, z_taken = sem("pb_z_done"), sem("pb_z_taken")
        ell_ready, exps = sem("pb_ell_ready"), sem("pb_exps")
        kk_ready, sq_ready, ss_done, ss_taken, root = (sem("pb_kk"), sem("pb_sq"), sem("pb_ss_done"),
                                                       sem("pb_ss_taken"), sem("pb_root"))
        rk_ready, bon_done, bon_taken, q_free = sem("pb_rk"), sem("pb_bon_done"), sem("pb_bon_taken"), sem("pb_q_free")
        g_sq, g_in, g_tanh, z2_ready = sem("pb_gsq"), sem("pb_gin"), sem("pb_gtanh"), sem("pb_z2")
        glu_done, glu_tanh = sem("pb_glu_done"), sem("pb_glu_tanh")
        dve_c = sem("pb_dve")
        w = io["w_in"].rearrange("o (k p) n -> p (o k) n", p=P)
        H = VO // 2
        blocks = [(C_QK, DA), (C_VO, H), (C_VO + H, H)]
        n_cm = 2 * QA
        tok_groups = [(i, hf) for hf in range(2) for i in range(NT)]

        with nc.Block() as block:
            @block.sync
            def _(sp):
                sp.dma_start(lora[:, :], io["lora"]).then_inc(small_in, 16)
                sp.dma_start(cst[:, :], io["rwkv_cst"]).then_inc(small_in, 16)
                sp.dma_start(gluw[:, :, :], io["glu_w"].rearrange("o (k p) n -> p (o k) n", p=P)).then_inc(small_in, 16)
                for b, (c0, n) in enumerate(blocks):
                    if b == 2:
                        sp.wait_ge(proj_done, n_cm)
                    sp.dma_start(ring[:, b % 2, :, 0:n], w[:, :, c0:c0 + n]).then_inc(w_in_s[b % 2], 16)

            @block.gpsimd
            def _(pool):
                nc.gpsimd.memset(t["qk"][:, :, 0:CONV_K - 1], 0.0)
                nc.gpsimd.memset(t["seg64"][:, :], 1.0).then_inc(seg_ready, 1)
                pool.wait_ge(seg_ready, 1)
                nc.gpsimd.memset(t["seg64"][:, 0::HD], 0.0).then_inc(seg_ready, 1)

            @block.scalar
            def _(act):
                A = nc.scalar.activation

                def take_proj(g):
                    act.wait_ge(proj_done, g + 1)
                    if g < n_cm:
                        m, hf = divmod(g, 2)
                        dst = t["qk"][:, m, CONV_K - 1 + hf * 512:CONV_K - 1 + hf * 512 + 512]
                        src = ps[g % 2][:, :]
                    else:
                        i, hf = tok_groups[g - n_cm]
                        dst, src = t["vo"][:, i, hf * H:(hf + 1) * H], ps[g % 2][:, 0:H]
                    A(dst, src, ACT.Copy).then_inc(proj_taken, 1)

                def elementwise(q):
                    if q:
                        act.wait_ge(q_free, q)
                    for part in range(4):
                        c, hf = divmod(part, 2)
                        act.wait_ge(z_done, 4 * q + part + 1)
                        A(T[:, c, hf * 512:hf * 512 + 512], ps[2 + part][:, :], ACT.Tanh,
                          bias=hcol[:, c, q:q + 1], scale=0.5).then_inc(z_taken, 1)
                    act.wait_ge(kk_ready, q + 1)
                    A(T[:, 4, :], T[:, 3, :], ACT.Square).then_inc(sq_ready, 1)
                    act.wait_ge(ell_ready, q + 1)
                    A(T[:, 0, :], T[:, 0, :], ACT.Exp).then_inc(exps, 1)
                    A(T[:, 2, :], T[:, 2, :], ACT.Exp).then_inc(exps, 1)
                    act.wait_ge(ss_taken, 2 * (q + 1))
                    A(T[:, 4, :], T[:, 4, :], ACT.Sqrt).then_inc(root, 1)

                for g in range(n_cm):
                    take_proj(g)
                    if g == 1:
                        act.wait_ge(lora_ready, 2)
                        A(pB[0:HD, 9, 1:], pB[0:HD, 9, 1:], ACT.Tanh).then_inc(lora_tanh, 1)
                        A(pB[:, 10, 1:], pB[:, 10, 1:], ACT.Tanh, scale=0.5).then_inc(lora_tanh, 1)
                for n in range(2 * NT):
                    if n in (0, 4, 8):
                        elementwise(n // 4)
                    take_proj(n_cm + n)
                    if n in (3, 7, 11):
                        q = n // 4
                        act.wait_ge(bon_done, q + 1)
                        A(bonus[:, :, 2 * q:2 * q + 2], ps[2][:, 0:2 * NT].rearrange("p (i e) -> p i e", e=2),
                          ACT.Copy).then_inc(bon_taken, 1)
                y = t["ycT"]
                for a in range(2):
                    if a == 0:
                        act.wait_ge(q_free, QB)
                    A(T[:, a, :], y[:, a, :], ACT.Square).then_inc(g_sq, 1)
                for a in range(2):
                    act.wait_ge(g_in, a + 1)
                    A(T[:, a, :], T[:, a, :], ACT.Tanh, scale=float(np.sqrt(2 / np.pi))).then_inc(g_tanh, 1)
                for g in range(4):
                    a, hf = divmod(g, 2)
                    act.wait_ge(glu_done, g + 1)
                    A(T[:, 2 + a, hf * 512:hf * 512 + 512], ps[4 + g][:, :], ACT.Tanh, bias=hcol[:, 2, a:a + 1],
                      scale=0.25).then_inc(glu_tanh, 1)

            @block.vector
            def _(dve):
                ch = Chain(dve, dve_c)
                V = nc.vector

                def shift(i):
                    ch.link(V.tensor_tensor(T[:, 4, :], pB[:, i, 0:S], pB[:, i, 1:1 + S], ALU.subtract))
                    return V.scalar_tensor_tensor(pB[:, i, 1:1 + S], T[:, 4, :], col(t, "mu", i), pB[:, i, 1:1 + S],
                                                  ALU.mult, ALU.add)

                ch.add(V.tensor_scalar(hcol[:, 0, :], col(t, "w0", 0, QB), 0.5, None, ALU.mult))
                ch.add(V.tensor_scalar(hcol[:, 1, :], col(t, "a0", 0, QB), 0.5, None, ALU.mult))
                ch.link(V.tensor_scalar(hcol[:, 2, 0:2], col(t, "glu_b", 0, 2), 0.5, None, ALU.mult))
                for i in (9, 10):
                    shift(i).then_inc(lora_ready, 1)
                    dve.wait_ge(lora_ready, i - 8)
                for i in range(9):
                    ch.link(shift(i))
                dve.wait_ge(lora_tanh, 2)
                ch.link(V.tensor_scalar(pB[:, 10, 1:], pB[:, 10, 1:], 1.0, 0.5, ALU.add, ALU.mult))
                dve.wait_ge(seg_ready, 2)
                for q in range(QB):
                    r, k = pB[:, q, 1:], pB[:, 3 + q, 1:]
                    V.tensor_scalar(T[:, 3, :], k, col(t, "k_k", q), None, ALU.mult).then_inc(kk_ready, 1)
                    dve.wait_ge(z_taken, 4 * (q + 1))
                    ch.add(V.tensor_scalar(T[:, 1, :], T[:, 1, :], 1.0, 0.5, ALU.add, ALU.mult))
                    ch.link(V.tensor_scalar(T[:, 0, :], T[:, 0, :], 1.0, RWKV_DECAY, ALU.add, ALU.mult))
                    ch.link(V.tensor_tensor_scan(T[:, 2, :], t["seg64"][:, :], T[:, 0, :], 0.0, ALU.mult, ALU.add))
                    V.tensor_tensor(T[:, 0, :], T[:, 2, :], T[:, 0, :], ALU.subtract).then_inc(ell_ready, 1)
                    for hf in range(2):
                        dve.wait_ge(ss_done, 2 * q + hf + 1)
                        V.tensor_scalar(T[:, 4, hf * 512:hf * 512 + 512], ps[6 + hf][:, :], 1e-24, None,
                                        ALU.max).then_inc(ss_taken, 1)
                    f = at[:, q, :]
                    ch.link(V.tensor_scalar(f, T[:, 1, :], -1.0, col(t, "k_a", q), ALU.add, ALU.mult))
                    ch.link(V.scalar_tensor_tensor(k, f, 1.0, k, ALU.add, ALU.mult))
                    ch.link(V.tensor_scalar(f, r, col(t, "r_k", q), None, ALU.mult))
                    dve.wait_ge(root, q + 1)
                    ch.link(V.reciprocal(T[:, 4, :], T[:, 4, :]))
                    ch.link(V.tensor_tensor(T[:, 3, :], T[:, 3, :], T[:, 4, :], ALU.mult))
                    V.tensor_tensor(T[:, 4, :], f, k, ALU.mult).then_inc(rk_ready, 1)
                    ch.add(V.tensor_tensor(T[:, 1, :], T[:, 3, :], T[:, 1, :], ALU.mult))
                    dve.wait_ge(exps, 2 * (q + 1))
                    ch.add(V.tensor_tensor(r, r, T[:, 2, :], ALU.mult))
                    ch.add(V.tensor_copy(ec[:, q, :], T[:, 2, 63::64]))
                    dve.wait_ge(rk_ready, q + 1)
                    ch.link(V.scalar_tensor_tensor(f, T[:, 3, :], -1.0, T[:, 0, :], ALU.mult, ALU.mult))
                    ch.link(V.reciprocal(T[:, 0, :], T[:, 2, :]))
                    ch.add(V.tensor_tensor(k, k, T[:, 0, :], ALU.mult))
                    ch.link(V.tensor_tensor(bt[:, q, :], T[:, 1, :], T[:, 0, :], ALU.mult))
                    dve.wait_ge(bon_done, q + 1)
                    dve.sem_inc(q_free, 1)
                y = t["ycT"]
                for a in range(2):
                    dve.wait_ge(g_sq, a + 1)
                    ch.link(V.tensor_scalar(T[:, a, :], T[:, a, :], 0.044715, 1.0, ALU.mult, ALU.add))
                    V.tensor_tensor(T[:, a, :], T[:, a, :], y[:, a, :], ALU.mult).then_inc(g_in, 1)
                for a in range(2):
                    dve.wait_ge(g_tanh, a + 1)
                    V.scalar_tensor_tensor(y[:, a, :], T[:, a, :], 1.0, y[:, a, :], ALU.add,
                                           ALU.mult).then_inc(z2_ready, 1)
                dve.wait_ge(z2_ready, 2)
                dve.wait_ge(glu_done, 4)
                for a in range(2):
                    dve.wait_ge(glu_tanh, 2 * (a + 1))
                    ch.link(V.scalar_tensor_tensor(T[:, 2 + a, :], T[:, 2 + a, :], 1.0, y[:, a, :], ALU.add, ALU.mult))
                    ch.link(V.tensor_scalar(y[:, a, :], T[:, 2 + a, :], 0.25, None, ALU.mult))

            @block.tensor
            def _(pe):
                def proj(g):
                    if g < n_cm:
                        if g == 0:
                            pe.wait_ge(w_in_s[0], 16)
                        m, hf = divmod(g, 2)
                        ops = [(ring[:, 0, k, m * P:(m + 1) * P], t["hT"][:, k, hf * 512:hf * 512 + 512])
                               for k in range(KT)]
                        out = ps[g % 2][:, :]
                    else:
                        i, hf = tok_groups[g - n_cm]
                        pe.wait_ge(w_in_s[(1 + hf) % 2], 16 * (1 + hf))
                        ops = [(t["hT"][:, k, i * P:(i + 1) * P], ring[:, (1 + hf) % 2, k, :]) for k in range(KT)]
                        out = ps[g % 2][:, 0:H]
                    if g >= 2:
                        pe.wait_ge(proj_taken, g - 1)
                    for k, (a, b) in enumerate(ops):
                        last = nc.tensor.matmul(out, a, b, start=(k == 0), stop=(k == KT - 1))
                    last.then_inc(proj_done, 1)

                def z(q):
                    if q == 0:
                        pe.wait_ge(small_in, 48)
                        pe.wait_ge(lora_tanh, 1)
                        pe.wait_ge(lora_ready, 1)
                    for part in range(4):
                        c, hf = divmod(part, 2)
                        if q:
                            pe.wait_ge(z_taken, 4 * (q - 1) + part + 1)
                            pe.wait_ge(bon_taken, q)
                        rows = slice(c * HD, (c + 1) * HD)
                        nc.tensor.matmul(ps[2 + part][:, :], lora[rows, q * P:(q + 1) * P],
                                         pB[rows, 9, 1 + hf * 512:1 + hf * 512 + 512], start=True, stop=True
                                         ).then_inc(z_done, 1)

                def ss(q):
                    pe.wait_ge(sq_ready, q + 1)
                    for hf in range(2):
                        if q:
                            pe.wait_ge(ss_taken, 2 * (q - 1) + hf + 1)
                        nc.tensor.matmul(ps[6 + hf][:, :], cst[:, 0:P], T[:, 4, hf * 512:hf * 512 + 512],
                                         start=True, stop=True).then_inc(ss_done, 1)

                def bon(q):
                    pe.wait_ge(rk_ready, q + 1)
                    pe.wait_ge(z_taken, 4 * (q + 1))
                    for i in range(NT):
                        last = nc.tensor.matmul(ps[2][:, 2 * i:2 * i + 2], T[:, 4, i * P:(i + 1) * P],
                                                cst[:, P:P + 2], start=True, stop=True)
                    last.then_inc(bon_done, 1)

                for g in range(n_cm):
                    proj(g)
                for n in range(2 * NT):
                    if n in (0, 4, 8):
                        z(n // 4)
                        ss(n // 4)
                    proj(n_cm + n)
                    if n in (3, 7, 11):
                        bon(n // 4)
                pe.wait_ge(z2_ready, 2)
                for g in range(4):
                    a, hf = divmod(g, 2)
                    if g == 0:
                        pe.wait_ge(ss_taken, 2 * QB)
                    for k in range(2):
                        last = nc.tensor.matmul(ps[4 + g][:, :], gluw[:, k, a * P:(a + 1) * P],
                                                t["ycT"][:, k, hf * 512:hf * 512 + 512], start=(k == 0), stop=(k == 1))
                    last.then_inc(glu_done, 1)


def phase_c(nc, t, io):
    ps = t["ps"]
    pB, at, bt = t["pB"], t["a_til"], t["b_hat"]
    with ExitStack() as ctx:
        sb = lambda n, s, d=F32: ctx.enter_context(nc.sbuf_tensor(n, s, d, side="right"))
        sem = ctx.enter_context(phase_semaphores(nc))
        msk = sb("pc_msk", [P, 384 + 3 * 384])
        rows = sb("pc_rows", [P, 2, DB])
        gup = sb("pc_gup", [P, DB])
        tok = sb("pc_tok", [P, 2, DB])
        v = sb("pc_v", [P, 2, DB])
        gm = sb("pc_gm", [P, HB, 3 * P])
        ad, adT, aoT = sb("pc_ad", [P, HB, P]), sb("pc_adT", [P, HB, P]), sb("pc_aoT", [P, HB, P])
        p2, p2T, p4, p4T = (sb(f"pc_{n}", [P, HB, P]) for n in ("p2", "p2T", "p4", "p4T"))
        X = sb("pc_X", [P, HB, P])
        av = sb("pc_av", [P, DB])
        ra = sb("pc_ra", [P, DB])
        sa = sb("pc_sa", [P, DB])
        st = sb("pc_state", [P, QB, P])
        sd = sb("pc_sdec", [P, QB, P])
        y = sb("pc_y", [P, 2, DB])
        g = sb("pc_g", [P, DB])
        o = sb("pc_o", [P, 2, DB])
        m = sb("pc_m", [P, 4, HB])
        small_in, zeroed = sem("pc_small_in"), sem("pc_zeroed")
        tr_done, tr_taken = sem("pc_tr_done"), sem("pc_tr_taken")
        gate_done, gate_taken = sem("pc_gate_done"), sem("pc_gate_taken")
        gram_done, gram_taken = sem("pc_gram_done"), sem("pc_gram_taken")
        a_done, a_taken = sem("pc_a_done"), sem("pc_a_taken")
        av_done, av_taken = sem("pc_av_done"), sem("pc_av_taken")
        st_done = [sem(f"pc_stage_done{h}") for h in range(2)]
        copied = [sem(f"pc_copied{h}") for h in range(2)]
        added = [sem(f"pc_added{h}") for h in range(2)]
        ra_done, ra_taken, sa_done, sa_taken = sem("pc_ra_done"), sem("pc_ra_taken"), sem("pc_sa_done"), sem("pc_sa_taken")
        sn_done, s_ready = sem("pc_sn_done"), sem("pc_s_ready")
        y1_taken, y2_done, y_ready = sem("pc_y1_taken"), sem("pc_y2_done"), sem("pc_y_ready")
        var_ready, root = sem("pc_var"), sem("pc_root")
        o_ready, ot_done, ot_taken = sem("pc_o_ready"), sem("pc_ot_done"), sem("pc_ot_taken")
        dve_c = sem("pc_dve")
        CP = [0, 2, 4, 5, 5, 6, 8, 9, 9]
        AD = [0, 0, 1, 2, 3, 3, 3, 4, 5]
        NST, NCP, NAD = 8, CP[-1], AD[-1]
        bank = lambda h, b: ps[3 * h + b]
        ORDER = [0, 2, 4, 1, 3, 5]
        cols3 = lambda a: a[:, 0:384].rearrange("p (h n) -> p h n", h=3)

        with nc.Block() as block:
            @block.sync
            def _(sp):
                sp.dma_start(msk[:, :], io["rwkv_masks"]).then_inc(small_in, 16)
                sp.dma_start(rows[:, :, :], io["rows_rwkv"].rearrange("p (a n) -> p a n", a=2)).then_inc(small_in, 16)
                sp.dma_start(gup[:, :], io["g_up"]).then_inc(small_in, 16)

            @block.gpsimd
            def _(pool):
                nc.gpsimd.memset(st[:, :, :], 0.0).then_inc(zeroed, 1)

            @block.scalar
            def _(act):
                cp = lambda d, s: nc.scalar.activation(d, s, ACT.Copy)

                def take_ot(i):
                    act.wait_ge(ot_done, i + 1)
                    cp(pB[:, 0:QB, 1 + i * P:1 + (i + 1) * P], cols3(ps[4])).then_inc(ot_taken, 1)

                def take_gate(i):
                    act.wait_ge(gate_done, i + 1)
                    if i:
                        act.wait_ge(o_ready, i)
                    cp(g[:, :], ps[3][:, 0:DB]).then_inc(gate_taken, 1)

                def roots(i):
                    act.wait_ge(var_ready, i + 1)
                    nc.scalar.activation(m[:, 2, :], m[:, 1, :], ACT.Sqrt).then_inc(root, 1)

                for i in range(NT):
                    for b, dst in enumerate((tok[:, 0, :], tok[:, 1, :], v[:, i % 2, :])):
                        act.wait_ge(tr_done, 3 * i + b + 1)
                        if b == 2 and i >= 2:
                            act.wait_ge(o_ready, i - 1)
                        cp(dst, ps[b][:, 0:DB]).then_inc(tr_taken, 1)
                    if i:
                        take_gate(i - 1)
                    copies = [[(p2, 1), (p2T, 2)], [(p4, 1), (p4T, 2)], [(p2, 1)], [], [(p4, 1)],
                              [(p2, 0), (p2T, 2)], [(p4, 1)], []]
                    for s in range(NST):
                        for h in range(2):
                            if copies[s]:
                                act.wait_ge(st_done[h], NST * i + s + 1)
                            for dst, b in copies[s]:
                                cp(dst[:, 3 * h:3 * h + 3, :], cols3(bank(h, b))).then_inc(copied[h], 1)
                        if s == 0 and i:
                            roots(i - 1)
                    if i:
                        take_ot(i - 1)
                    for c in range(2):
                        R = slice(64 * c, 64 * c + 64)
                        act.wait_ge(sa_done, 2 * i + c + 1)
                        cp(sa[R, :], ps[4][R, 0:DB]).then_inc(sa_taken, 1)
                    act.wait_ge(sn_done, 2 * (i + 1))
                    if i >= 2:
                        act.wait_ge(o_ready, i - 1)
                    cp(y[:, i % 2, :], ps[6][:, 0:DB]).then_inc(y1_taken, 1)
                take_gate(NT - 1)
                roots(NT - 1)
                take_ot(NT - 1)

            @block.vector
            def _(dve):
                ch = Chain(dve, dve_c)
                V = nc.vector
                L = lambda *a: ch.link(V.tensor_tensor(*a))
                M3 = lambda k: msk[:, 384 * (k + 1):384 * (k + 2)].rearrange("p (h n) -> p h n", h=3)

                def out(i):
                    yi = y[:, i % 2, :].rearrange("p (h n) -> p h n", h=HB)
                    ov = [o[:, k, :].rearrange("p (h n) -> p h n", h=HB) for k in range(2)]
                    vv = v[:, i % 2, :].rearrange("p (h n) -> p h n", h=HB)
                    bc = lambda a: a.unsqueeze(2).broadcast_to([P, HB, HD])
                    if i:
                        dve.wait_ge(ot_done, i)
                    dve.wait_ge(y_ready, i + 1)
                    ch.link(V.tensor_reduce(m[:, 0, :], yi, AX.X, ALU.add))
                    ch.link(V.tensor_scalar(m[:, 0, :], m[:, 0, :], 1.0 / HD, None, ALU.mult))
                    L(ov[0], yi, bc(m[:, 0, :]), ALU.subtract)
                    L(ov[1], ov[0], ov[0], ALU.mult)
                    ch.link(V.tensor_reduce(m[:, 1, :], ov[1], AX.X, ALU.add))
                    V.tensor_scalar(m[:, 1, :], m[:, 1, :], 1.0 / HD, GN_EPS, ALU.mult, ALU.add).then_inc(var_ready, 1)
                    L(ov[1], vv, bc(t["bonus"][:, i, :]), ALU.mult)
                    L(o[:, 1, :], o[:, 1, :], rows[:, 1, :], ALU.add)
                    dve.wait_ge(root, i + 1)
                    ch.link(V.reciprocal(m[:, 3, :], m[:, 2, :]))
                    L(ov[0], ov[0], bc(m[:, 3, :]), ALU.mult)
                    L(o[:, 0, :], o[:, 0, :], rows[:, 0, :], ALU.mult)
                    L(o[:, 0, :], o[:, 0, :], o[:, 1, :], ALU.add)
                    dve.wait_ge(gate_taken, i + 1)
                    V.tensor_tensor(o[:, 0, :], o[:, 0, :], g[:, :], ALU.mult).then_inc(o_ready, 1)

                dve.wait_ge(small_in, 48)
                dve.wait_ge(zeroed, 1)
                for i in range(NT):
                    for h in range(HB):
                        dve.wait_ge(gram_done, HB * i + h + 1)
                        G = ps[6 + h % 2]
                        ch.add(V.tensor_tensor(gm[:, h, :], G[:, P:512], msk[:, 0:384], ALU.mult))
                        ch.add(V.tensor_tensor(adT[:, h, :], G[:, 0:P], msk[:, 384:384 + P], ALU.mult))
                        V.tensor_tensor(aoT[:, h, :], G[:, 0:P], msk[:, 768:768 + P], ALU.mult).then_inc(gram_taken, 1)
                        if h % 3 == 2:
                            half = h // 3
                            hs = slice(3 * half, 3 * half + 3)
                            dve.wait_ge(a_done, 2 * i + half + 1)
                            ch.add(V.tensor_tensor(ad[:, hs, :], cols3(bank(half, 0)), M3(2), ALU.mult))
                            ch.sync()
                            V.tensor_tensor(X[:, hs, :], adT[:, hs, :],
                                            t["ident"][:, :].unsqueeze(1).broadcast_to([P, 3, P]),
                                            ALU.add).then_inc(a_taken, 1)
                    dve.wait_ge(av_done, i + 1)
                    V.tensor_copy(av[:, :], ps[6][:, 0:DB]).then_inc(av_taken, 1)
                    if i:
                        out(i - 1)
                    for s in (1, 2, 3, 6, 7):
                        for h in range(2):
                            hs = slice(3 * h, 3 * h + 3)
                            dve.wait_ge(st_done[h], NST * i + s + 1)
                            V.tensor_tensor(X[:, hs, :], X[:, hs, :], cols3(bank(h, 0)), ALU.add).then_inc(added[h], 1)
                    for c in range(2):
                        n = 2 * i + c
                        R = slice(64 * c, 64 * c + 64)
                        dve.wait_ge(ra_done, n + 1)
                        V.tensor_tensor(ra[R, :], ps[7][R, 0:DB], av[R, :], ALU.add).then_inc(ra_taken, 1)
                        for q in range(QB):
                            ch.add(V.tensor_scalar(sd[:, q, :], st[:, q, :], t["chunk_decay"][:, q, n:n + 1], None,
                                                   ALU.mult))
                        ch.sync()
                        dve.wait_ge(sn_done, n + 1)
                        for q in range(QB):
                            for e in range(2):
                                r = slice(64 * e, 64 * e + 64)
                                last = V.scalar_tensor_tensor(
                                    st[r, q, 64 * e:64 * e + 64], ps[5][r, q * P + 64 * e:q * P + 64 * e + 64],
                                    t["chunk_decay"][r, q, n:n + 1], sd[r, q, 64 * e:64 * e + 64], ALU.mult, ALU.add)
                                ch.add(last)
                        ch.sync()
                        dve.sem_inc(s_ready, 1)
                    dve.wait_ge(y2_done, i + 1)
                    dve.wait_ge(y1_taken, i + 1)
                    V.tensor_tensor(y[:, i % 2, :], y[:, i % 2, :], ps[3][:, 0:DB], ALU.add).then_inc(y_ready, 1)
                out(NT - 1)

            @block.tensor
            def _(pe):
                mm = nc.tensor.matmul

                def gate(i):
                    mm(ps[3][:, 0:DB], pB[:, 10, 1 + i * P:1 + (i + 1) * P], gup[:, :], start=True, stop=True
                       ).then_inc(gate_done, 1)

                def out_t(i):
                    pe.wait_ge(o_ready, i + 1)
                    for q in range(QB):
                        last = nc.tensor.transpose(ps[4][:, q * P:(q + 1) * P], o[:, 0, q * P:(q + 1) * P],
                                                   t["ident"][:, :])
                    last.then_inc(ot_done, 1)

                pe.wait_ge(small_in, 48)
                pe.wait_ge(zeroed, 1)
                for i in range(NT):
                    T0, T1 = i * P, (i + 1) * P
                    vi = v[:, i % 2, :]
                    if i:
                        pe.wait_ge(added[0], NAD * i)
                        pe.wait_ge(copied[0], NCP * i)
                    for b in range(3):
                        for q in range(QB):
                            src = (bt[:, q, T0:T1], pB[:, 3 + q, 1 + T0:1 + T1], pB[:, 6 + q, 1 + T0:1 + T1])[b]
                            last = nc.tensor.transpose(ps[b][:, q * P:(q + 1) * P], src, t["ident"][:, :])
                        last.then_inc(tr_done, 1)
                    if i:
                        pe.wait_ge(y_ready, i)
                        gate(i - 1)
                    for h, head in enumerate(ORDER):
                        q, e = divmod(head, 2)
                        r = slice(64 * e, 64 * e + 64)
                        A_, R_ = at[r, q, T0:T1], pB[r, q, 1 + T0:1 + T1]
                        B_, K_ = bt[r, q, T0:T1], pB[r, 3 + q, 1 + T0:1 + T1]
                        if HB * i + h >= 2:
                            pe.wait_ge(gram_taken, HB * i + h - 1)
                        if h < 2 and i:
                            pe.wait_ge(y1_taken, i)
                            pe.wait_ge(ra_taken, 2 * i)
                        G = ps[6 + h % 2]
                        mm(G[:, 0:P], B_, A_, start=True, stop=True)
                        mm(G[:, P:2 * P], B_, R_, start=True, stop=True)
                        mm(G[:, 2 * P:3 * P], K_, A_, start=True, stop=True)
                        mm(G[:, 3 * P:], K_, R_, start=True, stop=True).then_inc(gram_done, 1)
                        half = h // 3
                        if h % 3 == 0:
                            if half == 0:
                                pe.wait_ge(tr_taken, 3 * i + 1)
                            elif i:
                                pe.wait_ge(gate_taken, i)
                        last = mm(bank(half, 0)[:, (h % 3) * P:(h % 3 + 1) * P], A_, B_, start=True, stop=True)
                        if h % 3 == 2:
                            last.then_inc(a_done, 1)
                    pe.wait_ge(gram_taken, HB * (i + 1))
                    pe.wait_ge(tr_taken, 3 * (i + 1))
                    for h, head in enumerate(ORDER):
                        last = mm(ps[6][:, head * HD:(head + 1) * HD], gm[:, h, P:2 * P], vi[:, head * HD:(head + 1) * HD],
                                  start=True, stop=True)
                    last.then_inc(av_done, 1)
                    stages = [[(1, adT, ad), (2, ad, adT)], [(0, p2, X), (1, p2T, p2), (2, p2, p2T)],
                              [(0, p4, X), (1, p4T, p4)], [(0, p2, X)], None, [(0, aoT, p4), (2, p4, aoT)],
                              [(0, p2, X), (1, p2T, p2)], [(0, p4, X)]]
                    for s, prods in enumerate(stages):
                        for h in range(2):
                            if s == 0:
                                pe.wait_ge(a_taken, 2 * i + h + 1)
                                if h and i:
                                    pe.wait_ge(added[1], NAD * i)
                                    pe.wait_ge(copied[1], NCP * i)
                                    pe.wait_ge(s_ready, 2 * i)
                                    pe.wait_ge(sa_taken, 2 * i)
                            else:
                                if NCP * i + CP[s]:
                                    pe.wait_ge(copied[h], NCP * i + CP[s])
                                if NAD * i + AD[s]:
                                    pe.wait_ge(added[h], NAD * i + AD[s])
                            for j in range(3):
                                n = 3 * h + j
                                if prods is None:
                                    last = nc.tensor.transpose(bank(h, 1)[:, j * P:(j + 1) * P], X[:, n, :],
                                                               t["ident"][:, :])
                                    continue
                                for b, lhs, rhs in prods:
                                    last = mm(bank(h, b)[:, j * P:(j + 1) * P], lhs[:, n, :], rhs[:, n, :],
                                              start=True, stop=True)
                            last.then_inc(st_done[h], 1)
                    pe.wait_ge(added[1], NAD * (i + 1))
                    pe.wait_ge(added[0], NAD * (i + 1))
                    pe.wait_ge(copied[1], NCP * (i + 1))
                    if i:
                        out_t(i - 1)
                    pe.wait_ge(av_taken, i + 1)
                    for c in range(2):
                        n = 2 * i + c
                        R = slice(64 * c, 64 * c + 64)
                        if n:
                            pe.wait_ge(s_ready, n)
                        for q in range(QB):
                            last = mm(ps[7][R, q * P:(q + 1) * P], at[:, q, T0 + 64 * c:T0 + 64 * c + 64],
                                      st[:, q, :], start=True, stop=True)
                        last.then_inc(ra_done, 1)
                        for q in range(QB):
                            mm(ps[6][R, q * P:(q + 1) * P], pB[:, q, 1 + T0 + 64 * c:1 + T0 + 64 * c + 64],
                               st[:, q, :], start=True, stop=True)
                        pe.wait_ge(ra_taken, n + 1)
                        if c == 0 and i:
                            pe.wait_ge(ot_taken, i)
                        for h, head in enumerate(ORDER):
                            last = mm(ps[4][R, head * HD:(head + 1) * HD], X[R, h, 64 * c:64 * c + 64],
                                      ra[R, head * HD:(head + 1) * HD], start=True, stop=True)
                        last.then_inc(sa_done, 1)
                        pe.wait_ge(sa_taken, n + 1)
                        for q in range(QB):
                            o_ = ps[5][:, q * P:(q + 1) * P]
                            mm(o_, tok[R, 1, q * P:(q + 1) * P], vi[R, q * P:(q + 1) * P], start=True, stop=False)
                            last = mm(o_, tok[R, 0, q * P:(q + 1) * P], sa[R, q * P:(q + 1) * P], start=False, stop=True)
                        last.then_inc(sn_done, 1)
                    for h, head in enumerate(ORDER):
                        hc = slice(head * HD, (head + 1) * HD)
                        o_ = ps[3][:, hc]
                        mm(o_, gm[:, h, 2 * P:], vi[:, hc], start=True, stop=False)
                        last = mm(o_, gm[:, h, 0:P], sa[:, hc], start=False, stop=True)
                    last.then_inc(y2_done, 1)
                pe.wait_ge(y_ready, NT)
                gate(NT - 1)
                out_t(NT - 1)


def phase_d(nc, t, io):
    ps = t["ps"]
    pB, vo, qk = t["pB"], t["vo"], t["qk"]
    qT, kT = t["a_til"], t["b_hat"]
    W65 = HD + 1
    with ExitStack() as ctx:
        sb = lambda n, s, d=F32: ctx.enter_context(nc.sbuf_tensor(n, s, d, side="right"))
        sem = ctx.enter_context(phase_semaphores(nc))
        cst = sb("pd_cst", [P, (HA + QA + 1) * P])
        wqk = sb("pd_wqk", [P, 2, QA, P])
        nw = sb("pd_nw", [P, DA])
        vaug = sb("pd_vaug", [P, NT, HA, W65])
        M = sb("pd_M", [P, S])
        R4 = sb("pd_R4", [HA, 4, S])
        fz, bc_ = sb("pd_fz", [HA, S]), sb("pd_b", [HA, S])
        mp = sb("pd_mp", [HA, NT + 1])
        gcol = sb("pd_gcol", [P, NT, 4, HA])
        dec = sb("pd_dec", [P, QA, NT])
        E = sb("pd_E", [P, HA, P])
        Pm = sb("pd_P", [P, HA, P])
        kw = sb("pd_kw", [P, 2, DA])
        C = sb("pd_C", [P, QA, 2, W65])
        hb = sb("pd_h", [P, NT, HA, W65])
        mom = sb("pd_mom", [P, 3, NT, HA])
        small_in, prep = sem("pd_small_in"), sem("pd_prep")
        gt_done, f_ready, f_exp, f_ln = sem("pd_gt_done"), sem("pd_f_ready"), sem("pd_f_exp"), sem("pd_f_ln")
        arg_ready, exps, rows_ready = sem("pd_arg_ready"), sem("pd_exps"), sem("pd_rows_ready")
        gc_done, gc_taken, m_ready = sem("pd_gc_done"), sem("pd_gc_taken"), sem("pd_m_ready")
        cv_ready, cv_tanh, cx_ready = sem("pd_cv_ready"), sem("pd_cv_tanh"), sem("pd_cx_ready")
        qk_done, qk_taken = sem("pd_qk_done"), sem("pd_qk_taken")
        e_done, e_taken, sc_done, p_ready = sem("pd_e_done"), sem("pd_e_taken"), sem("pd_sc_done"), sem("pd_p_ready")
        kt_done, kt_taken, kw_ready = sem("pd_kt_done"), sem("pd_kt_taken"), sem("pd_kw_ready")
        it_done, ia_done, h_taken = sem("pd_it_done"), sem("pd_ia_done"), sem("pd_h_taken")
        c_done, c_ready = sem("pd_c_done"), sem("pd_c_ready")
        o_tanh, var_ready, root = sem("pd_o_tanh"), sem("pd_var"), sem("pd_root")
        y_ready, yt_done, yt_taken = sem("pd_y_ready"), sem("pd_yt_done"), sem("pd_yt_taken")
        dve_c, pool_c = sem("pd_dve"), sem("pd_pool")
        sel = lambda h: cst[:, h * P:(h + 1) * P]
        pair_sel = lambda q: cst[0:HA, (HA + q) * P:(HA + q + 1) * P]
        causal = cst[:, (HA + QA) * P:(HA + QA + 1) * P]
        ORDER = [0, 2, 4, 1, 3, 5]
        cx = pB[:, 3:6, 1:]
        ov = vo[:, :, DA:2 * DA]

        with nc.Block() as block:
            @block.sync
            def _(sp):
                sp.dma_start(cst[:, :], io["mlstm_cst"]).then_inc(small_in, 16)
                sp.dma_start(wqk[:, :, :, :], io["wqk"]).then_inc(small_in, 16)
                sp.dma_start(nw[:, :], io["rows_mlstm"]).then_inc(small_in, 16)

            @block.gpsimd
            def _(pool):
                nc.gpsimd.memset(M[:, :], 0.0).then_inc(prep, 1)
                nc.gpsimd.memset(t["seg64"][:, HD::2 * HD], 1.0).then_inc(prep, 1)
                nc.gpsimd.memset(C[:, :, :, :], 0.0).then_inc(prep, 1)
                nc.gpsimd.memset(mp[:, 0:1], 0.0).then_inc(prep, 1)
                nc.gpsimd.memset(vaug[:, :, :, HD:W65], 1.0).then_inc(prep, 1)
                for i in range(NT):
                    nc.gpsimd.tensor_copy(vaug[:, i, :, 0:HD],
                                          vo[:, i, 0:DA].rearrange("p (h n) -> p h n", h=HA)).then_inc(prep, 1)

            @block.scalar
            def _(act):
                A = nc.scalar.activation
                act.wait_ge(f_ready, 2)
                A(fz[:, :], fz[:, :], ACT.Exp, scale=-1.0).then_inc(f_exp, 1)
                act.wait_ge(f_exp, 1)
                A(fz[:, :], fz[:, :], ACT.Ln, bias=1.0).then_inc(f_ln, 1)
                for q in range(QA):
                    act.wait_ge(cv_ready, q + 1)
                    A(kT[:, q, :], cx[:, q, :], ACT.Tanh, scale=0.5).then_inc(cv_tanh, 1)
                A(ov, ov, ACT.Tanh, scale=0.5).then_inc(o_tanh, 1)
                for k in range(3):
                    act.wait_ge(arg_ready, k + 1)
                    A(R4[:, k + 1, :], R4[:, k + 1, :], ACT.Exp).then_inc(exps, 1)
                for g in range(4 * QA):
                    which, rem = divmod(g, 2 * QA)
                    q, hf = divmod(rem, 2)
                    act.wait_ge(qk_done, g + 1)
                    A((qT, kT)[which][:, q, hf * 512:hf * 512 + 512], ps[4 + g % 2][:, :], ACT.Copy,
                      scale=(0.5, 0.0625)[which]).then_inc(qk_taken, 1)
                act.wait_ge(gc_done, 2)
                A(gcol[:, :, :, :].rearrange("p i k h -> p (i k h)"), ps[6][:, 0:4 * HA * NT], ACT.Copy).then_inc(gc_taken, 1)
                A(dec[:, :, :].rearrange("p q i -> p (q i)"), ps[7][:, 0:QA * NT], ACT.Copy).then_inc(gc_taken, 1)
                act.wait_ge(gc_taken, 2)
                for i in range(NT):
                    act.wait_ge(kt_done, i + 1)
                    if i >= 2:
                        act.wait_ge(c_done, i - 1)
                    A(kw[:, i % 2, :], ps[7][:, 0:DA], ACT.Copy, scale=0.0625).then_inc(kt_taken, 1)
                    for n, h in enumerate(ORDER):
                        act.wait_ge(e_done, 2 * i + n // 3 + 1)
                        if i and n == 0:
                            act.wait_ge(p_ready, 2 * i)
                        A(E[:, n, :], ps[n // 3][:, (n % 3) * P:(n % 3 + 1) * P], ACT.Exp,
                          bias=gcol[:, i, 0, h:h + 1], scale=-1.0).then_inc(e_taken, 1)
                act.wait_ge(var_ready, 1)
                A(mom[:, 1, :, :], mom[:, 1, :, :], ACT.Sqrt).then_inc(root, 1)
                for g in range(2 * QA):
                    act.wait_ge(yt_done, g + 1)
                    q, hf = divmod(g, 2)
                    A(qk[:, q, hf * 512:hf * 512 + 512], ps[g % 4][:, :], ACT.Copy).then_inc(yt_taken, 1)

            @block.vector
            def _(dve):
                ch = Chain(dve, dve_c)
                V = nc.vector
                T = lambda *a: ch.add(V.tensor_tensor(*a))
                L = lambda *a: ch.link(V.tensor_tensor(*a))
                dve.wait_ge(gt_done, 1)
                for hf in range(2):
                    n = slice(hf * 512, hf * 512 + 512)
                    ch.add(V.tensor_scalar(R4[:, 0, n], ps[hf][0:HA, :], col(t, "b_i")[0:HA, :], None, ALU.add))
                    ch.add(V.tensor_scalar(bc_[:, n], ps[2 + hf][0:HA, :], col(t, "b_f")[0:HA, :], None, ALU.add))
                    ch.sync()
                    V.scalar_tensor_tensor(fz[:, n], bc_[:, n], -1.0, bc_[:, n], ALU.mult, ALU.max).then_inc(f_ready, 1)
                for q in range(QA):
                    c = cx[:, q, :]
                    cw = lambda j: col(t, "conv_w", q * CONV_K + j)
                    ch.link(V.tensor_scalar(c, qk[:, q, 0:S], cw(0), col(t, "conv_b", q), ALU.mult, ALU.add))
                    for j in range(1, CONV_K):
                        ins = V.scalar_tensor_tensor(c, qk[:, q, j:j + S], cw(j), c, ALU.mult, ALU.add)
                        if j < CONV_K - 1:
                            ch.link(ins)
                    ins.then_inc(cv_ready, 1)
                dve.wait_ge(f_ln, 1)
                dve.wait_ge(prep, 4)
                ch.link(V.scalar_tensor_tensor(fz[:, :], bc_[:, :], 0.0, fz[:, :], ALU.min, ALU.subtract))
                ch.link(V.tensor_tensor_scan(bc_[:, :], t["seg64"][0:HA, :], fz[:, :], 0.0, ALU.mult, ALU.add))
                L(R4[:, 0, :], R4[:, 0, :], bc_[:, :], ALU.subtract)
                for i in range(NT):
                    n = slice(i * P, (i + 1) * P)
                    ch.link(V.tensor_tensor_scan(M[0:HA, n], R4[:, 0, n], R4[:, 0, n], mp[:, i:i + 1], ALU.max, ALU.max))
                    L(mp[:, i + 1:i + 2], bc_[:, (i + 1) * P - 1:(i + 1) * P], M[0:HA, (i + 1) * P - 1:(i + 1) * P], ALU.add)
                dve.sem_inc(m_ready, 1)
                c3 = lambda a: a.rearrange("p (i n) -> p i n", i=NT)
                V.tensor_tensor(c3(R4[:, 1, :]), mp[:, 0:NT].unsqueeze(2).broadcast_to([HA, NT, P]), c3(M[0:HA, :]),
                                ALU.subtract).then_inc(arg_ready, 1)
                L(R4[:, 2, :], bc_[:, :], M[0:HA, :], ALU.add)
                V.tensor_scalar(R4[:, 2, :], R4[:, 2, :], -1.0, 80.0, ALU.mult, ALU.min).then_inc(arg_ready, 1)
                V.tensor_tensor(c3(R4[:, 3, :]), c3(R4[:, 0, :]), M[0:HA, P - 1::P].unsqueeze(2).broadcast_to([HA, NT, P]),
                                ALU.subtract).then_inc(arg_ready, 1)
                for q in range(QA):
                    dve.wait_ge(cv_tanh, q + 1)
                    V.scalar_tensor_tensor(cx[:, q, :], kT[:, q, :], 1.0, cx[:, q, :], ALU.add, ALU.mult
                                           ).then_inc(cx_ready, 1)
                dve.wait_ge(gc_taken, 2)
                dve.wait_ge(prep, 5 + NT)
                dve.wait_ge(o_tanh, 1)
                h6 = lambda a: a.rearrange("p (h n) -> p h n", h=HA)
                bcast = lambda a, n: a.unsqueeze(2).broadcast_to([P, HA, n])
                for i in range(NT):
                    dve.wait_ge(kt_taken, i + 1)
                    V.tensor_tensor(h6(kw[:, i % 2, :]), h6(kw[:, i % 2, :]), bcast(gcol[:, i, 3, :], HD), ALU.mult
                                    ).then_inc(kw_ready, 1)
                    for b in range(2):
                        dve.wait_ge(e_taken, 6 * i + 3 * b + 3)
                        dve.wait_ge(sc_done, 2 * i + b + 1)
                        if i:
                            dve.wait_ge(ia_done, i)
                        V.tensor_tensor(Pm[:, 3 * b:3 * b + 3, :], ps[2 + b][:, 0:384].rearrange("p (h n) -> p h n", h=3),
                                        E[:, 3 * b:3 * b + 3, :], ALU.mult).then_inc(p_ready, 1)
                    dve.wait_ge(it_done, i + 1)
                    L(hb[:, i, :, :], h6(ps[5][:, 0:HA * W65]), bcast(gcol[:, i, 1, :], W65), ALU.mult)
                    dve.wait_ge(ia_done, i + 1)
                    V.tensor_tensor(hb[:, i, :, :], hb[:, i, :, :], h6(ps[4][:, 0:HA * W65]), ALU.add).then_inc(h_taken, 1)
                    dve.wait_ge(c_done, i + 1)
                    for q in range(QA):
                        for e in range(2):
                            r = slice(64 * e, 64 * e + 64)
                            a = q * 2 * W65 + e * W65
                            ch.add(V.scalar_tensor_tensor(C[r, q, e, :], C[r, q, e, :], dec[r, q, i:i + 1],
                                                          ps[6][r, a:a + W65], ALU.mult, ALU.add))
                    ch.sync()
                    dve.sem_inc(c_ready, 1)
                dve.wait_ge(h_taken, NT)
                U = NT * HA
                f48 = lambda a: a.rearrange("p i h -> p (i h)")
                hv = hb[:, :, :, :].rearrange("p i h n -> p (i h) n")
                num = hv[:, :, 0:HD]
                scr = pB[:, 6:9, 1:]
                bu = lambda a: a.unsqueeze(2).broadcast_to([P, U, HD])
                m0, m1, m2 = (f48(mom[:, k, :, :]) for k in range(3))
                ch.link(V.scalar_tensor_tensor(m0, hv[:, :, HD], -1.0, hv[:, :, HD], ALU.mult, ALU.max))
                L(mom[:, 0, :, :], mom[:, 0, :, :], gcol[:, :, 2, :], ALU.max)
                ch.link(V.reciprocal(m0, m0))
                L(num, num, bu(m0), ALU.mult)
                ch.link(V.tensor_reduce(m0, num, AX.X, ALU.add))
                ch.link(V.tensor_scalar(m0, m0, 1.0 / HD, None, ALU.mult))
                L(num, num, bu(m0), ALU.subtract)
                for j in range(3):
                    a = slice(16 * j, 16 * j + 16)
                    T(scr[:, j, :].rearrange("p (u n) -> p u n", n=HD), num[:, a, :], num[:, a, :], ALU.mult)
                ch.sync()
                for j in range(3):
                    ch.add(V.tensor_reduce(m1[:, 16 * j:16 * j + 16], scr[:, j, :].rearrange("p (u n) -> p u n", n=HD),
                                           AX.X, ALU.add))
                ch.sync()
                V.tensor_scalar(m1, m1, 1.0 / HD, HEAD_EPS, ALU.mult, ALU.add).then_inc(var_ready, 1)
                dve.wait_ge(root, 1)
                ch.link(V.reciprocal(m2, m1))
                ch.link(V.tensor_scalar(m2, m2, 0.5, None, ALU.mult))
                L(num, num, bu(m2), ALU.mult)
                for i in range(NT):
                    ch.add(V.scalar_tensor_tensor(ov[:, i, :], ov[:, i, :], 1.0, nw[:, :], ALU.add, ALU.mult))
                ch.sync()
                for i in range(NT):
                    V.tensor_tensor(h6(ov[:, i, :]), h6(ov[:, i, :]), hb[:, i, :, 0:HD], ALU.mult).then_inc(y_ready, 1)

            @block.tensor
            def _(pe):
                mm, tr = nc.tensor.matmul, nc.tensor.transpose
                ident = t["ident"]
                for k in range(2):
                    for i in range(NT):
                        last = tr(ps[2 * k + i // 4][0:HA, (i % 4) * P:(i % 4 + 1) * P],
                                  vo[:, i, 2 * DA + k * HA:2 * DA + (k + 1) * HA], ident[:, :])
                last.then_inc(gt_done, 1)
                pe.wait_ge(small_in, 48)
                for g in range(4 * QA):
                    which, rem = divmod(g, 2 * QA)
                    q, hf = divmod(rem, 2)
                    pe.wait_ge(cx_ready, q + 1)
                    if g >= 2:
                        pe.wait_ge(qk_taken, g - 1)
                    mm(ps[4 + g % 2][:, :], wqk[:, which, q, :], cx[:, q, hf * 512:hf * 512 + 512],
                       start=True, stop=True).then_inc(qk_done, 1)
                pe.wait_ge(exps, 3)
                for i in range(NT):
                    for k in range(4):
                        a = (i * 4 + k) * HA
                        last = tr(ps[6][:, a:a + HA], R4[:, k, i * P:(i + 1) * P], ident[0:HA, 0:HA])
                last.then_inc(gc_done, 1)
                for q in range(QA):
                    last = mm(ps[7][:, q * NT:(q + 1) * NT], pair_sel(q), R4[:, 1, P - 1::P], start=True, stop=True)
                last.then_inc(gc_done, 1)
                pe.wait_ge(m_ready, 1)
                pe.wait_ge(qk_taken, 4 * QA)
                pe.wait_ge(prep, 5 + NT)
                pe.wait_ge(gc_taken, 2)
                for i in range(NT):
                    n = slice(i * P, (i + 1) * P)
                    if i:
                        pe.wait_ge(kt_taken, i)
                    for q in range(QA):
                        last = mm(ps[7][:, q * P:(q + 1) * P], cx[:, q, n], wqk[:, 1, q, :], start=True, stop=True)
                    last.then_inc(kt_done, 1)
                    for b in range(2):
                        if i:
                            pe.wait_ge(e_taken, 6 * (i - 1) + 3 * b + 3)
                        for j in range(3):
                            mm(ps[b][:, j * P:(j + 1) * P], ident[:, :], causal, start=True, stop=False)
                            last = mm(ps[b][:, j * P:(j + 1) * P], sel(ORDER[3 * b + j]), M[:, n],
                                      start=False, stop=True)
                        last.then_inc(e_done, 1)
                    for b in range(2):
                        if i:
                            pe.wait_ge(p_ready, 2 * (i - 1) + b + 1)
                        for j in range(3):
                            h = ORDER[3 * b + j]
                            q, r = h // 2, slice(64 * (h % 2), 64 * (h % 2) + 64)
                            last = mm(ps[2 + b][:, j * P:(j + 1) * P], kT[r, q, n], qT[r, q, n], start=True, stop=True)
                        last.then_inc(sc_done, 1)
                    if i:
                        pe.wait_ge(c_ready, i)
                        pe.wait_ge(h_taken, i)
                    for q in range(QA):
                        last = mm(ps[5][:, q * 2 * W65:(q + 1) * 2 * W65], qT[:, q, n],
                                  C[:, q, :, :].rearrange("p e n -> p (e n)"), start=True, stop=True)
                    last.then_inc(it_done, 1)
                    pe.wait_ge(kw_ready, i + 1)
                    for q in range(QA):
                        last = mm(ps[6][:, q * 2 * W65:(q + 1) * 2 * W65], kw[:, i % 2, q * P:(q + 1) * P],
                                  vaug[:, i, 2 * q:2 * q + 2, :].rearrange("p e n -> p (e n)"), start=True, stop=True)
                    last.then_inc(c_done, 1)
                    for s, h in enumerate(ORDER):
                        pe.wait_ge(p_ready, 2 * i + s // 3 + 1)
                        last = mm(ps[4][:, h * W65:(h + 1) * W65], Pm[:, s, :], vaug[:, i, h, :], start=True, stop=True)
                    last.then_inc(ia_done, 1)
                for g in range(2 * QA):
                    q, hf = divmod(g, 2)
                    if g >= 4:
                        pe.wait_ge(yt_taken, g - 3)
                    for j in range(4):
                        i = 4 * hf + j
                        pe.wait_ge(y_ready, i + 1)
                        last = tr(ps[g % 4][:, j * P:(j + 1) * P], ov[:, i, q * P:(q + 1) * P], ident[:, :])
                    last.then_inc(yt_done, 1)


def phase_mod2(nc, t, io):
    ps = t["ps"]
    mod = t["mod2"]
    with ExitStack() as ctx:
        ring = ctx.enter_context(nc.sbuf_tensor("m2_ring", [P, 3, KT * 512], F32, side="right"))
        sem = ctx.enter_context(phase_semaphores(nc))
        rows_in, x_in = sem("m2_rows_in"), sem("m2_x_in")
        w_in = [sem(f"m2_w_in{i}") for i in range(3)]
        mod_done, mod_taken, dve_c = sem("m2_mod_done"), sem("m2_mod_taken"), sem("m2_dve")
        ada = io["ada_w"].rearrange("o (k p) n -> p (o k) n", p=P)
        with nc.Block() as block:
            @block.sync
            def _(sp):
                sp.dma_start(mod[:, :, :], io["rows_mod"][:, 2 * D:].rearrange("p (a d) -> p a d", a=4)
                             ).then_inc(rows_in, 16)
                for n in range(8):
                    if n >= 3:
                        sp.wait_ge(mod_done, n - 2)
                    c0 = 2 * D + n * 512
                    sp.dma_start(ring[:, n % 3, :].rearrange("p (k n) -> p k n", k=KT), ada[:, :, c0:c0 + 512]
                                 ).then_inc(w_in[n % 3], 16)
                sp.dma_start(t["wout"][:, :, :], io["w_out"].rearrange("o (k p) n -> p (o k) n", p=P)).then_inc(x_in, 16)
                sp.dma_start(t["x1"][:, :, :], io["x"].rearrange("b (i p) d -> p (b i) d", p=P)).then_inc(x_in, 16)
                sp.dma_start(t["nffn"][:, :], io["rows_norm"][:, D:2 * D]).then_inc(x_in, 16)
                sp.wait_ge(x_in, 48)

            @block.vector
            def _(dve):
                ch = Chain(dve, dve_c)
                dve.wait_ge(rows_in, 16)
                for n in range(8):
                    dve.wait_ge(mod_done, n + 1)
                    part = mod[:, n // 2, (n % 2) * 512:(n % 2) * 512 + 512]
                    nc.vector.tensor_tensor(part, ps[n % 2][:, :], part, ALU.add).then_inc(mod_taken, 1)
                dve.wait_ge(mod_taken, 8)
                dve.wait_ge(x_in, 48)
                ch.add(nc.vector.tensor_scalar(mod[:, 0, :], mod[:, 0, :], 1.0, None, ALU.add))
                ch.add(nc.vector.tensor_scalar(mod[:, 3, :], mod[:, 3, :], 1.0, None, ALU.add))
                ch.link(nc.vector.scalar_tensor_tensor(mod[:, 2, :], mod[:, 2, :], 1.0, t["nffn"][:, :], ALU.add, ALU.mult))

            @block.tensor
            def _(pe):
                for n in range(8):
                    pe.wait_ge(w_in[n % 3], 16 * (n // 3 + 1))
                    if n >= 2:
                        pe.wait_ge(mod_taken, n - 1)
                    w = ring[:, n % 3, :].rearrange("p (k n) -> p k n", k=KT)
                    for k in range(KT):
                        last = nc.tensor.matmul(ps[n % 2][:, :], t["cond_bc"][:, k, :], w[:, k, :],
                                                start=(k == 0), stop=(k == KT - 1))
                    last.then_inc(mod_done, 1)


def phase_e(nc, t, io):
    ps = t["ps"]
    mod, x1 = t["mod2"], t["x1"]
    with ExitStack() as ctx:
        sb = lambda n, s, d=F32: ctx.enter_context(nc.sbuf_tensor(n, s, d, side="right"))
        sem = ctx.enter_context(phase_semaphores(nc))
        wr = sb("pe_wr", [P, KT, NG + NE])
        br = sb("pe_br", [P, NG + NE])
        cst = sb("pe_cst", [P, 2 * P + NG + NE + NE * MAXBLK + MAXBLK // 2])
        entry = sb("pe_entry", [P, 2, NT, 2], I32)
        tmp = sb("pe_tmp", [P, 2, D])
        h2 = sb("pe_h2", [P, 2, D])
        hT = sb("pe_hT", [P, 2, KT, P])
        ss = sb("pe_ss", [P, 3, NT])
        lg = sb("pe_lg", [P, NT, NG + NE])
        R = sb("pe_R", [P, 8, NT])
        g4 = sb("pe_g4", [P, 3, NT, NG])
        e32 = sb("pe_e32", [P, 6, NT, NE])
        dest = sb("pe_dest", [P, 2, NT], I32)
        cum = sb("pe_cum", [P, NT + 1, NE])
        cb = sb("pe_cb", [P, 4, NE])
        cmp_ = sb("pe_cmp", [1, MAXBLK, NE])
        bf = sb("pe_bf", [1, 2, MAXBLK])
        small_in, tab_zero, scattered = sem("pe_small_in"), sem("pe_tab_zero"), sem("pe_scattered")
        mix_done, x1_ready, mix_taken = sem("pe_mix_done"), sem("pe_x1_ready"), sem("pe_mix_taken")
        sq, var_ready, root, h2_ready = sem("pe_sq"), sem("pe_var"), sem("pe_root"), sem("pe_h2_ready")
        h2_out = [sem("pe_h2_out0"), sem("pe_h2_out1")]
        t_done, t_taken, lg_done = sem("pe_t_done"), sem("pe_t_taken"), sem("pe_lg_done")
        x_ready, x_done = sem("pe_x_ready"), sem("pe_x_done")
        cum_ready, rank_done, dest_ready, dve_c = sem("pe_cum"), sem("pe_rank"), sem("pe_dest_ready"), sem("pe_dve")
        ltri, ones = cst[:, 0:P], cst[:, P:2 * P]
        w4, w32 = cst[:, 2 * P:2 * P + NG], cst[:, 2 * P + NG:2 * P + NG + NE]
        c0 = 2 * P + NG + NE
        jrow = cst[0:1, c0:c0 + NE * MAXBLK].rearrange("p (j e) -> p j e", e=NE)
        prow = cst[0:1, c0 + NE * MAXBLK:]
        table = io["slots"]

        def lhs(k, i):
            if k < 3:
                return t["qk"][:, k, i * P:(i + 1) * P]
            if k < 6:
                return t["pB"][:, k - 3, 1 + i * P:1 + (i + 1) * P]
            return t["ycT"][:, k - 6, i * P:(i + 1) * P]

        with nc.Block() as block:
            @block.sync
            def _(sp):
                sp.dma_start(wr[:, :, :], io["w_router"].rearrange("(k p) n -> p k n", p=P)).then_inc(small_in, 16)
                sp.dma_start(br[:, :], io["rows_router"]).then_inc(small_in, 16)
                sp.dma_start(cst[:, :], io["route_cst"]).then_inc(small_in, 16)
                sp.dma_start(entry[:, :, :, :], io["slot_entries"]).then_inc(small_in, 16)
                sp.dma_start(table, io["empty_slots"]).then_inc(tab_zero, 16)
                for i in range(NT):
                    sp.wait_ge(h2_ready, i + 1)
                    sp.dma_start(io["h2"][i * P:(i + 1) * P, :], h2[:, i % 2, :]).then_inc(h2_out[i % 2], 16)
                for u in range(2):
                    sp.wait_ge(h2_out[u], 16 * (NT // 2))

            @block.gpsimd
            def _(pool):
                pool.wait_ge(tab_zero, 16)
                pool.wait_ge(small_in, 64)
                pool.wait_ge(dest_ready, 1)
                for k in range(2):
                    for i in range(NT):
                        nc.gpsimd.indirect_dma_start(
                            out=table, out_offset=bass.IndirectOffsetOnAxis(ap=dest[:, k, i:i + 1], axis=0),
                            in_=entry[:, k, i, :], in_offset=None).then_inc(scattered, 16)
                pool.wait_ge(scattered, 16 * 2 * NT)

            @block.scalar
            def _(act):
                A = nc.scalar.activation
                for i in range(NT + 1):
                    if i < NT:
                        act.wait_ge(x1_ready, i + 1)
                        if i:
                            act.wait_ge(sq, i)
                        A(tmp[:, 1, :], x1[:, i, :], ACT.Square, accum_out=ss[:, 0, i:i + 1]).then_inc(sq, 1)
                        act.wait_ge(var_ready, i + 1)
                        A(ss[:, 1, i:i + 1], ss[:, 1, i:i + 1], ACT.Sqrt).then_inc(root, 1)
                    if i:
                        for g in range(2):
                            act.wait_ge(t_done, 2 * (i - 1) + g + 1)
                            if i >= 3:
                                act.wait_ge(lg_done, i - 2)
                            A(hT[:, (i - 1) % 2, 4 * g:4 * g + 4, :], ps[4 + g][:, :].rearrange("p (k n) -> p k n", k=4),
                              ACT.Copy).then_inc(t_taken, 1)
                act.wait_ge(x_ready, 1)
                A(g4[:, 1, :, :], g4[:, 1, :, :], ACT.Exp).then_inc(x_done, 1)
                act.wait_ge(x_ready, 2)
                A(R[:, 5, :], R[:, 5, :], ACT.Exp).then_inc(x_done, 1)

            @block.vector
            def _(dve):
                ch = Chain(dve, dve_c)
                V = nc.vector
                L = lambda *a: ch.link(V.tensor_tensor(*a))
                dve.wait_ge(small_in, 64)
                for i in range(NT):
                    for hf in range(2):
                        n = slice(hf * 512, hf * 512 + 512)
                        dve.wait_ge(mix_done, 2 * i + hf + 1)
                        V.tensor_tensor(tmp[:, 0, n], ps[hf][:, :], mod[:, 0, n], ALU.mult).then_inc(mix_taken, 1)
                        dve.wait_ge(mix_taken, 2 * i + hf + 1)
                        ch.add(V.tensor_tensor(x1[:, i, n], x1[:, i, n], tmp[:, 0, n], ALU.add))
                    ch.sync()
                    dve.sem_inc(x1_ready, 1)
                    dve.wait_ge(sq, i + 1)
                    V.tensor_scalar(ss[:, 1, i:i + 1], ss[:, 0, i:i + 1], 1.0 / D, NORM_EPS, ALU.mult, ALU.add
                                    ).then_inc(var_ready, 1)
                    dve.wait_ge(root, i + 1)
                    ch.link(V.reciprocal(ss[:, 2, i:i + 1], ss[:, 1, i:i + 1]))
                    if i >= 2:
                        dve.wait_ge(h2_out[i % 2], 16 * (i // 2))
                        dve.wait_ge(t_done, 2 * (i - 1))
                    ch.link(V.scalar_tensor_tensor(h2[:, i % 2, :], x1[:, i, :], ss[:, 2, i:i + 1], mod[:, 2, :],
                                                   ALU.mult, ALU.mult))
                    V.tensor_tensor(h2[:, i % 2, :], h2[:, i % 2, :], mod[:, 1, :], ALU.add).then_inc(h2_ready, 1)
                    if i:
                        dve.wait_ge(lg_done, i)
                        ch.add(V.tensor_tensor(lg[:, i - 1, :], ps[6 + (i - 1) % 2][:, 0:NG + NE], br[:, :], ALU.add))
                dve.wait_ge(lg_done, NT)
                ch.link(V.tensor_tensor(lg[:, NT - 1, :], ps[6 + (NT - 1) % 2][:, 0:NG + NE], br[:, :], ALU.add))
                lg4, lg32 = lg[:, :, 0:NG], lg[:, :, NG:]
                b3 = lambda a, n: a.unsqueeze(2).broadcast_to([P, NT, n])
                r3 = lambda a, n: a.unsqueeze(1).broadcast_to([P, NT, n])
                ch.link(V.tensor_reduce(R[:, 0, :], lg4, AX.X, ALU.max))
                V.tensor_tensor(g4[:, 1, :, :], lg4, b3(R[:, 0, :], NG), ALU.subtract).then_inc(x_ready, 1)
                L(g4[:, 0, :, :], lg4, b3(R[:, 0, :], NG), ALU.is_equal)
                L(g4[:, 0, :, :], g4[:, 0, :, :], r3(w4, NG), ALU.mult)
                ch.link(V.tensor_reduce(R[:, 0, :], g4[:, 0, :, :], AX.X, ALU.max))
                L(g4[:, 0, :, :], g4[:, 0, :, :], b3(R[:, 0, :], NG), ALU.is_equal)
                ch.link(V.tensor_scalar(g4[:, 2, :, :], g4[:, 0, :, :], -1.0, BIG, ALU.add, ALU.mult))
                dve.wait_ge(x_done, 1)
                ch.link(V.tensor_reduce(R[:, 1, :], g4[:, 1, :, :], AX.X, ALU.add))
                ch.link(V.reciprocal(R[:, 1, :], R[:, 1, :]))
                em = e32[:, 0, :, :]
                for i in range(NT):
                    ch.add(V.tensor_tensor(em[:, i, :].rearrange("p (g e) -> p g e", g=NG),
                                           lg32[:, i, :].rearrange("p (g e) -> p g e", g=NG),
                                           g4[:, 2, i, :].unsqueeze(2).broadcast_to([P, NG, EPG]), ALU.add))
                ch.sync()

                def first_largest(oh, src, m):
                    ch.link(V.tensor_reduce(m, src, AX.X, ALU.max))
                    L(oh, src, b3(m, NE), ALU.is_equal)
                    L(oh, oh, r3(w32, NE), ALU.mult)
                    ch.link(V.tensor_reduce(R[:, 7, :], oh, AX.X, ALU.max))
                    L(oh, oh, b3(R[:, 7, :], NE), ALU.is_equal)

                oh1, oh2 = e32[:, 1, :, :], e32[:, 2, :, :]
                first_largest(oh1, em, R[:, 2, :])
                ch.link(V.scalar_tensor_tensor(em, oh1, -3 * BIG, em, ALU.mult, ALU.add))
                first_largest(oh2, em, R[:, 3, :])
                V.tensor_tensor(R[:, 5, :], R[:, 3, :], R[:, 2, :], ALU.subtract).then_inc(x_ready, 1)
                L(e32[:, 3, :, :], oh1, oh2, ALU.add)
                ch.add(V.memset(cum[:, 0, :], 0.0))
                ch.sync()
                for i in range(NT):
                    L(cum[:, i + 1, :], cum[:, i, :], e32[:, 3, i, :], ALU.add)
                dve.sem_inc(cum_ready, 1)
                dve.wait_ge(x_done, 2)
                ch.link(V.tensor_scalar(R[:, 4, :], R[:, 5, :], 1.0, None, ALU.add))
                ch.link(V.reciprocal(R[:, 4, :], R[:, 4, :]))
                L(t["wts"][:, 0, :], R[:, 1, :], R[:, 4, :], ALU.mult)
                L(t["wts"][:, 1, :], t["wts"][:, 0, :], R[:, 5, :], ALU.mult)
                dve.wait_ge(rank_done, 1)
                cnt, nb, end, base = (cb[:, k, :] for k in range(4))
                ch.add(V.tensor_copy(cnt, ps[1][:, 0:NE]))
                ch.link(V.memset(nb, 0.0))
                for k in range(S // P):
                    ch.link(V.scalar_tensor_tensor(nb, cnt, float(P * k), nb, ALU.is_gt, ALU.add))
                ch.link(V.tensor_tensor_scan(end, ones[:, 0:NE], nb, 0.0, ALU.mult, ALU.add))
                L(base, end, nb, ALU.subtract)
                ch.link(V.tensor_scalar(base, base, float(P), None, ALU.mult))
                rb = e32[:, 4, :, :]
                L(rb, ps[0][:, 0:NT * NE].rearrange("p (i e) -> p i e", e=NE), r3(base, NE), ALU.add)
                for k, oh in enumerate((oh1, oh2)):
                    L(e32[:, 5, :, :], oh, rb, ALU.mult)
                    ch.link(V.tensor_reduce(R[:, 6, :], e32[:, 5, :, :], AX.X, ALU.add))
                    ch.link(V.tensor_copy(dest[:, k, :], R[:, 6, :]))
                dve.sem_inc(dest_ready, 1)
                L(cmp_[:, :, :], end[0:1, :].unsqueeze(1).broadcast_to([1, MAXBLK, NE]), jrow, ALU.is_le)
                ch.link(V.tensor_reduce(bf[:, 0, :], cmp_[:, :, :], AX.X, ALU.add))
                ch.link(V.tensor_scalar(bf[:, 0, :], bf[:, 0, :], float(NE - 1), None, ALU.min))
                ch.link(V.tensor_copy(t["blk"][:, 0:MAXBLK], bf[:, 0, :]))
                ch.link(V.tensor_scalar(bf[:, 1, 0:MAXBLK // 2], prow, end[0:1, NE - 1:NE], None, ALU.is_lt))
                ch.link(V.tensor_reduce(bf[:, 0, 0:1], bf[:, 1, 0:MAXBLK // 2], AX.X, ALU.add))
                for k in range(1, 3):
                    ch.link(V.tensor_scalar(bf[:, 0, k:k + 1], bf[:, 0, 0:1], -float(k), None, ALU.add))
                ch.link(V.tensor_copy(t["blk"][:, MAXBLK:MAXBLK + 3], bf[:, 0, 0:3]))

            @block.tensor
            def _(pe):
                pe.wait_ge(small_in, 64)

                def route(i):
                    pe.wait_ge(h2_ready, i + 1)
                    for g in range(2):
                        if i:
                            pe.wait_ge(t_taken, 2 * (i - 1) + g + 1)
                        for k in range(4):
                            last = nc.tensor.transpose(ps[4 + g][:, k * P:(k + 1) * P],
                                                       h2[:, i % 2, (4 * g + k) * P:(4 * g + k + 1) * P], t["ident"][:, :])
                        last.then_inc(t_done, 1)
                    pe.wait_ge(t_taken, 2 * (i + 1))
                    for k in range(KT):
                        last = nc.tensor.matmul(ps[6 + i % 2][:, 0:NG + NE], hT[:, i % 2, k, :], wr[:, k, :],
                                                start=(k == 0), stop=(k == KT - 1))
                    last.then_inc(lg_done, 1)

                for i in range(NT):
                    for hf in range(2):
                        if i:
                            pe.wait_ge(mix_taken, 2 * (i - 1) + hf + 1)
                        for k in range(KT):
                            last = nc.tensor.matmul(ps[hf][:, :], lhs(k, i), t["wout"][:, k, hf * 512:hf * 512 + 512],
                                                    start=(k == 0), stop=(k == KT - 1))
                        last.then_inc(mix_done, 1)
                    if i:
                        route(i - 1)
                route(NT - 1)
                pe.wait_ge(cum_ready, 1)
                for i in range(NT):
                    o = ps[0][:, i * NE:(i + 1) * NE]
                    nc.tensor.matmul(o, ltri, e32[:, 3, i, :], start=True, stop=False)
                    nc.tensor.matmul(o, ones, cum[:, i, :], start=False, stop=True)
                nc.tensor.matmul(ps[1][:, 0:NE], ones, cum[:, NT, :], start=True, stop=True).then_inc(rank_done, 1)


def phase_moe(nc, t, io):
    ps = t["ps"]
    KF = DE // P
    with ExitStack() as ctx:
        sb = lambda n, s, d=F32: ctx.enter_context(nc.sbuf_tensor(n, s, d))
        sem = ctx.enter_context(phase_semaphores(nc))
        w13 = sb("mo_w13", [P, 2, 2, KT * DE])
        w2 = sb("mo_w2", [P, 2, KF * D])
        slot = sb("mo_slot", [P, 2, 2], I32)
        xg = sb("mo_xg", [P, 2, D])
        xT = sb("mo_xT", [P, 2, KT, P])
        th = sb("mo_th", [P, DE])
        hh = sb("mo_hh", [P, 2, DE])
        hT = sb("mo_hT", [P, KF, P])
        yb = sb("mo_y", [P, 2, D])
        w13_in = [sem(f"mo_w13_in{u}") for u in range(2)]
        w2_in = [sem(f"mo_w2_in{u}") for u in range(2)]
        id_in = [sem(f"mo_id_in{u}") for u in range(2)]
        x_in = [sem(f"mo_x_in{u}") for u in range(2)]
        y_out = [sem(f"mo_y_out{u}") for u in range(2)]
        t_done, t_taken, h_done, tanh_done = sem("mo_t_done"), sem("mo_t_taken"), sem("mo_h_done"), sem("mo_tanh")
        hh_ready, ht_done, ht_taken = sem("mo_hh"), sem("mo_ht_done"), sem("mo_ht_taken")
        held = sem("mo_held")
        y_done, y_taken, dve_c = sem("mo_y_done"), sem("mo_y_taken"), sem("mo_dve")
        ident, blk = t["ident"], t["blk"]
        W1 = io["moe_w1"].rearrange("o e (p k) n -> p (o e) (k n)", p=P)
        W3 = io["moe_w3"].rearrange("o e (p k) n -> p (o e) (k n)", p=P)
        W2 = io["moe_w2"].rearrange("o e (p k) n -> p (o e) (k n)", p=P)
        table, ydram = io["slots"], io["y_rows"]

        def rounds_after_first(eng):
            return eng.value_load(blk[0:1, MAXBLK + 1:MAXBLK + 2], min_val=1, max_val=MAXBLK // 2 - 1)

        def rounds_after_second(eng):
            return eng.value_load(blk[0:1, MAXBLK + 2:MAXBLK + 3], min_val=1, max_val=MAXBLK // 2 - 2)

        def at(r, u):
            return 2 * r + u

        with nc.Block() as block:
            @block.sync
            def _(sp):
                def load(r, u, before=None):
                    e = sp.value_load(blk[0:1, bass.ds(at(r, u), 1)], min_val=0, max_val=NE - 1)
                    if before is not None:
                        sp.wait_ge(h_done, at(before, u) + 1)
                    for c, W in enumerate((W1, W3)):
                        sp.dma_start(w13[:, u, c, :], W[:, bass.ds(e, 1), :].rearrange("p a n -> p (a n)")
                                     ).then_inc(w13_in[u], 16)
                    if before is not None:
                        sp.wait_ge(y_done, 2 * at(before, u) + 2)
                    sp.dma_start(w2[:, u, :], W2[:, bass.ds(e, 1), :].rearrange("p a n -> p (a n)")).then_inc(w2_in[u], 16)

                n = rounds_after_first(sp)
                load(0, 0)
                load(0, 1)
                with sp.Fori(0, n) as r:
                    load(r + 1, 0, r)
                    load(r + 1, 1, r)

            @block.gpsimd
            def _(pool):
                def gather(r, u, before=None):
                    if before is not None:
                        pool.wait_ge(t_done, 2 * at(before, u) + 2)
                        pool.wait_ge(y_out[u], 16 * before + 16)
                    pool.dma_start(slot[:, u, :], table[bass.ds(at(r, u) * P, P), :]).then_inc(id_in[u], 16)
                    pool.wait_ge(id_in[u], 16 * r + 16)
                    pool.sem_inc(held, 1)
                    nc.gpsimd.indirect_dma_start(
                        out=xg[:, u, :], out_offset=None, in_=io["h2"],
                        in_offset=bass.IndirectOffsetOnAxis(ap=slot[:, u, 0:1], axis=0)).then_inc(x_in[u], 16)

                def scatter(r, u, before=None):
                    pool.wait_ge(y_taken, 2 * at(r, u) + 2)
                    if before is not None:
                        pool.wait_ge(y_out[1 - u], 16 * before + 16)
                    pool.sem_inc(held, 1)
                    nc.gpsimd.indirect_dma_start(
                        out=ydram, out_offset=bass.IndirectOffsetOnAxis(ap=slot[:, u, 1:2], axis=0),
                        in_=yb[:, u, :], in_offset=None).then_inc(y_out[u], 16)

                n, n2 = rounds_after_first(pool), rounds_after_second(pool)
                gather(0, 0)
                gather(0, 1)
                scatter(0, 0)
                gather(1, 0, 0)
                scatter(0, 1, 0)
                gather(1, 1, 0)
                with pool.Fori(0, n2) as r:
                    scatter(r + 1, 0, r)
                    gather(r + 2, 0, r + 1)
                    scatter(r + 1, 1, r + 1)
                    gather(r + 2, 1, r + 1)
                scatter(n, 0, n2)
                scatter(n, 1, n)
                for u in range(2):
                    pool.wait_ge(y_out[u], 16 * n + 16)

            @block.scalar
            def _(act):
                A = nc.scalar.activation

                def first_part(r, u):
                    j = at(r, u)
                    for g in range(2):
                        act.wait_ge(t_done, 2 * j + g + 1)
                        A(xT[:, u, 4 * g:4 * g + 4, :], ps[g][:, :].rearrange("p (k n) -> p k n", k=4), ACT.Copy
                          ).then_inc(t_taken, 1)
                    act.wait_ge(h_done, j + 1)
                    A(th[:, :], ps[2][:, :], ACT.Tanh, scale=0.5).then_inc(tanh_done, 1)

                def second_part(r, u, before=None):
                    j = at(r, u)
                    act.wait_ge(ht_done, j + 1)
                    A(hT[:, :, :], ps[4][:, :].rearrange("p (k n) -> p k n", k=KF), ACT.Copy).then_inc(ht_taken, 1)
                    if before is not None:
                        act.wait_ge(y_out[u], 16 * before + 16)
                    for g in range(2):
                        act.wait_ge(y_done, 2 * j + g + 1)
                        A(yb[:, u, g * 512:g * 512 + 512], ps[5 + g][:, :], ACT.Copy, scale=0.5).then_inc(y_taken, 1)

                n, n2 = rounds_after_first(act), rounds_after_second(act)
                first_part(0, 0)
                first_part(0, 1)
                second_part(0, 0)
                first_part(1, 0)
                second_part(0, 1)
                first_part(1, 1)
                second_part(1, 0, 0)
                with act.Fori(0, n2) as r:
                    first_part(r + 2, 0)
                    second_part(r + 1, 1, r)
                    first_part(r + 2, 1)
                    second_part(r + 2, 0, r + 1)
                second_part(n, 1, n2)

            @block.vector
            def _(dve):
                V = nc.vector

                def swiglu(r, u):
                    j = at(r, u)
                    dve.wait_ge(tanh_done, j + 1)
                    V.scalar_tensor_tensor(hh[:, u, :], th[:, :], 1.0, ps[2][:, :], ALU.add, ALU.mult).then_inc(dve_c, 1)
                    dve.wait_ge(dve_c, j + 1)
                    V.tensor_tensor(hh[:, u, :], hh[:, u, :], ps[3][:, :], ALU.mult).then_inc(hh_ready, 1)

                n = rounds_after_first(dve)
                swiglu(0, 0)
                swiglu(0, 1)
                with dve.Fori(0, n) as r:
                    swiglu(r + 1, 0)
                    swiglu(r + 1, 1)

            @block.tensor
            def _(pe):
                mm, tr = nc.tensor.matmul, nc.tensor.transpose

                def first_part(r, u, before=None):
                    j = at(r, u)
                    pe.wait_ge(x_in[u], 16 * r + 16)
                    for g in range(2):
                        if before is not None:
                            pe.wait_ge(t_taken, 2 * before + 1 + g)
                        for k in range(4):
                            last = tr(ps[g][:, k * P:(k + 1) * P], xg[:, u, 4 * g + k::KT], ident[:, :])
                        last.then_inc(t_done, 1)
                    pe.wait_ge(t_taken, 2 * j + 2)
                    pe.wait_ge(w13_in[u], 32 * r + 32)
                    if before is not None:
                        pe.wait_ge(hh_ready, before + 1)
                    for k in range(KT):
                        for c in range(2):
                            last = mm(ps[2 + c][:, :], xT[:, u, k, :], w13[:, u, c, k * DE:(k + 1) * DE],
                                      start=(k == 0), stop=(k == KT - 1))
                    last.then_inc(h_done, 1)

                def second_part(r, u, before=None):
                    j = at(r, u)
                    pe.wait_ge(hh_ready, j + 1)
                    for k in range(KF):
                        last = tr(ps[4][:, k * P:(k + 1) * P], hh[:, u, k::KF], ident[:, :])
                    last.then_inc(ht_done, 1)
                    pe.wait_ge(ht_taken, j + 1)
                    pe.wait_ge(w2_in[u], 16 * r + 16)
                    for g in range(2):
                        if before is not None:
                            pe.wait_ge(y_taken, 2 * before + 1 + g)
                        for k in range(KF):
                            last = mm(ps[5 + g][:, :], hT[:, k, :], w2[:, u, k * D + g * 512:k * D + g * 512 + 512],
                                      start=(k == 0), stop=(k == KF - 1))
                        last.then_inc(y_done, 1)

                n = rounds_after_first(pe)
                first_part(0, 0)
                first_part(0, 1, 0)
                second_part(0, 0)
                with pe.Fori(0, n) as r:
                    first_part(r + 1, 0, at(r, 1))
                    second_part(r, 1, at(r, 0))
                    first_part(r + 1, 1, at(r + 1, 0))
                    second_part(r + 1, 0, at(r, 1))
                second_part(n, 1, at(n, 0))


def phase_out(nc, t, io):
    x1 = t["x1"]
    with ExitStack() as ctx:
        sb = lambda n, s, d=F32: ctx.enter_context(nc.sbuf_tensor(n, s, d))
        sem = ctx.enter_context(phase_semaphores(nc))
        nf = sb("po_nf", [P, D])
        yg = sb("po_y", [P, NT, 2, D])
        sq_out = sb("po_sq", [P, D])
        ss = sb("po_ss", [P, 3, NT])
        nf_in, y_in = sem("po_nf_in"), [sem(f"po_y_in{i}") for i in range(NT)]
        x2_ready, sq, var_ready, root, o_ready, out_done = (sem("po_x2"), sem("po_sqs"), sem("po_var"), sem("po_root"),
                                                            sem("po_o"), sem("po_out"))
        dve_c = sem("po_dve")
        out = io["out"].rearrange("b (i p) d -> p (b i) d", p=P)
        with nc.Block() as block:
            @block.sync
            def _(sp):
                sp.dma_start(nf[:, :], io["rows_norm"][:, 2 * D:]).then_inc(nf_in, 16)
                for i in range(NT):
                    for k in range(2):
                        sp.dma_start(yg[:, i, k, :], io["y_rows"][k * S + i * P:k * S + (i + 1) * P, :]
                                     ).then_inc(y_in[i], 16)
                for i in range(NT):
                    sp.wait_ge(o_ready, i + 1)
                    sp.dma_start(out[:, i, :], x1[:, i, :]).then_inc(out_done, 16)
                sp.wait_ge(out_done, 16 * NT)

            @block.scalar
            def _(act):
                for i in range(NT):
                    act.wait_ge(x2_ready, i + 1)
                    if i:
                        act.wait_ge(sq, i)
                    nc.scalar.activation(sq_out[:, :], x1[:, i, :], ACT.Square, accum_out=ss[:, 0, i:i + 1]).then_inc(sq, 1)
                    act.wait_ge(var_ready, i + 1)
                    nc.scalar.activation(ss[:, 1, i:i + 1], ss[:, 1, i:i + 1], ACT.Sqrt).then_inc(root, 1)

            @block.vector
            def _(dve):
                ch = Chain(dve, dve_c)
                V = nc.vector

                def finish(i):
                    dve.wait_ge(sq, i + 1)
                    V.tensor_scalar(ss[:, 1, i:i + 1], ss[:, 0, i:i + 1], 1.0 / D, NORM_EPS, ALU.mult, ALU.add
                                    ).then_inc(var_ready, 1)
                    dve.wait_ge(root, i + 1)
                    ch.link(V.reciprocal(ss[:, 2, i:i + 1], ss[:, 1, i:i + 1]))
                    V.scalar_tensor_tensor(x1[:, i, :], x1[:, i, :], ss[:, 2, i:i + 1], nf[:, :], ALU.mult, ALU.mult
                                           ).then_inc(o_ready, 1)

                dve.wait_ge(nf_in, 16)
                for i in range(NT):
                    dve.wait_ge(y_in[i], 32)
                    a, b = yg[:, i, 0, :], yg[:, i, 1, :]
                    ch.link(V.tensor_scalar(a, a, t["wts"][:, 0, i:i + 1], None, ALU.mult))
                    ch.link(V.scalar_tensor_tensor(a, b, t["wts"][:, 1, i:i + 1], a, ALU.mult, ALU.add))
                    ch.link(V.tensor_tensor(a, a, t["mod2"][:, 3, :], ALU.mult))
                    V.tensor_tensor(x1[:, i, :], x1[:, i, :], a, ALU.add).then_inc(x2_ready, 1)
                    if i:
                        finish(i - 1)
                finish(NT - 1)


def build_program(nc, io):
    io["slots"] = nc.dram_tensor("slots", (SLOTS, 2), I32, kind="Internal").ap()
    io["h2"] = nc.dram_tensor("h2_rows", (S, D), F32, kind="Internal").ap()
    io["y_rows"] = nc.dram_tensor("y_rows", (2 * S + P, D), F32, kind="Internal").ap()
    with ExitStack() as ctx:
        def put(stack, name, shape, dtype=F32, side="left"):
            t[name] = stack.enter_context(nc.sbuf_tensor(name, shape, dtype, side=side))

        t = {"ps": [ctx.enter_context(nc.psum_tensor(f"bank{i}", [P, 512], F32)) for i in range(8)]}
        put(ctx, "ident", [P, P])
        with ExitStack() as late, ExitStack() as mix:
            put(mix, "cols", [P, NCOLS])
            put(mix, "cond", [P, KT])
            put(mix, "cond_bc", [P, KT, P])
            put(mix, "ycT", [P, 2, S])
            with ExitStack() as heads:
                with ExitStack() as norm:
                    put(norm, "hT", [P, KT, S], side="right")
                    phase_norm1(nc, t, io)
                    put(mix, "qk", [P, QA, CONV_K - 1 + S])
                    put(mix, "pB", [P, 11, 1 + S])
                    phase_a(nc, t, io)
                    put(heads, "a_til", [P, QB, S])
                    put(heads, "b_hat", [P, QB, S])
                    put(heads, "bonus", [P, NT, HB])
                    put(heads, "chunk_decay", [P, QB, S // HD])
                    put(heads, "vo", [P, NT, VO])
                    put(heads, "seg64", [P, S])
                    phase_b(nc, t, io)
                phase_c(nc, t, io)
                phase_d(nc, t, io)
            put(late, "x1", [P, NT, D], side="right")
            put(late, "mod2", [P, 4, D], side="right")
            put(late, "wts", [P, 2, NT], side="right")
            put(late, "blk", [1, MAXBLK + 3], I32, side="right")
            with ExitStack() as proj:
                put(proj, "wout", [P, KT, D], side="right")
                put(proj, "nffn", [P, D], side="right")
                phase_mod2(nc, t, io)
                phase_e(nc, t, io)
            mix.close()
            phase_moe(nc, t, io)
            phase_out(nc, t, io)


def host_layout(inp):
    f = np.float32
    a = {k: np.asarray(v) for k, v in inp.items()}
    tile_cols = lambda v: v.reshape(-1, P).T
    cols = np.zeros((P, NCOLS), f)

    def put(name, v):
        lo, hi = COLS[name]
        cols[:v.shape[0], lo:hi] = v

    put("c", tile_cols(a["c"][0]))
    put("conv_w", a["mlstm_conv_w"][0].reshape(CONV_K, QA, P).transpose(2, 1, 0).reshape(P, -1))
    put("conv_b", tile_cols(a["mlstm_conv_b"][0]))
    put("mu", tile_cols(a["rwkv_mu"][0]))
    for name, key in (("w0", "rwkv_w0"), ("a0", "rwkv_a0"), ("k_k", "rwkv_k_k"), ("k_a", "rwkv_k_a"),
                      ("r_k", "rwkv_r_k")):
        put(name, tile_cols(a[key][0].reshape(-1)))
    put("a_re", tile_cols(a["s5_a_re"][0].reshape(-1)))
    put("a_im", tile_cols(a["s5_a_im"][0].reshape(-1)))
    put("log_dt", tile_cols(np.repeat(a["s5_log_dt"][0], P5)))
    put("d5", tile_cols(a["s5_d"][0]))
    put("glu_b", tile_cols(a["s5_glu_b"][0]))
    put("b_i", a["mlstm_b_i"][0][:, None])
    put("b_f", a["mlstm_b_f"][0][:, None])
    s5 = np.zeros((P, 4, QS, 2, GC), f)
    for e in range(2):
        r = slice(e * P5, (e + 1) * P5)
        s5[r, 0, :, e, :] = a["s5_b_re"][0][e::2].transpose(1, 0, 2)
        s5[r, 1, :, e, :] = a["s5_b_im"][0][e::2].transpose(1, 0, 2)
        s5[r, 2, :, e, :] = a["s5_c_re"][0][e::2].transpose(2, 0, 1)
        s5[r, 3, :, e, :] = a["s5_c_im"][0][e::2].transpose(2, 0, 1)
    rows = lambda *v: np.ascontiguousarray(np.broadcast_to(np.concatenate([x.reshape(-1) for x in v]), (P, sum(x.size for x in v))))
    rwkv_cst = np.zeros((P, P + 2), f)
    for e in range(2):
        rwkv_cst[e * HD:(e + 1) * HD, e * HD:(e + 1) * HD] = 1.0
        rwkv_cst[e * HD:(e + 1) * HD, P + e] = 1.0
    s_, t_ = np.arange(P)[:, None], np.arange(P)[None, :]
    same = lambda n: s_ // n == t_ // n
    strict, incl = ((s_ < t_) & same(HD)), ((s_ <= t_) & same(HD))
    u16, rest, l16 = (s_ < t_) & same(16), strict & ~same(16), (s_ > t_) & same(16)
    rwkv_masks = np.concatenate([incl, strict, incl] + [u16] * 3 + [rest] * 3 + [l16] * 3, axis=1).astype(f)
    mc = np.zeros((P, HA + QA + 1, P), f)
    wqk = np.zeros((P, 2, QA, P), f)
    for h in range(HA):
        q, e = divmod(h, 2)
        r = slice(e * HD, (e + 1) * HD)
        mc[h, h, :] = 1.0
        mc[h, HA + q, r] = 1.0
        wqk[r, 0, q, r] = a["mlstm_w_q"][0][h]
        wqk[r, 1, q, r] = a["mlstm_w_k"][0][h]
    mc[:, HA + QA:, :] = np.where(s_ > t_, f(BIG), f(0))[:, None, :]
    token = (np.arange(NT)[None, :] * P + np.arange(P)[:, None]).astype(np.int32)
    entries = np.stack([np.stack([token, token + k * S], axis=2) for k in range(2)], axis=1)
    empty = np.zeros((SLOTS, 2), np.int32)
    empty[:, 1] = 2 * S + np.arange(SLOTS) % P
    route = np.zeros((P, 2 * P + NG + NE + NE * MAXBLK + MAXBLK // 2), f)
    route[:, 0:P] = s_ < t_
    route[:, P:2 * P] = 1.0
    route[:, 2 * P:2 * P + NG] = NG - np.arange(NG)
    route[:, 2 * P + NG:2 * P + NG + NE] = NE - np.arange(NE)
    c0 = 2 * P + NG + NE
    route[0, c0:c0 + NE * MAXBLK] = np.repeat(np.arange(MAXBLK), NE)
    route[0, c0 + NE * MAXBLK:] = 2 * np.arange(MAXBLK // 2)
    out = {
        "moe_w1": a["moe_w1"], "moe_w3": a["moe_w3"], "moe_w2": a["moe_w2"], "w_out": a["w_out"],
        "w_router": np.concatenate([a["moe_w_rg"][0], a["moe_w_re"][0]], axis=1),
        "rows_router": rows(a["moe_b_rg"], a["moe_b_re"]), "route_cst": route,
        "slot_entries": entries, "empty_slots": empty,
        "mlstm_cst": mc.reshape(P, -1), "wqk": wqk, "rows_mlstm": rows(a["mlstm_norm_w"]),
        "rwkv_masks": rwkv_masks, "rows_rwkv": rows(a["rwkv_ln_w"], a["rwkv_ln_b"]), "g_up": a["rwkv_g_up"][0],
        "lora": np.concatenate([a["rwkv_w_up"][0], a["rwkv_a_up"][0]]), "rwkv_cst": rwkv_cst,
        "glu_w": a["s5_glu_w"],
        "x": a["x"], "ada_w": a["ada_w"], "w_in": a["w_in"],
        "cols": cols, "ident": np.eye(P, dtype=f),
        "rows_mod": rows(a["ada_b"]), "rows_norm": rows(a["norm_mix"], a["norm_ffn"], a["norm_final"]),
        "s5_bc": s5.reshape(P, 4, QS * 32),
    }
    return out


def kernel(**inputs):
    import concourse.bacc as bacc
    from concourse.bass_utils import run_bass_kernel_spmd

    nc = bacc.Bacc("TRN2", target_bir_lowering=False, num_devices=1)
    arrays, io = {}, {}
    for name, a in host_layout(inputs).items():
        a = np.ascontiguousarray(a)
        arrays[f"in_{name}"] = a
        io[name] = nc.dram_tensor(f"in_{name}", a.shape, mybir.dt.from_np(a.dtype), kind="ExternalInput").ap()
    io["out"] = nc.dram_tensor("out_y", (1, S, D), F32, kind="ExternalOutput").ap()
    build_program(nc, io)
    r = run_bass_kernel_spmd(nc, [arrays], core_ids=[0])
    return r.results[0]["out_y"]
```

```python
from contextlib import ExitStack, contextmanager

import numpy as np

import concourse.bass as bass
from concourse import mybir

F32 = mybir.dt.float32
I32 = mybir.dt.int32
ALU = mybir.AluOpType
ACT = mybir.ActivationFunctionType
AX = mybir.AxisListType

P = 128
D = 1024
S = 1024
KT = D // P
NT = S // P
HD = 64
DA, DB, DC = 384, 384, 256
HA, HB = DA // HD, DB // HD
QA = DA // P
QB = DB // P
CONV_K = 4
C_QK, C_VO, C_R, C_LORA, C_U = 0, DA, 3 * DA + 2 * HA, 3 * DA + 2 * HA + 3 * DB, 3 * DA + 2 * HA + 3 * DB + 256
VO = 2 * DA + 2 * HA
IN_COLS = C_U + DC
G5, P5, GC = 16, 64, 16
QS = G5 // 2
J5, M5 = 8, S // 8
NG, EPG, NE = 4, 8, 32
DE = 512
BT = 96
MAXBLK = 2 * -(-((2 * S + NE * (BT - 1)) // BT) // 2)
SLOTS = MAXBLK * BT
BIG = 1.0e30
NORM_EPS, HEAD_EPS, GN_EPS = 1e-6, 1e-5, 64e-5
RWKV_DECAY = -0.5 * float(np.exp(-0.5))

COLS = {}
_n = 0
for _name, _w in (("c", KT), ("conv_w", QA * CONV_K), ("conv_b", QA), ("mu", 11), ("w0", QB), ("a0", QB),
                  ("k_k", QB), ("k_a", QB), ("r_k", QB), ("a_re", QS), ("a_im", QS), ("log_dt", QS),
                  ("d5", G5), ("glu_b", 2), ("b_i", 1), ("b_f", 1)):
    COLS[_name] = (_n, _n + _w)
    _n += _w
NCOLS = _n


class Chain:

    def __init__(self, eng, sem):
        self.eng, self.sem, self.n = eng, sem, 0

    def add(self, ins):
        ins.then_inc(self.sem, 1)
        self.n += 1

    def sync(self):
        if self.n:
            self.eng.wait_ge(self.sem, self.n)

    def link(self, ins):
        self.add(ins)
        self.sync()


@contextmanager
def phase_semaphores(nc):
    taken = []

    def sem(name):
        taken.append(nc.alloc_semaphore(name))
        return taken[-1]

    yield sem
    nc.clear_and_free_semaphores(taken)
    nc.all_engine_barrier()


def col(t, name, i=0, n=1):
    a = COLS[name][0] + i
    return t["cols"][:, a:a + n]


def phase_norm1(nc, t, io):
    ps = t["ps"]
    with ExitStack() as ctx:
        sb = lambda n, s, d=F32: ctx.enter_context(nc.sbuf_tensor(n, s, d))
        sem = ctx.enter_context(phase_semaphores(nc))
        ring = sb("ada_ring", [P, 3, KT * 512])
        xs = sb("n1_x", [P, NT, D])
        h = sb("n1_h", [P, 2, D])
        junk = sb("n1_junk", [P, D])
        mod = sb("n1_mod", [P, 2, D])
        scale = sb("n1_scale", [P, D])
        ss = sb("n1_ss", [P, NT])
        rstd = sb("n1_rstd", [P, NT])
        const_in, x_in = sem("n1_const_in"), [sem(f"n1_x_in{i}") for i in range(4)]
        w_in = [sem(f"n1_ada_in{i}") for i in range(3)]
        cond_tanh, cond_ready = sem("n1_cond_tanh"), sem("n1_cond_ready")
        mod_done, mod_taken = sem("n1_mod_done"), sem("n1_mod_taken")
        sums_ready, var_ready, root_ready = sem("n1_sums"), sem("n1_var"), sem("n1_root")
        h_ready, tr_done, tr_taken = sem("n1_h_ready"), sem("n1_tr_done"), sem("n1_tr_taken")
        dve_c, = [sem("n1_dve")]
        ada = io["ada_w"].rearrange("o (k p) n -> p (o k) n", p=P)
        x = io["x"].rearrange("b (i p) d -> p (b i) d", p=P)
        with nc.Block() as block:
            @block.sync
            def _(sp):
                sp.dma_start(t["cols"][:, :], io["cols"]).then_inc(const_in, 16)
                sp.dma_start(t["ident"][:, :], io["ident"]).then_inc(const_in, 16)
                sp.dma_start(mod[:, :, :], io["rows_mod"][:, 0:2 * D].rearrange("p (a d) -> p a d", a=2)
                             ).then_inc(const_in, 16)
                sp.dma_start(scale[:, :], io["rows_norm"][:, 0:D]).then_inc(const_in, 16)
                for n in range(4):
                    if n >= 3:
                        sp.wait_ge(mod_done, n - 2)
                    sp.dma_start(ring[:, n % 3, :].rearrange("p (k n) -> p k n", k=KT),
                                 ada[:, :, n * 512:(n + 1) * 512]).then_inc(w_in[n % 3], 16)
                    sp.dma_start(xs[:, 2 * n:2 * n + 2, :], x[:, 2 * n:2 * n + 2, :]).then_inc(x_in[n], 16)

            @block.scalar
            def _(act):
                act.wait_ge(const_in, 64)
                nc.scalar.activation(t["cond"][:, :], col(t, "c", 0, KT), ACT.Tanh, scale=0.5).then_inc(cond_tanh, 1)
                for i in range(NT):
                    act.wait_ge(x_in[i // 2], 16)
                    if i:
                        act.wait_ge(sums_ready, i)
                    nc.scalar.activation(junk[:, :], xs[:, i, :], ACT.Square,
                                         accum_out=ss[:, i:i + 1]).then_inc(sums_ready, 1)
                act.wait_ge(var_ready, 1)
                nc.scalar.activation(rstd[:, :], ss[:, :], ACT.Sqrt).then_inc(root_ready, 1)
                for g in range(2 * NT):
                    i, half = divmod(g, 2)
                    act.wait_ge(tr_done, g + 1)
                    nc.scalar.activation(t["hT"][:, 4 * half:4 * half + 4, i * P:(i + 1) * P],
                                         ps[4 + g % 4][:, :].rearrange("p (k n) -> p k n", k=4),
                                         ACT.Copy).then_inc(tr_taken, 1)

            @block.vector
            def _(dve):
                ch = Chain(dve, dve_c)
                dve.wait_ge(cond_tanh, 1)
                ch.link(dve.scalar_tensor_tensor(t["cond"][:, :], t["cond"][:, :], 1.0, col(t, "c", 0, KT),
                                                 ALU.add, ALU.mult))
                ch.link(dve.memset(t["cond_bc"][:, :, :], 0.5))
                for k in range(KT):
                    last = dve.tensor_scalar(t["cond_bc"][:, k, :], t["cond_bc"][:, k, :], t["cond"][:, k:k + 1], None,
                                             ALU.mult)
                    ch.add(last)
                ch.sync()
                dve.sem_inc(cond_ready, 1)
                for n in range(4):
                    dve.wait_ge(mod_done, n + 1)
                    part = mod[:, n // 2, (n % 2) * 512:(n % 2) * 512 + 512]
                    ins = dve.tensor_tensor(part, ps[n % 2][:, :], part, ALU.add)
                    ins.then_inc(mod_taken, 1)
                dve.wait_ge(mod_taken, 4)
                ch.link(dve.scalar_tensor_tensor(scale[:, :], mod[:, 1, :], 1.0, scale[:, :], ALU.add, ALU.mult))
                dve.wait_ge(sums_ready, NT)
                dve.tensor_scalar(ss[:, :], ss[:, :], 1.0 / D, NORM_EPS, ALU.mult, ALU.add).then_inc(var_ready, 1)
                dve.wait_ge(root_ready, 1)
                ch.link(dve.reciprocal(rstd[:, :], rstd[:, :]))
                for i in range(NT):
                    if i >= 2:
                        dve.wait_ge(tr_done, 2 * (i - 1))
                    ch.link(dve.scalar_tensor_tensor(h[:, i % 2, :], xs[:, i, :], rstd[:, i:i + 1], scale[:, :],
                                                     ALU.mult, ALU.mult))
                    dve.tensor_tensor(h[:, i % 2, :], h[:, i % 2, :], mod[:, 0, :], ALU.add).then_inc(h_ready, 1)

            @block.tensor
            def _(pe):
                pe.wait_ge(cond_ready, 1)
                for n in range(4):
                    pe.wait_ge(w_in[n % 3], 16 * (n // 3 + 1))
                    if n >= 2:
                        pe.wait_ge(mod_taken, n - 1)
                    w = ring[:, n % 3, :].rearrange("p (k n) -> p k n", k=KT)
                    for k in range(KT):
                        last = nc.tensor.matmul(ps[n % 2][:, :], t["cond_bc"][:, k, :], w[:, k, :],
                                                start=(k == 0), stop=(k == KT - 1))
                    last.then_inc(mod_done, 1)
                for g in range(2 * NT):
                    i, half = divmod(g, 2)
                    pe.wait_ge(h_ready, i + 1)
                    if g >= 4:
                        pe.wait_ge(tr_taken, g - 3)
                    for k in range(4):
                        a = (4 * half + k) * P
                        last = nc.tensor.transpose(ps[4 + g % 4][:, k * P:(k + 1) * P], h[:, i % 2, a:a + P],
                                                   t["ident"][:, :])
                    last.then_inc(tr_done, 1)


def phase_a(nc, t, io):
    ps = t["ps"]
    with ExitStack() as ctx:
        sb = lambda n, s, d=F32: ctx.enter_context(nc.sbuf_tensor(n, s, d))
        sem = ctx.enter_context(phase_semaphores(nc))
        ring = sb("pa_ring", [P, 2, KT, 384])
        chunks = sb("pa_chunks", [P, J5 * DC])
        um = chunks[:, :].rearrange("p (g j c) -> p g j c", g=G5, j=J5)
        ym = chunks[:, :].rearrange("p (j n) -> p j n", j=J5)
        us = sb("pa_us", [P, G5, M5])
        braw = sb("pa_b", [P, 4, QS, GC])
        bb = sb("pa_bb", [P, 2, QS, GC])
        co = sb("pa_co", [P, 16, QS])
        coi = sb("pa_coi", [P, QS], I32)
        pw = sb("pa_pw", [P, 2, QS, J5 + 1])
        pr = sb("pa_pr", [P, 2, QS, J5])
        ws = sb("pa_ws", [P, 2, QS, P])
        wt = sb("pa_wt", [P, QS, 2, P])
        cl = sb("pa_cl", [P, 2, QS, J5 + 1, GC])
        turn = sb("pa_turn", [P, 2, QS, M5])
        tmp = sb("pa_tmp", [P, 2, QS * (J5 + 1) * GC])
        kt = sb("pa_kt", [GC, G5, P])
        tz = sb("pa_tz", [P, G5, P])
        xb = sb("pa_xb", [P, 2, QS, 1 + M5])
        w_in = [sem(f"pa_w_in{i}") for i in range(2)]
        small_in, pads = sem("pa_small_in"), sem("pa_pads")
        u_done, u_taken, us_done, us_taken = sem("pa_u_done"), sem("pa_u_taken"), sem("pa_us_done"), sem("pa_us_taken")
        proj_done, proj_taken = sem("pa_proj_done"), sem("pa_proj_taken")
        dt_ready, act_dt, ang_ready, act_sin = sem("pa_dt"), sem("pa_actdt"), sem("pa_ang"), sem("pa_sin")
        ws_ready, wt_done, wt_taken, e_done = sem("pa_ws_ready"), sem("pa_wt_done"), sem("pa_wt_taken"), sem("pa_e_done")
        cl_ready, k_done, k_taken, k_ready, tz_in = (sem("pa_cl_ready"), sem("pa_k_done"), sem("pa_k_taken"),
                                                     sem("pa_k_ready"), sem("pa_tz_in"))
        x_ready, y_done, y_taken = sem("pa_x_ready"), sem("pa_y_done"), sem("pa_y_taken")
        yt_done, yt_taken, dve_c = sem("pa_yt_done"), sem("pa_yt_taken"), sem("pa_dve")
        w = io["w_in"].rearrange("o (k p) n -> p (o k) n", p=P)
        blocks = [(C_U, 2), (C_R, 3), (C_R + DB, 3), (C_R + 2 * DB, 3), (C_LORA, 2)]
        tiles = [(b, m) for b, (_, n) in enumerate(blocks) for m in range(n)][2:]
        prev_tiles = [sum(n for _, n in blocks[1:b]) for b in range(len(blocks))]
        WT_AT, E_AT, Y_AT, YT_AT = 1, 2, 6, 7

        with nc.Block() as block:
            @block.sync
            def _(sp):
                for b, (c0, n) in enumerate(blocks):
                    if b == 1:
                        sp.dma_start(braw[:, :, :, :], io["s5_bc"]).then_inc(small_in, 16)
                    if b == 2:
                        sp.wait_ge(u_done, J5)
                    if b > 2:
                        sp.wait_ge(proj_done, 2 * prev_tiles[b - 1])
                    sp.dma_start(ring[:, b % 2, :, 0:n * P], w[:, :, c0:c0 + n * P]).then_inc(w_in[b % 2], 16)
                sp.wait_ge(k_ready, 1)
                sp.wait_ge(pads, 3)
                for j in range(J5):
                    sp.dma_start(tz[j * GC:(j + 1) * GC, :, j * GC:], kt[:, :, 0:P - j * GC]).then_inc(tz_in, 16)

            @block.gpsimd
            def _(pool):
                nc.gpsimd.memset(t["pB"][:, :, 0:1], 0.0).then_inc(pads, 1)
                nc.gpsimd.memset(xb[:, :, :, 0:1], 0.0).then_inc(pads, 1)
                nc.gpsimd.memset(tz[:, :, :], 0.0).then_inc(pads, 1)

            @block.scalar
            def _(act):
                A = nc.scalar.activation
                A(co[:, 0, :], col(t, "log_dt", 0, QS), ACT.Exp).then_inc(act_dt, 1)
                act.wait_ge(dt_ready, 1)
                A(co[:, 2, :], co[:, 1, :], ACT.Exp).then_inc(act_dt, 1)
                act.wait_ge(ang_ready, 1)
                A(co[:, 5, :], co[:, 5, :], ACT.Sin).then_inc(act_sin, 1)
                A(co[:, 6, :], co[:, 6, :], ACT.Sin).then_inc(act_sin, 1)
                for j in range(J5):
                    act.wait_ge(u_done, j + 1)
                    A(um[:, :, j, :], ps[j % 2][:, 0:DC].rearrange("p (g c) -> p g c", g=G5), ACT.Copy).then_inc(u_taken, 1)
                for b in range(4):
                    act.wait_ge(us_done, b + 1)
                    A(us[:, 4 * b:4 * b + 4, :].rearrange("p g m -> p (g m)"), ps[2 + b][:, :], ACT.Copy).then_inc(us_taken, 1)
                for mt in range(len(tiles)):
                    for half in range(2):
                        g = 2 * mt + half
                        act.wait_ge(proj_done, g + 1)
                        A(t["pB"][:, mt, 1 + half * 512:1 + (half + 1) * 512], ps[g % 2][:, :], ACT.Copy).then_inc(proj_taken, 1)
                    if mt == WT_AT:
                        for b in range(4):
                            act.wait_ge(wt_done, b + 1)
                            A(wt[:, 2 * b:2 * b + 2, :, :].rearrange("p q c n -> p (q c n)"), ps[2 + b][:, :], ACT.Copy
                              ).then_inc(wt_taken, 1)
                    if mt == E_AT:
                        for i in range(4):
                            act.wait_ge(k_done, i + 1)
                            A(kt[:, 8 * (i // 2) + i % 2:8 * (i // 2) + 8:2, :],
                              ps[6 + i % 2][0:GC, :].rearrange("p (q n) -> p q n", q=4), ACT.Copy).then_inc(k_taken, 1)
                    if mt == Y_AT:
                        for i in range(4):
                            act.wait_ge(y_done, i + 1)
                            for q in range(4):
                                g = 8 * (i // 2) + 2 * q + i % 2
                                last = A(ym[:, :, g * GC:(g + 1) * GC],
                                         ps[6 + i % 2][:, q * P:(q + 1) * P].rearrange("p (j c) -> p j c", j=J5), ACT.Copy)
                            last.then_inc(y_taken, 1)
                    if mt == YT_AT:
                        for b in range(4):
                            act.wait_ge(yt_done, b + 1)
                            out = t["ycT"][:, b // 2, :].rearrange("p (m j) -> p j m", j=J5)
                            A(out[:, 4 * (b % 2):4 * (b % 2) + 4, :], ps[2 + b][:, :].rearrange("p (j m) -> p j m", j=4),
                              ACT.Copy).then_inc(yt_taken, 1)

            @block.vector
            def _(dve):
                ch = Chain(dve, dve_c)
                V = nc.vector
                tt = lambda o, a, b, op: ch.add(V.tensor_tensor(o, a, b, op))
                LT = lambda o, a, b, op: ch.link(V.tensor_tensor(o, a, b, op))
                are, aim = col(t, "a_re", 0, QS), col(t, "a_im", 0, QS)
                dve.wait_ge(act_dt, 1)
                V.tensor_tensor(co[:, 1, :], are, co[:, 0, :], ALU.mult).then_inc(dt_ready, 1)
                LT(co[:, 3, :], aim, co[:, 0, :], ALU.mult)
                ch.link(V.tensor_scalar(co[:, 4, :], co[:, 3, :], float(1 / (2 * np.pi)), None, ALU.mult))
                ch.link(V.tensor_copy(coi[:, :], co[:, 4, :]))
                ch.link(V.tensor_copy(co[:, 4, :], coi[:, :]))
                ch.link(V.scalar_tensor_tensor(co[:, 3, :], co[:, 4, :], -6.28125, co[:, 3, :], ALU.mult, ALU.add))
                ch.link(V.scalar_tensor_tensor(co[:, 3, :], co[:, 4, :], -float(2 * np.pi - 6.28125), co[:, 3, :],
                                               ALU.mult, ALU.add))

                def wrap(x, tmp):
                    ch.link(V.tensor_scalar(tmp, x, float(np.pi), -float(2 * np.pi), ALU.is_gt, ALU.mult))
                    LT(x, x, tmp, ALU.add)
                    ch.link(V.tensor_scalar(tmp, x, -float(np.pi), float(2 * np.pi), ALU.is_lt, ALU.mult))
                    LT(x, x, tmp, ALU.add)

                wrap(co[:, 3, :], co[:, 4, :])
                ch.link(V.tensor_scalar(co[:, 6, :], co[:, 3, :], float(np.pi / 2), None, ALU.add))
                wrap(co[:, 6, :], co[:, 4, :])
                lim = 3.1415925
                ch.link(V.tensor_scalar(co[:, 5, :], co[:, 3, :], lim, -lim, ALU.min, ALU.max))
                V.tensor_scalar(co[:, 6, :], co[:, 6, :], lim, -lim, ALU.min, ALU.max).then_inc(ang_ready, 1)
                dve.wait_ge(act_dt, 2)
                dve.wait_ge(act_sin, 2)
                ch.add(V.memset(pw[:, 0, :, 0], 1.0))
                ch.add(V.memset(pw[:, 1, :, 0], 0.0))
                tt(pw[:, 0, :, 1], co[:, 2, :], co[:, 6, :], ALU.mult)
                LT(pw[:, 1, :, 1], co[:, 2, :], co[:, 5, :], ALU.mult)
                tt(co[:, 7, :], are, are, ALU.mult)
                LT(co[:, 8, :], aim, aim, ALU.mult)
                LT(co[:, 7, :], co[:, 7, :], co[:, 8, :], ALU.add)
                ch.link(V.reciprocal(co[:, 7, :], co[:, 7, :]))
                ch.link(V.tensor_scalar(co[:, 8, :], pw[:, 0, :, 1], -1.0, None, ALU.add))
                tt(co[:, 9, :], co[:, 8, :], are, ALU.mult)
                tt(co[:, 10, :], pw[:, 1, :, 1], aim, ALU.mult)
                tt(co[:, 11, :], pw[:, 1, :, 1], are, ALU.mult)
                LT(co[:, 12, :], co[:, 8, :], aim, ALU.mult)
                tt(co[:, 9, :], co[:, 9, :], co[:, 10, :], ALU.add)
                LT(co[:, 11, :], co[:, 11, :], co[:, 12, :], ALU.subtract)
                tt(co[:, 9, :], co[:, 9, :], co[:, 7, :], ALU.mult)
                LT(co[:, 11, :], co[:, 11, :], co[:, 7, :], ALU.mult)
                dve.wait_ge(small_in, 16)

                def cmul(ore, oim, xre, xim, yre, yim, t0, t1, sign=1):
                    minus, plus = (ALU.subtract, ALU.add) if sign > 0 else (ALU.add, ALU.subtract)
                    tt(t0, xim, yim, ALU.mult)
                    LT(t1, xre, yim, ALU.mult)
                    tt(ore, xre, yre, ALU.mult)
                    LT(oim, xim, yre, ALU.mult)
                    tt(ore, ore, t0, minus)
                    LT(oim, oim, t1, plus)

                def scratch(*dims):
                    n = int(np.prod(dims))
                    names = "qab"[:len(dims)]
                    spec = f"p ({' '.join(names)}) -> p {' '.join(names)}"
                    sizes = dict(zip(names, dims))
                    return [tmp[:, c, 0:n].rearrange(spec, **sizes) for c in range(2)]

                over = lambda a, n: a.unsqueeze(2).broadcast_to([P, QS, n])
                over_c = lambda a, n: a.unsqueeze(3).broadcast_to([P, QS, n, GC])
                over_j = lambda a, n: a.unsqueeze(2).broadcast_to([P, QS, n, GC])
                cmul(bb[:, 0, :, :], bb[:, 1, :, :], braw[:, 0, :, :], braw[:, 1, :, :],
                     over(co[:, 9, :], GC), over(co[:, 11, :], GC), *scratch(QS, GC))
                for n in (1, 2, 4):
                    cmul(pw[:, 0, :, n + 1:2 * n + 1], pw[:, 1, :, n + 1:2 * n + 1], pw[:, 0, :, 1:n + 1],
                         pw[:, 1, :, 1:n + 1], over(pw[:, 0, :, n], n), over(pw[:, 1, :, n], n), *scratch(QS, n))
                for j in range(J5):
                    ch.add(V.tensor_copy(pr[:, :, :, j], pw[:, :, :, J5 - 1 - j]))
                ch.sync()
                W4 = lambda c: ws[:, c, :, :].rearrange("p q (j c) -> p q j c", j=J5)
                cmul(W4(0), W4(1), over_c(pr[:, 0, :, :], J5), over_c(pr[:, 1, :, :], J5),
                     over_j(bb[:, 0, :, :], J5), over_j(bb[:, 1, :, :], J5), *scratch(QS, J5, GC))
                dve.sem_inc(ws_ready, 1)
                n = J5 + 1
                cmul(cl[:, 0, :, :, :], cl[:, 1, :, :, :], over_c(pw[:, 0, :, :], n), over_c(pw[:, 1, :, :], n),
                     over_j(braw[:, 2, :, :], n), over_j(braw[:, 3, :, :], n), *scratch(QS, n, GC))
                V.tensor_scalar(cl[:, 1, :, :, :], cl[:, 1, :, :, :], -1.0, None, ALU.mult).then_inc(cl_ready, 1)
                ch.add(V.tensor_copy(co[:, 13, :], co[:, 6, :]))
                ch.add(V.tensor_copy(co[:, 14, :], co[:, 5, :]))
                ch.link(V.tensor_copy(co[:, 15, :], co[:, 2, :]))
                unit = co[:, 13, :], co[:, 14, :]
                for _ in range(3):
                    ch.add(V.tensor_tensor(co[:, 15, :], co[:, 15, :], co[:, 15, :], ALU.mult))
                    cmul(co[:, 3, :], co[:, 4, :], *unit, *unit, co[:, 0, :], co[:, 1, :])
                    ch.add(V.tensor_copy(unit[0], co[:, 3, :]))
                    ch.link(V.tensor_copy(unit[1], co[:, 4, :]))
                ch.add(V.memset(turn[:, 0, :, 0], 1.0))
                ch.add(V.memset(turn[:, 1, :, 0], 0.0))
                ch.sync()
                n = 1
                while n < M5:
                    cmul(turn[:, 0, :, n:2 * n], turn[:, 1, :, n:2 * n], turn[:, 0, :, 0:n], turn[:, 1, :, 0:n],
                         over(unit[0], n), over(unit[1], n), *scratch(QS, n))
                    n *= 2
                    if n < M5:
                        cmul(co[:, 3, :], co[:, 4, :], *unit, *unit, co[:, 0, :], co[:, 1, :])
                        ch.add(V.tensor_copy(unit[0], co[:, 3, :]))
                        ch.link(V.tensor_copy(unit[1], co[:, 4, :]))
                dve.wait_ge(k_taken, 4)
                eye = t["ident"][0:GC, 0:GC].unsqueeze(1).broadcast_to([GC, G5, GC])
                d5 = col(t, "d5", 0, G5)[0:GC, :].unsqueeze(2).broadcast_to([GC, G5, GC])
                diag = tmp[0:GC, 0, 0:G5 * GC].rearrange("p (g c) -> p g c", g=G5)
                LT(diag, eye, d5, ALU.mult)
                V.tensor_tensor(kt[:, :, 0:GC], kt[:, :, 0:GC], diag, ALU.add).then_inc(k_ready, 1)
                dve.wait_ge(k_ready, 1)
                dve.wait_ge(e_done, 1)
                for h in range(2):
                    q4 = slice(4 * h, 4 * h + 4)
                    E = lambda c: ps[2 + 2 * c + h][:, :].rearrange("p (q m) -> p q m", q=4)
                    s0, s1 = (tmp[:, c, 512 * h:512 * h + 512].rearrange("p (q m) -> p q m", q=4) for c in range(2))
                    cmul(ws[:, 0, q4, :], ws[:, 1, q4, :], E(0), E(1), turn[:, 0, q4, :], turn[:, 1, q4, :], s0, s1, -1)
                for q in range(QS):
                    for c in range(2):
                        ch.add(V.tensor_tensor_scan(ws[:, c, q, :], co[:, 15, q:q + 1].broadcast_to([P, M5]),
                                                    ws[:, c, q, :], 0.0, ALU.mult, ALU.add))
                ch.sync()
                dve.wait_ge(pads, 3)
                cmul(xb[:, 0, :, 1:], xb[:, 1, :, 1:], ws[:, 0, :, :], ws[:, 1, :, :], turn[:, 0, :, :], turn[:, 1, :, :],
                     *scratch(QS, M5))
                dve.sem_inc(x_ready, 1)

            @block.tensor
            def _(pe):
                mm, tr, ident = nc.tensor.matmul, nc.tensor.transpose, t["ident"][:, :]
                pe.wait_ge(w_in[0], 16)
                for j in range(J5):
                    if j >= 2:
                        pe.wait_ge(u_taken, j - 1)
                    for k in range(KT):
                        last = mm(ps[j % 2][:, 0:DC], t["hT"][:, k, j::J5], ring[:, 0, k, 0:DC],
                                  start=(k == 0), stop=(k == KT - 1))
                    last.then_inc(u_done, 1)
                pe.wait_ge(u_taken, J5)
                for g in range(G5):
                    last = tr(ps[2 + g // 4][:, (g % 4) * P:(g % 4 + 1) * P], um[:, g, :, :].rearrange("p j c -> p (j c)"), ident)
                    if g % 4 == 3:
                        last.then_inc(us_done, 1)
                for mt, (b, m) in enumerate(tiles):
                    if m == 0:
                        pe.wait_ge(w_in[b % 2], 16 * (b // 2 + 1))
                    for half in range(2):
                        g = 2 * mt + half
                        if g >= 2:
                            pe.wait_ge(proj_taken, g - 1)
                        for k in range(KT):
                            last = mm(ps[g % 2][:, :], ring[:, b % 2, k, m * P:(m + 1) * P],
                                      t["hT"][:, k, half * 512:half * 512 + 512], start=(k == 0), stop=(k == KT - 1))
                        last.then_inc(proj_done, 1)
                    if mt == WT_AT:
                        pe.wait_ge(ws_ready, 1)
                        for i in range(2 * QS):
                            q, c = divmod(i, 2)
                            if i % 4 == 0:
                                pe.wait_ge(us_taken, i // 4 + 1)
                            last = tr(ps[2 + i // 4][:, (i % 4) * P:(i % 4 + 1) * P], ws[:, c, q, :], ident)
                            if i % 4 == 3:
                                last.then_inc(wt_done, 1)
                    if mt == E_AT:
                        pe.wait_ge(wt_taken, 4)
                        for q in range(QS):
                            for c in range(2):
                                for e in range(2):
                                    last = mm(ps[2 + 2 * c + q // 4][e * P5:(e + 1) * P5, (q % 4) * P:(q % 4 + 1) * P],
                                              wt[:, q, c, e * P5:(e + 1) * P5], us[:, 2 * q + e, :], start=True, stop=True)
                        last.then_inc(e_done, 1)
                        pe.wait_ge(cl_ready, 1)
                        for i in range(4):
                            h, e = divmod(i, 2)
                            r = slice(e * P5, (e + 1) * P5)
                            if h:
                                pe.wait_ge(k_taken, e + 1)
                            for q in range(4 * h, 4 * h + 4):
                                for c in range(2):
                                    last = mm(ps[6 + e][0:GC, (q % 4) * P:(q % 4 + 1) * P], bb[r, c, q, :],
                                              cl[r, c, q, 0:J5, :].rearrange("p l c -> p (l c)"),
                                              start=(c == 0), stop=(c == 1))
                            last.then_inc(k_done, 1)
                    if mt == Y_AT:
                        pe.wait_ge(k_taken, 4)
                        pe.wait_ge(tz_in, 16 * J5)
                        pe.wait_ge(x_ready, 1)
                        for i in range(4):
                            h, e = divmod(i, 2)
                            r = slice(e * P5, (e + 1) * P5)
                            if h:
                                pe.wait_ge(y_taken, e + 1)
                            for q in range(4 * h, 4 * h + 4):
                                o = ps[6 + e][:, (q % 4) * P:(q % 4 + 1) * P]
                                mm(o, us[:, 2 * q + e, :], tz[:, 2 * q + e, :], start=True, stop=False)
                                for c in range(2):
                                    last = mm(o, xb[r, c, q, 0:M5], cl[r, c, q, 1:, :].rearrange("p l c -> p (l c)"),
                                              start=False, stop=(c == 1))
                            last.then_inc(y_done, 1)
                    if mt == YT_AT:
                        pe.wait_ge(y_taken, 4)
                        for i in range(16):
                            last = tr(ps[2 + i // 4][:, (i % 4) * P:(i % 4 + 1) * P],
                                      ym[:, i % J5, (i // J5) * P:(i // J5 + 1) * P], ident)
                            if i % 4 == 3:
                                last.then_inc(yt_done, 1)


def phase_b(nc, t, io):
    ps = t["ps"]
    pB, at, bt, bonus, ec = t["pB"], t["a_til"], t["b_hat"], t["bonus"], t["chunk_decay"]
    with ExitStack() as ctx:
        sb = lambda n, s, d=F32: ctx.enter_context(nc.sbuf_tensor(n, s, d, side="right"))
        sem = ctx.enter_context(phase_semaphores(nc))
        ring = sb("pb_ring", [P, 2, KT, VO // 2])
        lora = sb("pb_lora", [P, DB])
        gluw = sb("pb_glu", [P, 2, DC])
        cst = sb("pb_cst", [P, P + 2])
        hcol = sb("pb_hcol", [P, 3, QB])
        T = sb("pb_t", [P, 5, S])
        w_in_s = [sem(f"pb_w_in{i}") for i in range(2)]
        small_in = sem("pb_small_in")
        proj_done, proj_taken = sem("pb_proj_done"), sem("pb_proj_taken")
        seg_ready, lora_ready, lora_tanh = sem("pb_seg"), sem("pb_lora_ready"), sem("pb_lora_tanh")
        z_done, z_taken = sem("pb_z_done"), sem("pb_z_taken")
        ell_ready, exps = sem("pb_ell_ready"), sem("pb_exps")
        kk_ready, sq_ready, ss_done, ss_taken, root = (sem("pb_kk"), sem("pb_sq"), sem("pb_ss_done"),
                                                       sem("pb_ss_taken"), sem("pb_root"))
        rk_ready, bon_done, bon_taken, q_free = sem("pb_rk"), sem("pb_bon_done"), sem("pb_bon_taken"), sem("pb_q_free")
        g_sq, g_in, g_tanh, z2_ready = sem("pb_gsq"), sem("pb_gin"), sem("pb_gtanh"), sem("pb_z2")
        glu_done, glu_tanh = sem("pb_glu_done"), sem("pb_glu_tanh")
        dve_c = sem("pb_dve")
        w = io["w_in"].rearrange("o (k p) n -> p (o k) n", p=P)
        H = VO // 2
        blocks = [(C_QK, DA), (C_VO, H), (C_VO + H, H)]
        n_cm = 2 * QA
        tok_groups = [(i, hf) for hf in range(2) for i in range(NT)]

        with nc.Block() as block:
            @block.sync
            def _(sp):
                sp.dma_start(lora[:, :], io["lora"]).then_inc(small_in, 16)
                sp.dma_start(cst[:, :], io["rwkv_cst"]).then_inc(small_in, 16)
                sp.dma_start(gluw[:, :, :], io["glu_w"].rearrange("o (k p) n -> p (o k) n", p=P)).then_inc(small_in, 16)
                for b, (c0, n) in enumerate(blocks):
                    if b == 2:
                        sp.wait_ge(proj_done, n_cm)
                    sp.dma_start(ring[:, b % 2, :, 0:n], w[:, :, c0:c0 + n]).then_inc(w_in_s[b % 2], 16)

            @block.gpsimd
            def _(pool):
                nc.gpsimd.memset(t["qk"][:, :, 0:CONV_K - 1], 0.0)
                nc.gpsimd.memset(t["seg64"][:, :], 1.0).then_inc(seg_ready, 1)
                pool.wait_ge(seg_ready, 1)
                nc.gpsimd.memset(t["seg64"][:, 0::HD], 0.0).then_inc(seg_ready, 1)

            @block.scalar
            def _(act):
                A = nc.scalar.activation

                def take_proj(g):
                    act.wait_ge(proj_done, g + 1)
                    if g < n_cm:
                        m, hf = divmod(g, 2)
                        dst = t["qk"][:, m, CONV_K - 1 + hf * 512:CONV_K - 1 + hf * 512 + 512]
                        src = ps[g % 2][:, :]
                    else:
                        i, hf = tok_groups[g - n_cm]
                        dst, src = t["vo"][:, i, hf * H:(hf + 1) * H], ps[g % 2][:, 0:H]
                    A(dst, src, ACT.Copy).then_inc(proj_taken, 1)

                def elementwise(q):
                    if q:
                        act.wait_ge(q_free, q)
                    for part in range(4):
                        c, hf = divmod(part, 2)
                        act.wait_ge(z_done, 4 * q + part + 1)
                        A(T[:, c, hf * 512:hf * 512 + 512], ps[2 + part][:, :], ACT.Tanh,
                          bias=hcol[:, c, q:q + 1], scale=0.5).then_inc(z_taken, 1)
                    act.wait_ge(kk_ready, q + 1)
                    A(T[:, 4, :], T[:, 3, :], ACT.Square).then_inc(sq_ready, 1)
                    act.wait_ge(ell_ready, q + 1)
                    A(T[:, 0, :], T[:, 0, :], ACT.Exp).then_inc(exps, 1)
                    A(T[:, 2, :], T[:, 2, :], ACT.Exp).then_inc(exps, 1)
                    act.wait_ge(ss_taken, 2 * (q + 1))
                    A(T[:, 4, :], T[:, 4, :], ACT.Sqrt).then_inc(root, 1)

                for g in range(n_cm):
                    take_proj(g)
                    if g == 1:
                        act.wait_ge(lora_ready, 2)
                        A(pB[0:HD, 9, 1:], pB[0:HD, 9, 1:], ACT.Tanh).then_inc(lora_tanh, 1)
                        A(pB[:, 10, 1:], pB[:, 10, 1:], ACT.Tanh, scale=0.5).then_inc(lora_tanh, 1)
                for n in range(2 * NT):
                    if n in (0, 4, 8):
                        elementwise(n // 4)
                    take_proj(n_cm + n)
                    if n in (3, 7, 11):
                        q = n // 4
                        act.wait_ge(bon_done, q + 1)
                        A(bonus[:, :, 2 * q:2 * q + 2], ps[2][:, 0:2 * NT].rearrange("p (i e) -> p i e", e=2),
                          ACT.Copy).then_inc(bon_taken, 1)
                y = t["ycT"]
                for a in range(2):
                    if a == 0:
                        act.wait_ge(q_free, QB)
                    A(T[:, a, :], y[:, a, :], ACT.Square).then_inc(g_sq, 1)
                for a in range(2):
                    act.wait_ge(g_in, a + 1)
                    A(T[:, a, :], T[:, a, :], ACT.Tanh, scale=float(np.sqrt(2 / np.pi))).then_inc(g_tanh, 1)
                for g in range(4):
                    a, hf = divmod(g, 2)
                    act.wait_ge(glu_done, g + 1)
                    A(T[:, 2 + a, hf * 512:hf * 512 + 512], ps[4 + g][:, :], ACT.Tanh, bias=hcol[:, 2, a:a + 1],
                      scale=0.25).then_inc(glu_tanh, 1)

            @block.vector
            def _(dve):
                ch = Chain(dve, dve_c)
                V = nc.vector

                def shift(i):
                    ch.link(V.tensor_tensor(T[:, 4, :], pB[:, i, 0:S], pB[:, i, 1:1 + S], ALU.subtract))
                    return V.scalar_tensor_tensor(pB[:, i, 1:1 + S], T[:, 4, :], col(t, "mu", i), pB[:, i, 1:1 + S],
                                                  ALU.mult, ALU.add)

                ch.add(V.tensor_scalar(hcol[:, 0, :], col(t, "w0", 0, QB), 0.5, None, ALU.mult))
                ch.add(V.tensor_scalar(hcol[:, 1, :], col(t, "a0", 0, QB), 0.5, None, ALU.mult))
                ch.link(V.tensor_scalar(hcol[:, 2, 0:2], col(t, "glu_b", 0, 2), 0.5, None, ALU.mult))
                for i in (9, 10):
                    shift(i).then_inc(lora_ready, 1)
                    dve.wait_ge(lora_ready, i - 8)
                for i in range(9):
                    ch.link(shift(i))
                dve.wait_ge(lora_tanh, 2)
                ch.link(V.tensor_scalar(pB[:, 10, 1:], pB[:, 10, 1:], 1.0, 0.5, ALU.add, ALU.mult))
                dve.wait_ge(seg_ready, 2)
                for q in range(QB):
                    r, k = pB[:, q, 1:], pB[:, 3 + q, 1:]
                    V.tensor_scalar(T[:, 3, :], k, col(t, "k_k", q), None, ALU.mult).then_inc(kk_ready, 1)
                    dve.wait_ge(z_taken, 4 * (q + 1))
                    ch.add(V.tensor_scalar(T[:, 1, :], T[:, 1, :], 1.0, 0.5, ALU.add, ALU.mult))
                    ch.link(V.tensor_scalar(T[:, 0, :], T[:, 0, :], 1.0, RWKV_DECAY, ALU.add, ALU.mult))
                    ch.link(V.tensor_tensor_scan(T[:, 2, :], t["seg64"][:, :], T[:, 0, :], 0.0, ALU.mult, ALU.add))
                    V.tensor_tensor(T[:, 0, :], T[:, 2, :], T[:, 0, :], ALU.subtract).then_inc(ell_ready, 1)
                    for hf in range(2):
                        dve.wait_ge(ss_done, 2 * q + hf + 1)
                        V.tensor_scalar(T[:, 4, hf * 512:hf * 512 + 512], ps[6 + hf][:, :], 1e-24, None,
                                        ALU.max).then_inc(ss_taken, 1)
                    f = at[:, q, :]
                    ch.link(V.tensor_scalar(f, T[:, 1, :], -1.0, col(t, "k_a", q), ALU.add, ALU.mult))
                    ch.link(V.scalar_tensor_tensor(k, f, 1.0, k, ALU.add, ALU.mult))
                    ch.link(V.tensor_scalar(f, r, col(t, "r_k", q), None, ALU.mult))
                    dve.wait_ge(root, q + 1)
                    ch.link(V.reciprocal(T[:, 4, :], T[:, 4, :]))
                    ch.link(V.tensor_tensor(T[:, 3, :], T[:, 3, :], T[:, 4, :], ALU.mult))
                    V.tensor_tensor(T[:, 4, :], f, k, ALU.mult).then_inc(rk_ready, 1)
                    ch.add(V.tensor_tensor(T[:, 1, :], T[:, 3, :], T[:, 1, :], ALU.mult))
                    dve.wait_ge(exps, 2 * (q + 1))
                    ch.add(V.tensor_tensor(r, r, T[:, 2, :], ALU.mult))
                    ch.add(V.tensor_copy(ec[:, q, :], T[:, 2, 63::64]))
                    dve.wait_ge(rk_ready, q + 1)
                    ch.link(V.scalar_tensor_tensor(f, T[:, 3, :], -1.0, T[:, 0, :], ALU.mult, ALU.mult))
                    ch.link(V.reciprocal(T[:, 0, :], T[:, 2, :]))
                    ch.add(V.tensor_tensor(k, k, T[:, 0, :], ALU.mult))
                    ch.link(V.tensor_tensor(bt[:, q, :], T[:, 1, :], T[:, 0, :], ALU.mult))
                    dve.wait_ge(bon_done, q + 1)
                    dve.sem_inc(q_free, 1)
                y = t["ycT"]
                for a in range(2):
                    dve.wait_ge(g_sq, a + 1)
                    ch.link(V.tensor_scalar(T[:, a, :], T[:, a, :], 0.044715, 1.0, ALU.mult, ALU.add))
                    V.tensor_tensor(T[:, a, :], T[:, a, :], y[:, a, :], ALU.mult).then_inc(g_in, 1)
                for a in range(2):
                    dve.wait_ge(g_tanh, a + 1)
                    V.scalar_tensor_tensor(y[:, a, :], T[:, a, :], 1.0, y[:, a, :], ALU.add,
                                           ALU.mult).then_inc(z2_ready, 1)
                dve.wait_ge(z2_ready, 2)
                dve.wait_ge(glu_done, 4)
                for a in range(2):
                    dve.wait_ge(glu_tanh, 2 * (a + 1))
                    ch.link(V.scalar_tensor_tensor(T[:, 2 + a, :], T[:, 2 + a, :], 1.0, y[:, a, :], ALU.add, ALU.mult))
                    ch.link(V.tensor_scalar(y[:, a, :], T[:, 2 + a, :], 0.25, None, ALU.mult))

            @block.tensor
            def _(pe):
                def proj(g):
                    if g < n_cm:
                        if g == 0:
                            pe.wait_ge(w_in_s[0], 16)
                        m, hf = divmod(g, 2)
                        ops = [(ring[:, 0, k, m * P:(m + 1) * P], t["hT"][:, k, hf * 512:hf * 512 + 512])
                               for k in range(KT)]
                        out = ps[g % 2][:, :]
                    else:
                        i, hf = tok_groups[g - n_cm]
                        pe.wait_ge(w_in_s[(1 + hf) % 2], 16 * (1 + hf))
                        ops = [(t["hT"][:, k, i * P:(i + 1) * P], ring[:, (1 + hf) % 2, k, :]) for k in range(KT)]
                        out = ps[g % 2][:, 0:H]
                    if g >= 2:
                        pe.wait_ge(proj_taken, g - 1)
                    for k, (a, b) in enumerate(ops):
                        last = nc.tensor.matmul(out, a, b, start=(k == 0), stop=(k == KT - 1))
                    last.then_inc(proj_done, 1)

                def z(q):
                    if q == 0:
                        pe.wait_ge(small_in, 48)
                        pe.wait_ge(lora_tanh, 1)
                        pe.wait_ge(lora_ready, 1)
                    for part in range(4):
                        c, hf = divmod(part, 2)
                        if q:
                            pe.wait_ge(z_taken, 4 * (q - 1) + part + 1)
                            pe.wait_ge(bon_taken, q)
                        rows = slice(c * HD, (c + 1) * HD)
                        nc.tensor.matmul(ps[2 + part][:, :], lora[rows, q * P:(q + 1) * P],
                                         pB[rows, 9, 1 + hf * 512:1 + hf * 512 + 512], start=True, stop=True
                                         ).then_inc(z_done, 1)

                def ss(q):
                    pe.wait_ge(sq_ready, q + 1)
                    for hf in range(2):
                        if q:
                            pe.wait_ge(ss_taken, 2 * (q - 1) + hf + 1)
                        nc.tensor.matmul(ps[6 + hf][:, :], cst[:, 0:P], T[:, 4, hf * 512:hf * 512 + 512],
                                         start=True, stop=True).then_inc(ss_done, 1)

                def bon(q):
                    pe.wait_ge(rk_ready, q + 1)
                    pe.wait_ge(z_taken, 4 * (q + 1))
                    for i in range(NT):
                        last = nc.tensor.matmul(ps[2][:, 2 * i:2 * i + 2], T[:, 4, i * P:(i + 1) * P],
                                                cst[:, P:P + 2], start=True, stop=True)
                    last.then_inc(bon_done, 1)

                for g in range(n_cm):
                    proj(g)
                for n in range(2 * NT):
                    if n in (0, 4, 8):
                        z(n // 4)
                        ss(n // 4)
                    proj(n_cm + n)
                    if n in (3, 7, 11):
                        bon(n // 4)
                pe.wait_ge(z2_ready, 2)
                for g in range(4):
                    a, hf = divmod(g, 2)
                    if g == 0:
                        pe.wait_ge(ss_taken, 2 * QB)
                    for k in range(2):
                        last = nc.tensor.matmul(ps[4 + g][:, :], gluw[:, k, a * P:(a + 1) * P],
                                                t["ycT"][:, k, hf * 512:hf * 512 + 512], start=(k == 0), stop=(k == 1))
                    last.then_inc(glu_done, 1)


def phase_c(nc, t, io):
    ps = t["ps"]
    pB, at, bt = t["pB"], t["a_til"], t["b_hat"]
    with ExitStack() as ctx:
        sb = lambda n, s, d=F32: ctx.enter_context(nc.sbuf_tensor(n, s, d, side="right"))
        sem = ctx.enter_context(phase_semaphores(nc))
        msk = sb("pc_msk", [P, 384 + 3 * 384])
        rows = sb("pc_rows", [P, 2, DB])
        gup = sb("pc_gup", [P, DB])
        tok = sb("pc_tok", [P, 2, DB])
        v = sb("pc_v", [P, 2, DB])
        gm = sb("pc_gm", [P, HB, 3 * P])
        ad, adT, aoT = sb("pc_ad", [P, HB, P]), sb("pc_adT", [P, HB, P]), sb("pc_aoT", [P, HB, P])
        p2, p2T, p4, p4T = (sb(f"pc_{n}", [P, HB, P]) for n in ("p2", "p2T", "p4", "p4T"))
        X = sb("pc_X", [P, HB, P])
        av = sb("pc_av", [P, DB])
        ra = sb("pc_ra", [P, DB])
        sa = sb("pc_sa", [P, DB])
        st = sb("pc_state", [P, QB, P])
        sd = sb("pc_sdec", [P, QB, P])
        y = sb("pc_y", [P, 2, DB])
        g = sb("pc_g", [P, DB])
        o = sb("pc_o", [P, 2, DB])
        m = sb("pc_m", [P, 4, HB])
        small_in, zeroed = sem("pc_small_in"), sem("pc_zeroed")
        tr_done, tr_taken = sem("pc_tr_done"), sem("pc_tr_taken")
        gate_done, gate_taken = sem("pc_gate_done"), sem("pc_gate_taken")
        gram_done, gram_taken = sem("pc_gram_done"), sem("pc_gram_taken")
        a_done, a_taken = sem("pc_a_done"), sem("pc_a_taken")
        av_done, av_taken = sem("pc_av_done"), sem("pc_av_taken")
        st_done = [sem(f"pc_stage_done{h}") for h in range(2)]
        copied = [sem(f"pc_copied{h}") for h in range(2)]
        added = [sem(f"pc_added{h}") for h in range(2)]
        ra_done, ra_taken, sa_done, sa_taken = sem("pc_ra_done"), sem("pc_ra_taken"), sem("pc_sa_done"), sem("pc_sa_taken")
        sn_done, s_ready = sem("pc_sn_done"), sem("pc_s_ready")
        y1_taken, y2_done, y_ready = sem("pc_y1_taken"), sem("pc_y2_done"), sem("pc_y_ready")
        var_ready, root = sem("pc_var"), sem("pc_root")
        o_ready, ot_done, ot_taken = sem("pc_o_ready"), sem("pc_ot_done"), sem("pc_ot_taken")
        dve_c = sem("pc_dve")
        CP = [0, 2, 4, 5, 5, 6, 8, 9, 9]
        AD = [0, 0, 1, 2, 3, 3, 3, 4, 5]
        NST, NCP, NAD = 8, CP[-1], AD[-1]
        bank = lambda h, b: ps[3 * h + b]
        ORDER = [0, 2, 4, 1, 3, 5]
        cols3 = lambda a: a[:, 0:384].rearrange("p (h n) -> p h n", h=3)

        with nc.Block() as block:
            @block.sync
            def _(sp):
                sp.dma_start(msk[:, :], io["rwkv_masks"]).then_inc(small_in, 16)
                sp.dma_start(rows[:, :, :], io["rows_rwkv"].rearrange("p (a n) -> p a n", a=2)).then_inc(small_in, 16)
                sp.dma_start(gup[:, :], io["g_up"]).then_inc(small_in, 16)

            @block.gpsimd
            def _(pool):
                nc.gpsimd.memset(st[:, :, :], 0.0).then_inc(zeroed, 1)

            @block.scalar
            def _(act):
                cp = lambda d, s: nc.scalar.activation(d, s, ACT.Copy)

                def take_ot(i):
                    act.wait_ge(ot_done, i + 1)
                    cp(pB[:, 0:QB, 1 + i * P:1 + (i + 1) * P], cols3(ps[4])).then_inc(ot_taken, 1)

                def take_gate(i):
                    act.wait_ge(gate_done, i + 1)
                    if i:
                        act.wait_ge(o_ready, i)
                    cp(g[:, :], ps[3][:, 0:DB]).then_inc(gate_taken, 1)

                def roots(i):
                    act.wait_ge(var_ready, i + 1)
                    nc.scalar.activation(m[:, 2, :], m[:, 1, :], ACT.Sqrt).then_inc(root, 1)

                for i in range(NT):
                    for b, dst in enumerate((tok[:, 0, :], tok[:, 1, :], v[:, i % 2, :])):
                        act.wait_ge(tr_done, 3 * i + b + 1)
                        if b == 2 and i >= 2:
                            act.wait_ge(o_ready, i - 1)
                        cp(dst, ps[b][:, 0:DB]).then_inc(tr_taken, 1)
                    if i:
                        take_gate(i - 1)
                    copies = [[(p2, 1), (p2T, 2)], [(p4, 1), (p4T, 2)], [(p2, 1)], [], [(p4, 1)],
                              [(p2, 0), (p2T, 2)], [(p4, 1)], []]
                    for s in range(NST):
                        for h in range(2):
                            if copies[s]:
                                act.wait_ge(st_done[h], NST * i + s + 1)
                            for dst, b in copies[s]:
                                cp(dst[:, 3 * h:3 * h + 3, :], cols3(bank(h, b))).then_inc(copied[h], 1)
                        if s == 0 and i:
                            roots(i - 1)
                    if i:
                        take_ot(i - 1)
                    for c in range(2):
                        R = slice(64 * c, 64 * c + 64)
                        act.wait_ge(sa_done, 2 * i + c + 1)
                        cp(sa[R, :], ps[4][R, 0:DB]).then_inc(sa_taken, 1)
                    act.wait_ge(sn_done, 2 * (i + 1))
                    if i >= 2:
                        act.wait_ge(o_ready, i - 1)
                    cp(y[:, i % 2, :], ps[6][:, 0:DB]).then_inc(y1_taken, 1)
                take_gate(NT - 1)
                roots(NT - 1)
                take_ot(NT - 1)

            @block.vector
            def _(dve):
                ch = Chain(dve, dve_c)
                V = nc.vector
                L = lambda *a: ch.link(V.tensor_tensor(*a))
                M3 = lambda k: msk[:, 384 * (k + 1):384 * (k + 2)].rearrange("p (h n) -> p h n", h=3)

                def out(i):
                    yi = y[:, i % 2, :].rearrange("p (h n) -> p h n", h=HB)
                    ov = [o[:, k, :].rearrange("p (h n) -> p h n", h=HB) for k in range(2)]
                    vv = v[:, i % 2, :].rearrange("p (h n) -> p h n", h=HB)
                    bc = lambda a: a.unsqueeze(2).broadcast_to([P, HB, HD])
                    if i:
                        dve.wait_ge(ot_done, i)
                    dve.wait_ge(y_ready, i + 1)
                    ch.link(V.tensor_reduce(m[:, 0, :], yi, AX.X, ALU.add))
                    ch.link(V.tensor_scalar(m[:, 0, :], m[:, 0, :], 1.0 / HD, None, ALU.mult))
                    L(ov[0], yi, bc(m[:, 0, :]), ALU.subtract)
                    L(ov[1], ov[0], ov[0], ALU.mult)
                    ch.link(V.tensor_reduce(m[:, 1, :], ov[1], AX.X, ALU.add))
                    V.tensor_scalar(m[:, 1, :], m[:, 1, :], 1.0 / HD, GN_EPS, ALU.mult, ALU.add).then_inc(var_ready, 1)
                    L(ov[1], vv, bc(t["bonus"][:, i, :]), ALU.mult)
                    L(o[:, 1, :], o[:, 1, :], rows[:, 1, :], ALU.add)
                    dve.wait_ge(root, i + 1)
                    ch.link(V.reciprocal(m[:, 3, :], m[:, 2, :]))
                    L(ov[0], ov[0], bc(m[:, 3, :]), ALU.mult)
                    L(o[:, 0, :], o[:, 0, :], rows[:, 0, :], ALU.mult)
                    L(o[:, 0, :], o[:, 0, :], o[:, 1, :], ALU.add)
                    dve.wait_ge(gate_taken, i + 1)
                    V.tensor_tensor(o[:, 0, :], o[:, 0, :], g[:, :], ALU.mult).then_inc(o_ready, 1)

                dve.wait_ge(small_in, 48)
                dve.wait_ge(zeroed, 1)
                for i in range(NT):
                    for h in range(HB):
                        dve.wait_ge(gram_done, HB * i + h + 1)
                        G = ps[6 + h % 2]
                        ch.add(V.tensor_tensor(gm[:, h, :], G[:, P:512], msk[:, 0:384], ALU.mult))
                        ch.add(V.tensor_tensor(adT[:, h, :], G[:, 0:P], msk[:, 384:384 + P], ALU.mult))
                        V.tensor_tensor(aoT[:, h, :], G[:, 0:P], msk[:, 768:768 + P], ALU.mult).then_inc(gram_taken, 1)
                        if h % 3 == 2:
                            half = h // 3
                            hs = slice(3 * half, 3 * half + 3)
                            dve.wait_ge(a_done, 2 * i + half + 1)
                            ch.add(V.tensor_tensor(ad[:, hs, :], cols3(bank(half, 0)), M3(2), ALU.mult))
                            ch.sync()
                            V.tensor_tensor(X[:, hs, :], adT[:, hs, :],
                                            t["ident"][:, :].unsqueeze(1).broadcast_to([P, 3, P]),
                                            ALU.add).then_inc(a_taken, 1)
                    dve.wait_ge(av_done, i + 1)
                    V.tensor_copy(av[:, :], ps[6][:, 0:DB]).then_inc(av_taken, 1)
                    if i:
                        out(i - 1)
                    for s in (1, 2, 3, 6, 7):
                        for h in range(2):
                            hs = slice(3 * h, 3 * h + 3)
                            dve.wait_ge(st_done[h], NST * i + s + 1)
                            V.tensor_tensor(X[:, hs, :], X[:, hs, :], cols3(bank(h, 0)), ALU.add).then_inc(added[h], 1)
                    for c in range(2):
                        n = 2 * i + c
                        R = slice(64 * c, 64 * c + 64)
                        dve.wait_ge(ra_done, n + 1)
                        V.tensor_tensor(ra[R, :], ps[7][R, 0:DB], av[R, :], ALU.add).then_inc(ra_taken, 1)
                        for q in range(QB):
                            ch.add(V.tensor_scalar(sd[:, q, :], st[:, q, :], t["chunk_decay"][:, q, n:n + 1], None,
                                                   ALU.mult))
                        ch.sync()
                        dve.wait_ge(sn_done, n + 1)
                        for q in range(QB):
                            for e in range(2):
                                r = slice(64 * e, 64 * e + 64)
                                last = V.scalar_tensor_tensor(
                                    st[r, q, 64 * e:64 * e + 64], ps[5][r, q * P + 64 * e:q * P + 64 * e + 64],
                                    t["chunk_decay"][r, q, n:n + 1], sd[r, q, 64 * e:64 * e + 64], ALU.mult, ALU.add)
                                ch.add(last)
                        ch.sync()
                        dve.sem_inc(s_ready, 1)
                    dve.wait_ge(y2_done, i + 1)
                    dve.wait_ge(y1_taken, i + 1)
                    V.tensor_tensor(y[:, i % 2, :], y[:, i % 2, :], ps[3][:, 0:DB], ALU.add).then_inc(y_ready, 1)
                out(NT - 1)

            @block.tensor
            def _(pe):
                mm = nc.tensor.matmul

                def gate(i):
                    mm(ps[3][:, 0:DB], pB[:, 10, 1 + i * P:1 + (i + 1) * P], gup[:, :], start=True, stop=True
                       ).then_inc(gate_done, 1)

                def out_t(i):
                    pe.wait_ge(o_ready, i + 1)
                    for q in range(QB):
                        last = nc.tensor.transpose(ps[4][:, q * P:(q + 1) * P], o[:, 0, q * P:(q + 1) * P],
                                                   t["ident"][:, :])
                    last.then_inc(ot_done, 1)

                pe.wait_ge(small_in, 48)
                pe.wait_ge(zeroed, 1)
                for i in range(NT):
                    T0, T1 = i * P, (i + 1) * P
                    vi = v[:, i % 2, :]
                    if i:
                        pe.wait_ge(added[0], NAD * i)
                        pe.wait_ge(copied[0], NCP * i)
                    for b in range(3):
                        for q in range(QB):
                            src = (bt[:, q, T0:T1], pB[:, 3 + q, 1 + T0:1 + T1], pB[:, 6 + q, 1 + T0:1 + T1])[b]
                            last = nc.tensor.transpose(ps[b][:, q * P:(q + 1) * P], src, t["ident"][:, :])
                        last.then_inc(tr_done, 1)
                    if i:
                        pe.wait_ge(y_ready, i)
                        gate(i - 1)
                    for h, head in enumerate(ORDER):
                        q, e = divmod(head, 2)
                        r = slice(64 * e, 64 * e + 64)
                        A_, R_ = at[r, q, T0:T1], pB[r, q, 1 + T0:1 + T1]
                        B_, K_ = bt[r, q, T0:T1], pB[r, 3 + q, 1 + T0:1 + T1]
                        if HB * i + h >= 2:
                            pe.wait_ge(gram_taken, HB * i + h - 1)
                        if h < 2 and i:
                            pe.wait_ge(y1_taken, i)
                            pe.wait_ge(ra_taken, 2 * i)
                        G = ps[6 + h % 2]
                        mm(G[:, 0:P], B_, A_, start=True, stop=True)
                        mm(G[:, P:2 * P], B_, R_, start=True, stop=True)
                        mm(G[:, 2 * P:3 * P], K_, A_, start=True, stop=True)
                        mm(G[:, 3 * P:], K_, R_, start=True, stop=True).then_inc(gram_done, 1)
                        half = h // 3
                        if h % 3 == 0:
                            if half == 0:
                                pe.wait_ge(tr_taken, 3 * i + 1)
                            elif i:
                                pe.wait_ge(gate_taken, i)
                        last = mm(bank(half, 0)[:, (h % 3) * P:(h % 3 + 1) * P], A_, B_, start=True, stop=True)
                        if h % 3 == 2:
                            last.then_inc(a_done, 1)
                    pe.wait_ge(gram_taken, HB * (i + 1))
                    pe.wait_ge(tr_taken, 3 * (i + 1))
                    for h, head in enumerate(ORDER):
                        last = mm(ps[6][:, head * HD:(head + 1) * HD], gm[:, h, P:2 * P], vi[:, head * HD:(head + 1) * HD],
                                  start=True, stop=True)
                    last.then_inc(av_done, 1)
                    stages = [[(1, adT, ad), (2, ad, adT)], [(0, p2, X), (1, p2T, p2), (2, p2, p2T)],
                              [(0, p4, X), (1, p4T, p4)], [(0, p2, X)], None, [(0, aoT, p4), (2, p4, aoT)],
                              [(0, p2, X), (1, p2T, p2)], [(0, p4, X)]]
                    for s, prods in enumerate(stages):
                        for h in range(2):
                            if s == 0:
                                pe.wait_ge(a_taken, 2 * i + h + 1)
                                if h and i:
                                    pe.wait_ge(added[1], NAD * i)
                                    pe.wait_ge(copied[1], NCP * i)
                                    pe.wait_ge(s_ready, 2 * i)
                                    pe.wait_ge(sa_taken, 2 * i)
                            else:
                                if NCP * i + CP[s]:
                                    pe.wait_ge(copied[h], NCP * i + CP[s])
                                if NAD * i + AD[s]:
                                    pe.wait_ge(added[h], NAD * i + AD[s])
                            for j in range(3):
                                n = 3 * h + j
                                if prods is None:
                                    last = nc.tensor.transpose(bank(h, 1)[:, j * P:(j + 1) * P], X[:, n, :],
                                                               t["ident"][:, :])
                                    continue
                                for b, lhs, rhs in prods:
                                    last = mm(bank(h, b)[:, j * P:(j + 1) * P], lhs[:, n, :], rhs[:, n, :],
                                              start=True, stop=True)
                            last.then_inc(st_done[h], 1)
                    pe.wait_ge(added[1], NAD * (i + 1))
                    pe.wait_ge(added[0], NAD * (i + 1))
                    pe.wait_ge(copied[1], NCP * (i + 1))
                    if i:
                        out_t(i - 1)
                    pe.wait_ge(av_taken, i + 1)
                    for c in range(2):
                        n = 2 * i + c
                        R = slice(64 * c, 64 * c + 64)
                        if n:
                            pe.wait_ge(s_ready, n)
                        for q in range(QB):
                            last = mm(ps[7][R, q * P:(q + 1) * P], at[:, q, T0 + 64 * c:T0 + 64 * c + 64],
                                      st[:, q, :], start=True, stop=True)
                        last.then_inc(ra_done, 1)
                        for q in range(QB):
                            mm(ps[6][R, q * P:(q + 1) * P], pB[:, q, 1 + T0 + 64 * c:1 + T0 + 64 * c + 64],
                               st[:, q, :], start=True, stop=True)
                        pe.wait_ge(ra_taken, n + 1)
                        if c == 0 and i:
                            pe.wait_ge(ot_taken, i)
                        for h, head in enumerate(ORDER):
                            last = mm(ps[4][R, head * HD:(head + 1) * HD], X[R, h, 64 * c:64 * c + 64],
                                      ra[R, head * HD:(head + 1) * HD], start=True, stop=True)
                        last.then_inc(sa_done, 1)
                        pe.wait_ge(sa_taken, n + 1)
                        for q in range(QB):
                            o_ = ps[5][:, q * P:(q + 1) * P]
                            mm(o_, tok[R, 1, q * P:(q + 1) * P], vi[R, q * P:(q + 1) * P], start=True, stop=False)
                            last = mm(o_, tok[R, 0, q * P:(q + 1) * P], sa[R, q * P:(q + 1) * P], start=False, stop=True)
                        last.then_inc(sn_done, 1)
                    for h, head in enumerate(ORDER):
                        hc = slice(head * HD, (head + 1) * HD)
                        o_ = ps[3][:, hc]
                        mm(o_, gm[:, h, 2 * P:], vi[:, hc], start=True, stop=False)
                        last = mm(o_, gm[:, h, 0:P], sa[:, hc], start=False, stop=True)
                    last.then_inc(y2_done, 1)
                pe.wait_ge(y_ready, NT)
                gate(NT - 1)
                out_t(NT - 1)


def phase_d(nc, t, io):
    ps = t["ps"]
    pB, vo, qk = t["pB"], t["vo"], t["qk"]
    qT, kT = t["a_til"], t["b_hat"]
    W65 = HD + 1
    with ExitStack() as ctx:
        sb = lambda n, s, d=F32: ctx.enter_context(nc.sbuf_tensor(n, s, d, side="right"))
        sem = ctx.enter_context(phase_semaphores(nc))
        cst = sb("pd_cst", [P, (HA + QA + 1) * P])
        wqk = sb("pd_wqk", [P, 2, QA, P])
        nw = sb("pd_nw", [P, DA])
        vaug = sb("pd_vaug", [P, NT, HA, W65])
        M = sb("pd_M", [P, S])
        R4 = sb("pd_R4", [HA, 4, S])
        fz, bc_ = sb("pd_fz", [HA, S]), sb("pd_b", [HA, S])
        mp = sb("pd_mp", [HA, NT + 1])
        gcol = sb("pd_gcol", [P, NT, 4, HA])
        dec = sb("pd_dec", [P, QA, NT])
        E = sb("pd_E", [P, HA, P])
        Pm = sb("pd_P", [P, HA, P])
        kw = sb("pd_kw", [P, 2, DA])
        C = sb("pd_C", [P, QA, 2, W65])
        hb = sb("pd_h", [P, NT, HA, W65])
        mom = sb("pd_mom", [P, 3, NT, HA])
        small_in, prep = sem("pd_small_in"), sem("pd_prep")
        gt_done, f_ready, f_exp, f_ln = sem("pd_gt_done"), sem("pd_f_ready"), sem("pd_f_exp"), sem("pd_f_ln")
        arg_ready, exps = sem("pd_arg_ready"), sem("pd_exps")
        gc_done, gc_taken, m_ready = sem("pd_gc_done"), sem("pd_gc_taken"), sem("pd_m_ready")
        cv_ready, cv_tanh, cx_ready = sem("pd_cv_ready"), sem("pd_cv_tanh"), sem("pd_cx_ready")
        qk_done, qk_taken = sem("pd_qk_done"), sem("pd_qk_taken")
        e_done, e_taken, sc_done, p_ready = sem("pd_e_done"), sem("pd_e_taken"), sem("pd_sc_done"), sem("pd_p_ready")
        kt_done, kt_taken, kw_ready = sem("pd_kt_done"), sem("pd_kt_taken"), sem("pd_kw_ready")
        it_done, ia_done, h_taken = sem("pd_it_done"), sem("pd_ia_done"), sem("pd_h_taken")
        c_done, c_ready = sem("pd_c_done"), sem("pd_c_ready")
        o_tanh, var_ready, root = sem("pd_o_tanh"), sem("pd_var"), sem("pd_root")
        y_ready, yt_done, yt_taken = sem("pd_y_ready"), sem("pd_yt_done"), sem("pd_yt_taken")
        dve_c = sem("pd_dve")
        sel = lambda h: cst[:, h * P:(h + 1) * P]
        pair_sel = lambda q: cst[0:HA, (HA + q) * P:(HA + q + 1) * P]
        causal = cst[:, (HA + QA) * P:(HA + QA + 1) * P]
        ORDER = [0, 2, 4, 1, 3, 5]
        cx = pB[:, 3:6, 1:]
        ov = vo[:, :, DA:2 * DA]

        with nc.Block() as block:
            @block.sync
            def _(sp):
                sp.dma_start(cst[:, :], io["mlstm_cst"]).then_inc(small_in, 16)
                sp.dma_start(wqk[:, :, :, :], io["wqk"]).then_inc(small_in, 16)
                sp.dma_start(nw[:, :], io["rows_mlstm"]).then_inc(small_in, 16)

            @block.gpsimd
            def _(pool):
                nc.gpsimd.memset(M[:, :], 0.0).then_inc(prep, 1)
                nc.gpsimd.memset(t["seg64"][:, HD::2 * HD], 1.0).then_inc(prep, 1)
                nc.gpsimd.memset(C[:, :, :, :], 0.0).then_inc(prep, 1)
                nc.gpsimd.memset(mp[:, 0:1], 0.0).then_inc(prep, 1)
                nc.gpsimd.memset(vaug[:, :, :, HD:W65], 1.0).then_inc(prep, 1)
                for i in range(NT):
                    nc.gpsimd.tensor_copy(vaug[:, i, :, 0:HD],
                                          vo[:, i, 0:DA].rearrange("p (h n) -> p h n", h=HA)).then_inc(prep, 1)

            @block.scalar
            def _(act):
                A = nc.scalar.activation
                act.wait_ge(f_ready, 2)
                A(fz[:, :], fz[:, :], ACT.Exp, scale=-1.0).then_inc(f_exp, 1)
                act.wait_ge(f_exp, 1)
                A(fz[:, :], fz[:, :], ACT.Ln, bias=1.0).then_inc(f_ln, 1)
                for q in range(QA):
                    act.wait_ge(cv_ready, q + 1)
                    A(kT[:, q, :], cx[:, q, :], ACT.Tanh, scale=0.5).then_inc(cv_tanh, 1)
                A(ov, ov, ACT.Tanh, scale=0.5).then_inc(o_tanh, 1)
                for k in range(3):
                    act.wait_ge(arg_ready, k + 1)
                    A(R4[:, k + 1, :], R4[:, k + 1, :], ACT.Exp).then_inc(exps, 1)
                for g in range(4 * QA):
                    which, rem = divmod(g, 2 * QA)
                    q, hf = divmod(rem, 2)
                    act.wait_ge(qk_done, g + 1)
                    A((qT, kT)[which][:, q, hf * 512:hf * 512 + 512], ps[4 + g % 2][:, :], ACT.Copy,
                      scale=(0.5, 0.0625)[which]).then_inc(qk_taken, 1)
                act.wait_ge(gc_done, 2)
                A(gcol[:, :, :, :].rearrange("p i k h -> p (i k h)"), ps[6][:, 0:4 * HA * NT], ACT.Copy).then_inc(gc_taken, 1)
                A(dec[:, :, :].rearrange("p q i -> p (q i)"), ps[7][:, 0:QA * NT], ACT.Copy).then_inc(gc_taken, 1)
                act.wait_ge(gc_taken, 2)
                for i in range(NT):
                    act.wait_ge(kt_done, i + 1)
                    if i >= 2:
                        act.wait_ge(c_done, i - 1)
                    A(kw[:, i % 2, :], ps[7][:, 0:DA], ACT.Copy, scale=0.0625).then_inc(kt_taken, 1)
                    for n, h in enumerate(ORDER):
                        act.wait_ge(e_done, 2 * i + n // 3 + 1)
                        if i and n == 0:
                            act.wait_ge(p_ready, 2 * i)
                        A(E[:, n, :], ps[n // 3][:, (n % 3) * P:(n % 3 + 1) * P], ACT.Exp,
                          bias=gcol[:, i, 0, h:h + 1], scale=-1.0).then_inc(e_taken, 1)
                act.wait_ge(var_ready, 1)
                A(mom[:, 1, :, :], mom[:, 1, :, :], ACT.Sqrt).then_inc(root, 1)
                for g in range(2 * QA):
                    act.wait_ge(yt_done, g + 1)
                    q, hf = divmod(g, 2)
                    A(qk[:, q, hf * 512:hf * 512 + 512], ps[g % 4][:, :], ACT.Copy).then_inc(yt_taken, 1)

            @block.vector
            def _(dve):
                ch = Chain(dve, dve_c)
                V = nc.vector
                T = lambda *a: ch.add(V.tensor_tensor(*a))
                L = lambda *a: ch.link(V.tensor_tensor(*a))
                dve.wait_ge(gt_done, 1)
                for hf in range(2):
                    n = slice(hf * 512, hf * 512 + 512)
                    ch.add(V.tensor_scalar(R4[:, 0, n], ps[hf][0:HA, :], col(t, "b_i")[0:HA, :], None, ALU.add))
                    ch.add(V.tensor_scalar(bc_[:, n], ps[2 + hf][0:HA, :], col(t, "b_f")[0:HA, :], None, ALU.add))
                    ch.sync()
                    V.scalar_tensor_tensor(fz[:, n], bc_[:, n], -1.0, bc_[:, n], ALU.mult, ALU.max).then_inc(f_ready, 1)
                for q in range(QA):
                    c = cx[:, q, :]
                    cw = lambda j: col(t, "conv_w", q * CONV_K + j)
                    ch.link(V.tensor_scalar(c, qk[:, q, 0:S], cw(0), col(t, "conv_b", q), ALU.mult, ALU.add))
                    for j in range(1, CONV_K):
                        ins = V.scalar_tensor_tensor(c, qk[:, q, j:j + S], cw(j), c, ALU.mult, ALU.add)
                        if j < CONV_K - 1:
                            ch.link(ins)
                    ins.then_inc(cv_ready, 1)
                dve.wait_ge(f_ln, 1)
                dve.wait_ge(prep, 4)
                ch.link(V.scalar_tensor_tensor(fz[:, :], bc_[:, :], 0.0, fz[:, :], ALU.min, ALU.subtract))
                ch.link(V.tensor_tensor_scan(bc_[:, :], t["seg64"][0:HA, :], fz[:, :], 0.0, ALU.mult, ALU.add))
                L(R4[:, 0, :], R4[:, 0, :], bc_[:, :], ALU.subtract)
                for i in range(NT):
                    n = slice(i * P, (i + 1) * P)
                    ch.link(V.tensor_tensor_scan(M[0:HA, n], R4[:, 0, n], R4[:, 0, n], mp[:, i:i + 1], ALU.max, ALU.max))
                    L(mp[:, i + 1:i + 2], bc_[:, (i + 1) * P - 1:(i + 1) * P], M[0:HA, (i + 1) * P - 1:(i + 1) * P], ALU.add)
                dve.sem_inc(m_ready, 1)
                c3 = lambda a: a.rearrange("p (i n) -> p i n", i=NT)
                V.tensor_tensor(c3(R4[:, 1, :]), mp[:, 0:NT].unsqueeze(2).broadcast_to([HA, NT, P]), c3(M[0:HA, :]),
                                ALU.subtract).then_inc(arg_ready, 1)
                L(R4[:, 2, :], bc_[:, :], M[0:HA, :], ALU.add)
                V.tensor_scalar(R4[:, 2, :], R4[:, 2, :], -1.0, 80.0, ALU.mult, ALU.min).then_inc(arg_ready, 1)
                V.tensor_tensor(c3(R4[:, 3, :]), c3(R4[:, 0, :]), M[0:HA, P - 1::P].unsqueeze(2).broadcast_to([HA, NT, P]),
                                ALU.subtract).then_inc(arg_ready, 1)
                for q in range(QA):
                    dve.wait_ge(cv_tanh, q + 1)
                    V.scalar_tensor_tensor(cx[:, q, :], kT[:, q, :], 1.0, cx[:, q, :], ALU.add, ALU.mult
                                           ).then_inc(cx_ready, 1)
                dve.wait_ge(gc_taken, 2)
                dve.wait_ge(prep, 5 + NT)
                dve.wait_ge(o_tanh, 1)
                h6 = lambda a: a.rearrange("p (h n) -> p h n", h=HA)
                bcast = lambda a, n: a.unsqueeze(2).broadcast_to([P, HA, n])
                for i in range(NT):
                    dve.wait_ge(kt_taken, i + 1)
                    V.tensor_tensor(h6(kw[:, i % 2, :]), h6(kw[:, i % 2, :]), bcast(gcol[:, i, 3, :], HD), ALU.mult
                                    ).then_inc(kw_ready, 1)
                    for b in range(2):
                        dve.wait_ge(e_taken, 6 * i + 3 * b + 3)
                        dve.wait_ge(sc_done, 2 * i + b + 1)
                        if i:
                            dve.wait_ge(ia_done, i)
                        V.tensor_tensor(Pm[:, 3 * b:3 * b + 3, :], ps[2 + b][:, 0:384].rearrange("p (h n) -> p h n", h=3),
                                        E[:, 3 * b:3 * b + 3, :], ALU.mult).then_inc(p_ready, 1)
                    dve.wait_ge(it_done, i + 1)
                    L(hb[:, i, :, :], h6(ps[5][:, 0:HA * W65]), bcast(gcol[:, i, 1, :], W65), ALU.mult)
                    dve.wait_ge(ia_done, i + 1)
                    V.tensor_tensor(hb[:, i, :, :], hb[:, i, :, :], h6(ps[4][:, 0:HA * W65]), ALU.add).then_inc(h_taken, 1)
                    dve.wait_ge(c_done, i + 1)
                    for q in range(QA):
                        for e in range(2):
                            r = slice(64 * e, 64 * e + 64)
                            a = q * 2 * W65 + e * W65
                            ch.add(V.scalar_tensor_tensor(C[r, q, e, :], C[r, q, e, :], dec[r, q, i:i + 1],
                                                          ps[6][r, a:a + W65], ALU.mult, ALU.add))
                    ch.sync()
                    dve.sem_inc(c_ready, 1)
                dve.wait_ge(h_taken, NT)
                U = NT * HA
                f48 = lambda a: a.rearrange("p i h -> p (i h)")
                hv = hb[:, :, :, :].rearrange("p i h n -> p (i h) n")
                num = hv[:, :, 0:HD]
                scr = pB[:, 6:9, 1:]
                bu = lambda a: a.unsqueeze(2).broadcast_to([P, U, HD])
                m0, m1, m2 = (f48(mom[:, k, :, :]) for k in range(3))
                ch.link(V.scalar_tensor_tensor(m0, hv[:, :, HD], -1.0, hv[:, :, HD], ALU.mult, ALU.max))
                L(mom[:, 0, :, :], mom[:, 0, :, :], gcol[:, :, 2, :], ALU.max)
                ch.link(V.reciprocal(m0, m0))
                L(num, num, bu(m0), ALU.mult)
                ch.link(V.tensor_reduce(m0, num, AX.X, ALU.add))
                ch.link(V.tensor_scalar(m0, m0, 1.0 / HD, None, ALU.mult))
                L(num, num, bu(m0), ALU.subtract)
                for j in range(3):
                    a = slice(16 * j, 16 * j + 16)
                    T(scr[:, j, :].rearrange("p (u n) -> p u n", n=HD), num[:, a, :], num[:, a, :], ALU.mult)
                ch.sync()
                for j in range(3):
                    ch.add(V.tensor_reduce(m1[:, 16 * j:16 * j + 16], scr[:, j, :].rearrange("p (u n) -> p u n", n=HD),
                                           AX.X, ALU.add))
                ch.sync()
                V.tensor_scalar(m1, m1, 1.0 / HD, HEAD_EPS, ALU.mult, ALU.add).then_inc(var_ready, 1)
                dve.wait_ge(root, 1)
                ch.link(V.reciprocal(m2, m1))
                ch.link(V.tensor_scalar(m2, m2, 0.5, None, ALU.mult))
                L(num, num, bu(m2), ALU.mult)
                for i in range(NT):
                    ch.add(V.scalar_tensor_tensor(ov[:, i, :], ov[:, i, :], 1.0, nw[:, :], ALU.add, ALU.mult))
                ch.sync()
                for i in range(NT):
                    V.tensor_tensor(h6(ov[:, i, :]), h6(ov[:, i, :]), hb[:, i, :, 0:HD], ALU.mult).then_inc(y_ready, 1)

            @block.tensor
            def _(pe):
                mm, tr = nc.tensor.matmul, nc.tensor.transpose
                ident = t["ident"]
                for k in range(2):
                    for i in range(NT):
                        last = tr(ps[2 * k + i // 4][0:HA, (i % 4) * P:(i % 4 + 1) * P],
                                  vo[:, i, 2 * DA + k * HA:2 * DA + (k + 1) * HA], ident[:, :])
                last.then_inc(gt_done, 1)
                pe.wait_ge(small_in, 48)
                for g in range(4 * QA):
                    which, rem = divmod(g, 2 * QA)
                    q, hf = divmod(rem, 2)
                    pe.wait_ge(cx_ready, q + 1)
                    if g >= 2:
                        pe.wait_ge(qk_taken, g - 1)
                    mm(ps[4 + g % 2][:, :], wqk[:, which, q, :], cx[:, q, hf * 512:hf * 512 + 512],
                       start=True, stop=True).then_inc(qk_done, 1)
                pe.wait_ge(exps, 3)
                for i in range(NT):
                    for k in range(4):
                        a = (i * 4 + k) * HA
                        last = tr(ps[6][:, a:a + HA], R4[:, k, i * P:(i + 1) * P], ident[0:HA, 0:HA])
                last.then_inc(gc_done, 1)
                for q in range(QA):
                    last = mm(ps[7][:, q * NT:(q + 1) * NT], pair_sel(q), R4[:, 1, P - 1::P], start=True, stop=True)
                last.then_inc(gc_done, 1)
                pe.wait_ge(m_ready, 1)
                pe.wait_ge(qk_taken, 4 * QA)
                pe.wait_ge(prep, 5 + NT)
                pe.wait_ge(gc_taken, 2)
                for i in range(NT):
                    n = slice(i * P, (i + 1) * P)
                    if i:
                        pe.wait_ge(kt_taken, i)
                    for q in range(QA):
                        last = mm(ps[7][:, q * P:(q + 1) * P], cx[:, q, n], wqk[:, 1, q, :], start=True, stop=True)
                    last.then_inc(kt_done, 1)
                    for b in range(2):
                        if i:
                            pe.wait_ge(e_taken, 6 * (i - 1) + 3 * b + 3)
                        for j in range(3):
                            mm(ps[b][:, j * P:(j + 1) * P], ident[:, :], causal, start=True, stop=False)
                            last = mm(ps[b][:, j * P:(j + 1) * P], sel(ORDER[3 * b + j]), M[:, n],
                                      start=False, stop=True)
                        last.then_inc(e_done, 1)
                    for b in range(2):
                        if i:
                            pe.wait_ge(p_ready, 2 * (i - 1) + b + 1)
                        for j in range(3):
                            h = ORDER[3 * b + j]
                            q, r = h // 2, slice(64 * (h % 2), 64 * (h % 2) + 64)
                            last = mm(ps[2 + b][:, j * P:(j + 1) * P], kT[r, q, n], qT[r, q, n], start=True, stop=True)
                        last.then_inc(sc_done, 1)
                    if i:
                        pe.wait_ge(c_ready, i)
                        pe.wait_ge(h_taken, i)
                    for q in range(QA):
                        last = mm(ps[5][:, q * 2 * W65:(q + 1) * 2 * W65], qT[:, q, n],
                                  C[:, q, :, :].rearrange("p e n -> p (e n)"), start=True, stop=True)
                    last.then_inc(it_done, 1)
                    pe.wait_ge(kw_ready, i + 1)
                    for q in range(QA):
                        last = mm(ps[6][:, q * 2 * W65:(q + 1) * 2 * W65], kw[:, i % 2, q * P:(q + 1) * P],
                                  vaug[:, i, 2 * q:2 * q + 2, :].rearrange("p e n -> p (e n)"), start=True, stop=True)
                    last.then_inc(c_done, 1)
                    for s, h in enumerate(ORDER):
                        pe.wait_ge(p_ready, 2 * i + s // 3 + 1)
                        last = mm(ps[4][:, h * W65:(h + 1) * W65], Pm[:, s, :], vaug[:, i, h, :], start=True, stop=True)
                    last.then_inc(ia_done, 1)
                for g in range(2 * QA):
                    q, hf = divmod(g, 2)
                    if g >= 4:
                        pe.wait_ge(yt_taken, g - 3)
                    for j in range(4):
                        i = 4 * hf + j
                        pe.wait_ge(y_ready, i + 1)
                        last = tr(ps[g % 4][:, j * P:(j + 1) * P], ov[:, i, q * P:(q + 1) * P], ident[:, :])
                    last.then_inc(yt_done, 1)


def phase_mod2(nc, t, io):
    ps = t["ps"]
    mod = t["mod2"]
    with ExitStack() as ctx:
        ring = ctx.enter_context(nc.sbuf_tensor("m2_ring", [P, 3, KT * 512], F32, side="right"))
        sem = ctx.enter_context(phase_semaphores(nc))
        rows_in, x_in = sem("m2_rows_in"), sem("m2_x_in")
        w_in = [sem(f"m2_w_in{i}") for i in range(3)]
        mod_done, mod_taken, dve_c = sem("m2_mod_done"), sem("m2_mod_taken"), sem("m2_dve")
        ada = io["ada_w"].rearrange("o (k p) n -> p (o k) n", p=P)
        with nc.Block() as block:
            @block.sync
            def _(sp):
                sp.dma_start(mod[:, :, :], io["rows_mod"][:, 2 * D:].rearrange("p (a d) -> p a d", a=4)
                             ).then_inc(rows_in, 16)
                for n in range(8):
                    if n >= 3:
                        sp.wait_ge(mod_done, n - 2)
                    c0 = 2 * D + n * 512
                    sp.dma_start(ring[:, n % 3, :].rearrange("p (k n) -> p k n", k=KT), ada[:, :, c0:c0 + 512]
                                 ).then_inc(w_in[n % 3], 16)
                sp.dma_start(t["wout"][:, :, :], io["w_out"].rearrange("o (k p) n -> p (o k) n", p=P)).then_inc(x_in, 16)
                sp.dma_start(t["x1"][:, :, :], io["x"].rearrange("b (i p) d -> p (b i) d", p=P)).then_inc(x_in, 16)
                sp.dma_start(t["nffn"][:, :], io["rows_norm"][:, D:2 * D]).then_inc(x_in, 16)
                sp.wait_ge(x_in, 48)

            @block.vector
            def _(dve):
                ch = Chain(dve, dve_c)
                dve.wait_ge(rows_in, 16)
                for n in range(8):
                    dve.wait_ge(mod_done, n + 1)
                    part = mod[:, n // 2, (n % 2) * 512:(n % 2) * 512 + 512]
                    nc.vector.tensor_tensor(part, ps[n % 2][:, :], part, ALU.add).then_inc(mod_taken, 1)
                dve.wait_ge(mod_taken, 8)
                dve.wait_ge(x_in, 48)
                ch.add(nc.vector.tensor_scalar(mod[:, 0, :], mod[:, 0, :], 1.0, None, ALU.add))
                ch.add(nc.vector.tensor_scalar(mod[:, 3, :], mod[:, 3, :], 1.0, None, ALU.add))
                ch.link(nc.vector.scalar_tensor_tensor(mod[:, 2, :], mod[:, 2, :], 1.0, t["nffn"][:, :], ALU.add, ALU.mult))

            @block.tensor
            def _(pe):
                for n in range(8):
                    pe.wait_ge(w_in[n % 3], 16 * (n // 3 + 1))
                    if n >= 2:
                        pe.wait_ge(mod_taken, n - 1)
                    w = ring[:, n % 3, :].rearrange("p (k n) -> p k n", k=KT)
                    for k in range(KT):
                        last = nc.tensor.matmul(ps[n % 2][:, :], t["cond_bc"][:, k, :], w[:, k, :],
                                                start=(k == 0), stop=(k == KT - 1))
                    last.then_inc(mod_done, 1)


def phase_e(nc, t, io):
    ps = t["ps"]
    mod, x1 = t["mod2"], t["x1"]
    with ExitStack() as ctx:
        sb = lambda n, s, d=F32: ctx.enter_context(nc.sbuf_tensor(n, s, d, side="right"))
        sem = ctx.enter_context(phase_semaphores(nc))
        wr = sb("pe_wr", [P, KT, NG + NE])
        br = sb("pe_br", [P, NG + NE])
        cst = sb("pe_cst", [P, 2 * P + NG + NE + NE * MAXBLK + MAXBLK // 2])
        tmp = sb("pe_tmp", [P, 2, D])
        h2 = sb("pe_h2", [P, 2, D])
        hT = sb("pe_hT", [P, 2, KT, P])
        ss = sb("pe_ss", [P, 3, NT])
        lg = sb("pe_lg", [P, NT, NG + NE])
        R = sb("pe_R", [P, 8, NT])
        g4 = sb("pe_g4", [P, 3, NT, NG])
        e32 = sb("pe_e32", [P, 6, NT, NE])
        place = sb("pe_place", [P, 3, 2, NT])
        cum = sb("pe_cum", [P, NT + 1, NE])
        cb = sb("pe_cb", [P, 4, NE])
        ends_by = sb("pe_cmp", [1, MAXBLK, NE])
        bf = sb("pe_bf", [1, 2, MAXBLK])
        small_in, tab_zero = sem("pe_small_in"), sem("pe_tab_zero")
        mix_done, x1_ready, mix_taken = sem("pe_mix_done"), sem("pe_x1_ready"), sem("pe_mix_taken")
        sq, var_ready, root, h2_ready = sem("pe_sq"), sem("pe_var"), sem("pe_root"), sem("pe_h2_ready")
        h2_out = [sem("pe_h2_out0"), sem("pe_h2_out1")]
        t_done, t_taken, lg_done = sem("pe_t_done"), sem("pe_t_taken"), sem("pe_lg_done")
        x_ready, x_done = sem("pe_x_ready"), sem("pe_x_done")
        cum_ready, rank_done, dve_c = sem("pe_cum"), sem("pe_rank"), sem("pe_dve")
        ltri, ones = cst[:, 0:P], cst[:, P:2 * P]
        w4, w32 = cst[:, 2 * P:2 * P + NG], cst[:, 2 * P + NG:2 * P + NG + NE]
        c0 = 2 * P + NG + NE
        jrow = cst[0:1, c0:c0 + NE * MAXBLK].rearrange("p (j e) -> p j e", e=NE)
        prow = cst[0:1, c0 + NE * MAXBLK:]
        table = io["slots"]

        def lhs(k, i):
            if k < 3:
                return t["qk"][:, k, i * P:(i + 1) * P]
            if k < 6:
                return t["pB"][:, k - 3, 1 + i * P:1 + (i + 1) * P]
            return t["ycT"][:, k - 6, i * P:(i + 1) * P]

        with nc.Block() as block:
            @block.sync
            def _(sp):
                sp.dma_start(wr[:, :, :], io["w_router"].rearrange("(k p) n -> p k n", p=P)).then_inc(small_in, 16)
                sp.dma_start(br[:, :], io["rows_router"]).then_inc(small_in, 16)
                sp.dma_start(cst[:, :], io["route_cst"]).then_inc(small_in, 16)
                sp.dma_start(t["entry"][:, :, :, :], io["slot_entries"]).then_inc(small_in, 16)
                sp.dma_start(table, io["empty_slots"]).then_inc(tab_zero, 16)
                for i in range(NT):
                    sp.wait_ge(h2_ready, i + 1)
                    sp.dma_start(io["h2"][i * P:(i + 1) * P, :], h2[:, i % 2, :]).then_inc(h2_out[i % 2], 16)
                for u in range(2):
                    sp.wait_ge(h2_out[u], 16 * (NT // 2))
                sp.wait_ge(tab_zero, 16)

            @block.scalar
            def _(act):
                A = nc.scalar.activation
                for i in range(NT + 1):
                    if i < NT:
                        act.wait_ge(x1_ready, i + 1)
                        if i:
                            act.wait_ge(sq, i)
                        A(tmp[:, 1, :], x1[:, i, :], ACT.Square, accum_out=ss[:, 0, i:i + 1]).then_inc(sq, 1)
                        act.wait_ge(var_ready, i + 1)
                        A(ss[:, 1, i:i + 1], ss[:, 1, i:i + 1], ACT.Sqrt).then_inc(root, 1)
                    if i:
                        for g in range(2):
                            act.wait_ge(t_done, 2 * (i - 1) + g + 1)
                            if i >= 3:
                                act.wait_ge(lg_done, i - 2)
                            A(hT[:, (i - 1) % 2, 4 * g:4 * g + 4, :], ps[4 + g][:, :].rearrange("p (k n) -> p k n", k=4),
                              ACT.Copy).then_inc(t_taken, 1)
                act.wait_ge(x_ready, 1)
                A(g4[:, 1, :, :], g4[:, 1, :, :], ACT.Exp).then_inc(x_done, 1)
                act.wait_ge(x_ready, 2)
                A(R[:, 5, :], R[:, 5, :], ACT.Exp).then_inc(x_done, 1)

            @block.vector
            def _(dve):
                ch = Chain(dve, dve_c)
                V = nc.vector
                L = lambda *a: ch.link(V.tensor_tensor(*a))
                dve.wait_ge(small_in, 64)
                for i in range(NT):
                    for hf in range(2):
                        n = slice(hf * 512, hf * 512 + 512)
                        dve.wait_ge(mix_done, 2 * i + hf + 1)
                        V.tensor_tensor(tmp[:, 0, n], ps[hf][:, :], mod[:, 0, n], ALU.mult).then_inc(mix_taken, 1)
                        dve.wait_ge(mix_taken, 2 * i + hf + 1)
                        ch.add(V.tensor_tensor(x1[:, i, n], x1[:, i, n], tmp[:, 0, n], ALU.add))
                    ch.sync()
                    dve.sem_inc(x1_ready, 1)
                    dve.wait_ge(sq, i + 1)
                    V.tensor_scalar(ss[:, 1, i:i + 1], ss[:, 0, i:i + 1], 1.0 / D, NORM_EPS, ALU.mult, ALU.add
                                    ).then_inc(var_ready, 1)
                    dve.wait_ge(root, i + 1)
                    ch.link(V.reciprocal(ss[:, 2, i:i + 1], ss[:, 1, i:i + 1]))
                    if i >= 2:
                        dve.wait_ge(h2_out[i % 2], 16 * (i // 2))
                        dve.wait_ge(t_done, 2 * (i - 1))
                    ch.link(V.scalar_tensor_tensor(h2[:, i % 2, :], x1[:, i, :], ss[:, 2, i:i + 1], mod[:, 2, :],
                                                   ALU.mult, ALU.mult))
                    V.tensor_tensor(h2[:, i % 2, :], h2[:, i % 2, :], mod[:, 1, :], ALU.add).then_inc(h2_ready, 1)
                    if i:
                        dve.wait_ge(lg_done, i)
                        ch.add(V.tensor_tensor(lg[:, i - 1, :], ps[6 + (i - 1) % 2][:, 0:NG + NE], br[:, :], ALU.add))
                dve.wait_ge(lg_done, NT)
                ch.link(V.tensor_tensor(lg[:, NT - 1, :], ps[6 + (NT - 1) % 2][:, 0:NG + NE], br[:, :], ALU.add))
                lg4, lg32 = lg[:, :, 0:NG], lg[:, :, NG:]
                b3 = lambda a, n: a.unsqueeze(2).broadcast_to([P, NT, n])
                r3 = lambda a, n: a.unsqueeze(1).broadcast_to([P, NT, n])
                ch.link(V.tensor_reduce(R[:, 0, :], lg4, AX.X, ALU.max))
                V.tensor_tensor(g4[:, 1, :, :], lg4, b3(R[:, 0, :], NG), ALU.subtract).then_inc(x_ready, 1)
                L(g4[:, 0, :, :], lg4, b3(R[:, 0, :], NG), ALU.is_equal)
                L(g4[:, 0, :, :], g4[:, 0, :, :], r3(w4, NG), ALU.mult)
                ch.link(V.tensor_reduce(R[:, 0, :], g4[:, 0, :, :], AX.X, ALU.max))
                L(g4[:, 0, :, :], g4[:, 0, :, :], b3(R[:, 0, :], NG), ALU.is_equal)
                ch.link(V.tensor_scalar(g4[:, 2, :, :], g4[:, 0, :, :], -1.0, BIG, ALU.add, ALU.mult))
                dve.wait_ge(x_done, 1)
                ch.link(V.tensor_reduce(R[:, 1, :], g4[:, 1, :, :], AX.X, ALU.add))
                ch.link(V.reciprocal(R[:, 1, :], R[:, 1, :]))
                em = e32[:, 0, :, :]
                for i in range(NT):
                    ch.add(V.tensor_tensor(em[:, i, :].rearrange("p (g e) -> p g e", g=NG),
                                           lg32[:, i, :].rearrange("p (g e) -> p g e", g=NG),
                                           g4[:, 2, i, :].unsqueeze(2).broadcast_to([P, NG, EPG]), ALU.add))
                ch.sync()

                def first_largest(oh, src, m):
                    ch.link(V.tensor_reduce(m, src, AX.X, ALU.max))
                    L(oh, src, b3(m, NE), ALU.is_equal)
                    L(oh, oh, r3(w32, NE), ALU.mult)
                    ch.link(V.tensor_reduce(R[:, 7, :], oh, AX.X, ALU.max))
                    L(oh, oh, b3(R[:, 7, :], NE), ALU.is_equal)

                oh1, oh2 = e32[:, 1, :, :], e32[:, 2, :, :]
                first_largest(oh1, em, R[:, 2, :])
                ch.link(V.scalar_tensor_tensor(em, oh1, -3 * BIG, em, ALU.mult, ALU.add))
                first_largest(oh2, em, R[:, 3, :])
                V.tensor_tensor(R[:, 5, :], R[:, 3, :], R[:, 2, :], ALU.subtract).then_inc(x_ready, 1)
                L(e32[:, 3, :, :], oh1, oh2, ALU.add)
                ch.add(V.memset(cum[:, 0, :], 0.0))
                ch.sync()
                for i in range(NT):
                    L(cum[:, i + 1, :], cum[:, i, :], e32[:, 3, i, :], ALU.add)
                dve.sem_inc(cum_ready, 1)
                dve.wait_ge(x_done, 2)
                ch.link(V.tensor_scalar(R[:, 4, :], R[:, 5, :], 1.0, None, ALU.add))
                ch.link(V.reciprocal(R[:, 4, :], R[:, 4, :]))
                L(t["wts"][:, 0, :], R[:, 1, :], R[:, 4, :], ALU.mult)
                L(t["wts"][:, 1, :], t["wts"][:, 0, :], R[:, 5, :], ALU.mult)
                dve.wait_ge(rank_done, 1)
                cnt, nb, end, base = (cb[:, k, :] for k in range(4))
                ch.add(V.tensor_copy(cnt, ps[1][:, 0:NE]))
                ch.link(V.memset(nb, 0.0))
                for k in range(-(-S // BT)):
                    ch.link(V.scalar_tensor_tensor(nb, cnt, float(BT * k), nb, ALU.is_gt, ALU.add))
                ch.link(V.tensor_tensor_scan(end, ones[:, 0:NE], nb, 0.0, ALU.mult, ALU.add))
                L(base, end, nb, ALU.subtract)
                ranks = ps[0][:, 0:NT * NE].rearrange("p (i e) -> p i e", e=NE)
                for k, oh in enumerate((oh1, oh2)):
                    L(e32[:, 5, :, :], oh, ranks, ALU.mult)
                    ch.link(V.tensor_reduce(place[:, 0, k, :], e32[:, 5, :, :], AX.X, ALU.add))
                    L(e32[:, 4, :, :], oh, r3(base, NE), ALU.mult)
                    ch.link(V.tensor_reduce(place[:, 1, k, :], e32[:, 4, :, :], AX.X, ALU.add))
                rank, first_block, b_in = (place[:, k, :, :] for k in range(3))
                ch.link(V.tensor_scalar(b_in, rank, float(BT), None, ALU.is_ge))
                for k in range(2, -(-S // BT)):
                    ch.link(V.scalar_tensor_tensor(b_in, rank, float(BT * k), b_in, ALU.is_ge, ALU.add))
                ch.link(V.scalar_tensor_tensor(first_block, rank, float(MAXBLK), first_block, ALU.mult, ALU.add))
                ch.link(V.scalar_tensor_tensor(first_block, b_in, float(1 - BT * MAXBLK), first_block, ALU.mult, ALU.add))
                ch.link(V.tensor_copy(t["dest"][:, :, :], first_block))
                L(ends_by[:, :, :], end[0:1, :].unsqueeze(1).broadcast_to([1, MAXBLK, NE]), jrow, ALU.is_le)
                ch.link(V.tensor_reduce(bf[:, 0, :], ends_by[:, :, :], AX.X, ALU.add))
                ch.link(V.tensor_scalar(bf[:, 0, :], bf[:, 0, :], float(NE - 1), None, ALU.min))
                ch.link(V.tensor_copy(t["blk"][:, 0:MAXBLK], bf[:, 0, :]))
                ch.link(V.tensor_scalar(bf[:, 1, 0:MAXBLK // 2], prow, end[0:1, NE - 1:NE], None, ALU.is_lt))
                ch.link(V.tensor_reduce(bf[:, 0, 0:1], bf[:, 1, 0:MAXBLK // 2], AX.X, ALU.add))
                for k in range(1, 4):
                    ch.link(V.tensor_scalar(bf[:, 0, k:k + 1], bf[:, 0, 0:1], -float(k), None, ALU.add))
                ch.link(V.tensor_copy(t["blk"][:, MAXBLK:MAXBLK + 4], bf[:, 0, 0:4]))

            @block.tensor
            def _(pe):
                pe.wait_ge(small_in, 64)

                def route(i):
                    pe.wait_ge(h2_ready, i + 1)
                    for g in range(2):
                        if i:
                            pe.wait_ge(t_taken, 2 * (i - 1) + g + 1)
                        for k in range(4):
                            last = nc.tensor.transpose(ps[4 + g][:, k * P:(k + 1) * P],
                                                       h2[:, i % 2, (4 * g + k) * P:(4 * g + k + 1) * P], t["ident"][:, :])
                        last.then_inc(t_done, 1)
                    pe.wait_ge(t_taken, 2 * (i + 1))
                    for k in range(KT):
                        last = nc.tensor.matmul(ps[6 + i % 2][:, 0:NG + NE], hT[:, i % 2, k, :], wr[:, k, :],
                                                start=(k == 0), stop=(k == KT - 1))
                    last.then_inc(lg_done, 1)

                for i in range(NT):
                    for hf in range(2):
                        if i:
                            pe.wait_ge(mix_taken, 2 * (i - 1) + hf + 1)
                        for k in range(KT):
                            last = nc.tensor.matmul(ps[hf][:, :], lhs(k, i), t["wout"][:, k, hf * 512:hf * 512 + 512],
                                                    start=(k == 0), stop=(k == KT - 1))
                        last.then_inc(mix_done, 1)
                    if i:
                        route(i - 1)
                route(NT - 1)
                pe.wait_ge(cum_ready, 1)
                for i in range(NT):
                    o = ps[0][:, i * NE:(i + 1) * NE]
                    nc.tensor.matmul(o, ltri, e32[:, 3, i, :], start=True, stop=False)
                    nc.tensor.matmul(o, ones, cum[:, i, :], start=False, stop=True)
                nc.tensor.matmul(ps[1][:, 0:NE], ones, cum[:, NT, :], start=True, stop=True).then_inc(rank_done, 1)


def phase_moe(nc, t, io):
    ps = t["ps"]
    KF = DE // P
    with ExitStack() as ctx:
        sb = lambda n, s, d=F32: ctx.enter_context(nc.sbuf_tensor(n, s, d))
        sem = ctx.enter_context(phase_semaphores(nc))
        w13 = sb("mo_w13", [P, 2, 2, KT * DE])
        w2 = sb("mo_w2", [P, 2, KF, D])
        tab = sb("mo_tab", [BT, MAXBLK, 2], I32)
        token_id = sb("mo_token", [BT, 2], I32)
        row_id = sb("mo_row", [BT, 2], I32)
        xg = sb("mo_xg", [BT, 2, D])
        xT = sb("mo_xT", [P, 2, KT, BT])
        th = sb("mo_th", [P, 2, KF * BT])
        hh = sb("mo_hh", [P, 2, KF * BT])
        yb = sb("mo_y", [BT, 2, D])
        w13_in = [sem(f"mo_w13_in{u}") for u in range(2)]
        w2_in = [sem(f"mo_w2_in{u}") for u in range(2)]
        x_in = [sem(f"mo_x_in{u}") for u in range(2)]
        y_out = [sem(f"mo_y_out{u}") for u in range(2)]
        scattered = sem("mo_scattered")
        tab_in, token_ready, row_ready, held = sem("mo_tab_in"), sem("mo_token"), sem("mo_row"), sem("mo_held")
        t_done, t_taken = sem("mo_t_done"), sem("mo_t_taken")
        a_done, h_done, tanh_done, hh_ready = sem("mo_a_done"), sem("mo_h_done"), sem("mo_tanh"), sem("mo_hh")
        y_done, y_taken, dve_c = sem("mo_y_done"), sem("mo_y_taken"), sem("mo_dve")
        ident, blk = t["ident"], t["blk"]
        x_banks, h_banks, y_banks = (ps[0], ps[1]), ((ps[2], ps[3]), (ps[4], ps[7])), (ps[5], ps[6])
        W1 = io["moe_w1"].rearrange("o e (p k) n -> p (o e) (k n)", p=P)
        W3 = io["moe_w3"].rearrange("o e (p k) n -> p (o e) (k n)", p=P)
        W2 = io["moe_w2"].rearrange("o e (k p) n -> p (o e) k n", p=P)

        def rounds_less(eng, k):
            return eng.value_load(blk[0:1, MAXBLK + k:MAXBLK + k + 1], min_val=1, max_val=MAXBLK // 2 - k)

        def at(r, u):
            return 2 * r + u

        def expert(eng, r, u):
            return eng.value_load(blk[0:1, bass.ds(at(r, u), 1)], min_val=0, max_val=NE - 1)

        with nc.Block() as block:
            @block.sync
            def _(sp):
                def load_w13(r, u, before=None):
                    e = expert(sp, r, u)
                    if before is not None:
                        sp.wait_ge(h_done, at(before, u) + 1)
                    for c, W in enumerate((W1, W3)):
                        sp.dma_start(w13[:, u, c, :], W[:, bass.ds(e, 1), :].rearrange("p a n -> p (a n)")
                                     ).then_inc(w13_in[u], 16)

                n = rounds_less(sp, 1)
                load_w13(0, 0)
                load_w13(0, 1)
                with sp.Fori(0, n) as r:
                    load_w13(r + 1, 0, r)
                    load_w13(r + 1, 1, r)

            @block.gpsimd
            def _(pool):
                def gather(r, u, before=None):
                    if before is not None:
                        pool.wait_ge(t_done, 2 * at(before, u) + 2)
                    nc.gpsimd.tensor_copy(token_id[:, u:u + 1], tab[:, bass.ds(at(r, u), 1), 0]).then_inc(token_ready, 1)
                    pool.wait_ge(token_ready, at(r, u) + 1)
                    pool.sem_inc(held, 1)
                    nc.gpsimd.indirect_dma_start(
                        out=xg[:, u, :], out_offset=None, in_=io["h2"],
                        in_offset=bass.IndirectOffsetOnAxis(ap=token_id[:, u:u + 1], axis=0)).then_inc(x_in[u], 16)

                def scatter(r, u, before=None):
                    pool.wait_ge(y_taken, 2 * at(r, u) + 2)
                    nc.gpsimd.tensor_copy(row_id[:, u:u + 1], tab[:, bass.ds(at(r, u), 1), 1]).then_inc(row_ready, 1)
                    pool.wait_ge(row_ready, at(r, u) + 1)
                    if before is not None:
                        pool.wait_ge(y_out[1 - u], 16 * before + 16)
                    pool.sem_inc(held, 1)
                    nc.gpsimd.indirect_dma_start(
                        out=io["y_rows"], out_offset=bass.IndirectOffsetOnAxis(ap=row_id[:, u:u + 1], axis=0),
                        in_=yb[:, u, :], in_offset=None).then_inc(y_out[u], 16)

                for k in range(2):
                    for i in range(NT):
                        nc.gpsimd.indirect_dma_start(
                            out=io["slots"], out_offset=bass.IndirectOffsetOnAxis(ap=t["dest"][:, k, i:i + 1], axis=0),
                            in_=t["entry"][:, k, i, :], in_offset=None).then_inc(scattered, 16)
                pool.wait_ge(scattered, 16 * 2 * NT)
                pool.dma_start(tab[:, :, :], io["slots"].rearrange("(p j) c -> p j c", j=MAXBLK)).then_inc(tab_in, 16)
                pool.wait_ge(tab_in, 16)
                n, n2 = rounds_less(pool, 1), rounds_less(pool, 2)
                gather(0, 0)
                gather(0, 1)
                gather(1, 0, 0)
                scatter(0, 0)
                gather(1, 1, 0)
                scatter(0, 1, 0)
                with pool.Fori(0, n2) as r:
                    gather(r + 2, 0, r + 1)
                    scatter(r + 1, 0, r)
                    gather(r + 2, 1, r + 1)
                    scatter(r + 1, 1, r + 1)
                scatter(n, 0, n2)
                scatter(n, 1, n)
                for u in range(2):
                    pool.wait_ge(y_out[u], 16 * n + 16)

            @block.scalar
            def _(act):
                A = nc.scalar.activation

                def load_w2(r, u, before=None):
                    e = expert(act, r, u)
                    if before is not None:
                        act.wait_ge(y_done, 2 * at(before, u) + 2)
                    act.dma_start(w2[:, u, :, :], W2[:, bass.ds(e, 1), :, :].rearrange("p a k n -> p (a k) n")
                                  ).then_inc(w2_in[u], 16)

                def tokens(r, u):
                    for g in range(2):
                        act.wait_ge(t_done, 2 * at(r, u) + g + 1)
                        A(xT[:, u, 4 * g:4 * g + 4, :], x_banks[g][:, 0:4 * BT].rearrange("p (k n) -> p k n", k=4), ACT.Copy
                          ).then_inc(t_taken, 1)

                def tanh(r, u):
                    act.wait_ge(a_done, at(r, u) + 1)
                    A(th[:, u, :], h_banks[u][0][:, 0:KF * BT], ACT.Tanh, scale=0.5).then_inc(tanh_done, 1)

                n, n2 = rounds_less(act, 1), rounds_less(act, 2)
                load_w2(0, 0)
                load_w2(0, 1)
                tokens(0, 0)
                tanh(0, 0)
                tokens(0, 1)
                tanh(0, 1)
                tokens(1, 0)
                load_w2(1, 0, 0)
                with act.Fori(0, n2) as r:
                    tanh(r + 1, 0)
                    tokens(r + 1, 1)
                    load_w2(r + 1, 1, r)
                    tanh(r + 1, 1)
                    tokens(r + 2, 0)
                    load_w2(r + 2, 0, r + 1)
                tanh(n, 0)
                tokens(n, 1)
                load_w2(n, 1, n2)
                tanh(n, 1)

            @block.vector
            def _(dve):
                V = nc.vector

                def swiglu(r, u):
                    a, b = (bank[:, 0:KF * BT] for bank in h_banks[u])
                    dve.wait_ge(tanh_done, at(r, u) + 1)
                    V.scalar_tensor_tensor(hh[:, u, :], th[:, u, :], 1.0, a, ALU.add, ALU.mult).then_inc(dve_c, 1)
                    dve.wait_ge(dve_c, at(r, u) + 1)
                    dve.wait_ge(h_done, at(r, u) + 1)
                    V.tensor_tensor(hh[:, u, :], hh[:, u, :], b, ALU.mult).then_inc(hh_ready, 1)

                def result(r, u, before=None):
                    if before is not None:
                        dve.wait_ge(y_out[u], 16 * before + 16)
                    for g in range(2):
                        n = slice(g * 512, g * 512 + 512)
                        dve.wait_ge(y_done, 2 * at(r, u) + g + 1)
                        V.scalar_tensor_tensor(yb[:, u, n], y_banks[g][0:BT, :], 0.5, t["mod2"][0:BT, 3, n],
                                               ALU.mult, ALU.mult).then_inc(y_taken, 1)

                n, n2, n3 = (rounds_less(dve, k) for k in range(1, 4))
                swiglu(0, 0)
                swiglu(0, 1)
                result(0, 0)
                swiglu(1, 0)
                result(0, 1)
                swiglu(1, 1)
                result(1, 0, 0)
                with dve.Fori(0, n3) as r:
                    swiglu(r + 2, 0)
                    result(r + 1, 1, r)
                    swiglu(r + 2, 1)
                    result(r + 2, 0, r + 1)
                swiglu(n, 0)
                result(n2, 1, n3)
                swiglu(n, 1)
                result(n, 0, n2)
                result(n, 1, n2)

            @block.tensor
            def _(pe):
                mm, tr = nc.tensor.matmul, nc.tensor.transpose

                def tokens(r, u, before=None):
                    pe.wait_ge(x_in[u], 16 * r + 16)
                    for g in range(2):
                        if before is not None:
                            pe.wait_ge(t_taken, 2 * before + 1 + g)
                        for k in range(4):
                            last = tr(x_banks[g][:, k * BT:(k + 1) * BT], xg[:, u, 4 * g + k::KT], ident[0:BT, 0:BT])
                        last.then_inc(t_done, 1)

                def first(r, u, before=None):
                    pe.wait_ge(t_taken, 2 * at(r, u) + 2)
                    pe.wait_ge(w13_in[u], 32 * r + 32)
                    if before is not None:
                        pe.wait_ge(hh_ready, at(before, u) + 1)
                    for c, done in enumerate((a_done, h_done)):
                        for m in range(KF):
                            for k in range(KT):
                                last = mm(h_banks[u][c][:, m * BT:(m + 1) * BT],
                                          w13[:, u, c, k * DE + m * P:k * DE + (m + 1) * P], xT[:, u, k, :],
                                          start=(k == 0), stop=(k == KT - 1))
                        last.then_inc(done, 1)

                def second(r, u, before=None):
                    pe.wait_ge(hh_ready, at(r, u) + 1)
                    pe.wait_ge(w2_in[u], 16 * r + 16)
                    for g in range(2):
                        if before is not None:
                            pe.wait_ge(y_taken, 2 * before + 1 + g)
                        for k in range(KF):
                            last = mm(y_banks[g][0:BT, :], hh[:, u, k * BT:(k + 1) * BT], w2[:, u, k, g * 512:g * 512 + 512],
                                      start=(k == 0), stop=(k == KF - 1))
                        last.then_inc(y_done, 1)

                n, n2 = rounds_less(pe, 1), rounds_less(pe, 2)
                tokens(0, 0)
                first(0, 0)
                tokens(0, 1, 0)
                first(0, 1)
                tokens(1, 0, 1)
                second(0, 0)
                with pe.Fori(0, n2) as r:
                    first(r + 1, 0, r)
                    tokens(r + 1, 1, at(r + 1, 0))
                    second(r, 1, at(r, 0))
                    first(r + 1, 1, r)
                    tokens(r + 2, 0, at(r + 1, 1))
                    second(r + 1, 0, at(r, 1))
                first(n, 0, n2)
                tokens(n, 1, at(n, 0))
                second(n2, 1, at(n2, 0))
                first(n, 1, n2)
                second(n, 0, at(n2, 1))
                second(n, 1, at(n, 0))


def phase_out(nc, t, io):
    x1 = t["x1"]
    with ExitStack() as ctx:
        sb = lambda n, s, d=F32: ctx.enter_context(nc.sbuf_tensor(n, s, d))
        sem = ctx.enter_context(phase_semaphores(nc))
        nf = sb("po_nf", [P, D])
        yg = sb("po_y", [P, NT, 2, D])
        sq_out = sb("po_sq", [P, D])
        ss = sb("po_ss", [P, 3, NT])
        nf_in, y_in = sem("po_nf_in"), [sem(f"po_y_in{i}") for i in range(NT)]
        x2_ready, sq, var_ready, root, o_ready, out_done = (sem("po_x2"), sem("po_sqs"), sem("po_var"), sem("po_root"),
                                                            sem("po_o"), sem("po_out"))
        dve_c = sem("po_dve")
        out = io["out"].rearrange("b (i p) d -> p (b i) d", p=P)
        with nc.Block() as block:
            @block.sync
            def _(sp):
                sp.dma_start(nf[:, :], io["rows_norm"][:, 2 * D:]).then_inc(nf_in, 16)
                for i in range(NT):
                    for k in range(2):
                        sp.dma_start(yg[:, i, k, :], io["y_rows"][k * S + i * P:k * S + (i + 1) * P, :]
                                     ).then_inc(y_in[i], 16)
                for i in range(NT):
                    sp.wait_ge(o_ready, i + 1)
                    sp.dma_start(out[:, i, :], x1[:, i, :]).then_inc(out_done, 16)
                sp.wait_ge(out_done, 16 * NT)

            @block.scalar
            def _(act):
                for i in range(NT):
                    act.wait_ge(x2_ready, i + 1)
                    if i:
                        act.wait_ge(sq, i)
                    nc.scalar.activation(sq_out[:, :], x1[:, i, :], ACT.Square, accum_out=ss[:, 0, i:i + 1]).then_inc(sq, 1)
                    act.wait_ge(var_ready, i + 1)
                    nc.scalar.activation(ss[:, 1, i:i + 1], ss[:, 1, i:i + 1], ACT.Sqrt).then_inc(root, 1)

            @block.vector
            def _(dve):
                ch = Chain(dve, dve_c)
                V = nc.vector

                def finish(i):
                    dve.wait_ge(sq, i + 1)
                    V.tensor_scalar(ss[:, 1, i:i + 1], ss[:, 0, i:i + 1], 1.0 / D, NORM_EPS, ALU.mult, ALU.add
                                    ).then_inc(var_ready, 1)
                    dve.wait_ge(root, i + 1)
                    ch.link(V.reciprocal(ss[:, 2, i:i + 1], ss[:, 1, i:i + 1]))
                    V.scalar_tensor_tensor(x1[:, i, :], x1[:, i, :], ss[:, 2, i:i + 1], nf[:, :], ALU.mult, ALU.mult
                                           ).then_inc(o_ready, 1)

                dve.wait_ge(nf_in, 16)
                for i in range(NT):
                    dve.wait_ge(y_in[i], 32)
                    a, b = yg[:, i, 0, :], yg[:, i, 1, :]
                    ch.link(V.scalar_tensor_tensor(x1[:, i, :], a, t["wts"][:, 0, i:i + 1], x1[:, i, :], ALU.mult, ALU.add))
                    V.scalar_tensor_tensor(x1[:, i, :], b, t["wts"][:, 1, i:i + 1], x1[:, i, :], ALU.mult, ALU.add
                                           ).then_inc(x2_ready, 1)
                    if i:
                        finish(i - 1)
                finish(NT - 1)


def build_program(nc, io):
    io["slots"] = nc.dram_tensor("slots", (SLOTS, 2), I32, kind="Internal").ap()
    io["h2"] = nc.dram_tensor("h2_rows", (S, D), F32, kind="Internal").ap()
    io["y_rows"] = nc.dram_tensor("y_rows", (2 * S + BT, D), F32, kind="Internal").ap()
    with ExitStack() as ctx:
        def put(stack, name, shape, dtype=F32, side="left"):
            t[name] = stack.enter_context(nc.sbuf_tensor(name, shape, dtype, side=side))

        t = {"ps": [ctx.enter_context(nc.psum_tensor(f"bank{i}", [P, 512], F32)) for i in range(8)]}
        put(ctx, "ident", [P, P])
        with ExitStack() as late, ExitStack() as mix:
            put(mix, "cols", [P, NCOLS])
            put(mix, "cond", [P, KT])
            put(mix, "cond_bc", [P, KT, P])
            put(mix, "ycT", [P, 2, S])
            with ExitStack() as heads:
                with ExitStack() as norm:
                    put(norm, "hT", [P, KT, S], side="right")
                    phase_norm1(nc, t, io)
                    put(mix, "pB", [P, 11, 1 + S])
                    phase_a(nc, t, io)
                    put(mix, "qk", [P, QA, CONV_K - 1 + S])
                    put(heads, "a_til", [P, QB, S])
                    put(heads, "b_hat", [P, QB, S])
                    put(heads, "bonus", [P, NT, HB])
                    put(heads, "chunk_decay", [P, QB, S // HD])
                    put(heads, "vo", [P, NT, VO])
                    put(heads, "seg64", [P, S])
                    phase_b(nc, t, io)
                phase_c(nc, t, io)
                phase_d(nc, t, io)
            put(late, "x1", [P, NT, D], side="right")
            put(late, "mod2", [P, 4, D], side="right")
            put(late, "wts", [P, 2, NT], side="right")
            put(late, "blk", [1, MAXBLK + 4], I32, side="right")
            put(late, "entry", [P, 2, NT, 2], I32, side="right")
            put(late, "dest", [P, 2, NT], I32, side="right")
            with ExitStack() as proj:
                put(proj, "wout", [P, KT, D], side="right")
                put(proj, "nffn", [P, D], side="right")
                phase_mod2(nc, t, io)
                phase_e(nc, t, io)
            mix.close()
            phase_moe(nc, t, io)
            phase_out(nc, t, io)


def host_layout(inp):
    f = np.float32
    a = {k: np.asarray(v) for k, v in inp.items()}
    tile_cols = lambda v: v.reshape(-1, P).T
    cols = np.zeros((P, NCOLS), f)

    def put(name, v):
        lo, hi = COLS[name]
        cols[:v.shape[0], lo:hi] = v

    put("c", tile_cols(a["c"][0]))
    put("conv_w", a["mlstm_conv_w"][0].reshape(CONV_K, QA, P).transpose(2, 1, 0).reshape(P, -1))
    put("conv_b", tile_cols(a["mlstm_conv_b"][0]))
    put("mu", tile_cols(a["rwkv_mu"][0]))
    for name, key in (("w0", "rwkv_w0"), ("a0", "rwkv_a0"), ("k_k", "rwkv_k_k"), ("k_a", "rwkv_k_a"),
                      ("r_k", "rwkv_r_k")):
        put(name, tile_cols(a[key][0].reshape(-1)))
    put("a_re", tile_cols(a["s5_a_re"][0].reshape(-1)))
    put("a_im", tile_cols(a["s5_a_im"][0].reshape(-1)))
    put("log_dt", tile_cols(np.repeat(a["s5_log_dt"][0], P5)))
    put("d5", a["s5_d"][0].reshape(G5, GC).T)
    put("glu_b", tile_cols(a["s5_glu_b"][0]))
    put("b_i", a["mlstm_b_i"][0][:, None])
    put("b_f", a["mlstm_b_f"][0][:, None])
    s5 = np.zeros((P, 4, QS, GC), f)
    for e in range(2):
        r = slice(e * P5, (e + 1) * P5)
        s5[r, 0] = a["s5_b_re"][0][e::2].transpose(1, 0, 2)
        s5[r, 1] = a["s5_b_im"][0][e::2].transpose(1, 0, 2)
        s5[r, 2] = a["s5_c_re"][0][e::2].transpose(2, 0, 1)
        s5[r, 3] = a["s5_c_im"][0][e::2].transpose(2, 0, 1)
    rows = lambda *v: np.ascontiguousarray(np.broadcast_to(np.concatenate([x.reshape(-1) for x in v]), (P, sum(x.size for x in v))))
    rwkv_cst = np.zeros((P, P + 2), f)
    for e in range(2):
        rwkv_cst[e * HD:(e + 1) * HD, e * HD:(e + 1) * HD] = 1.0
        rwkv_cst[e * HD:(e + 1) * HD, P + e] = 1.0
    s_, t_ = np.arange(P)[:, None], np.arange(P)[None, :]
    same = lambda n: s_ // n == t_ // n
    strict, incl = ((s_ < t_) & same(HD)), ((s_ <= t_) & same(HD))
    u16, rest, l16 = (s_ < t_) & same(16), strict & ~same(16), (s_ > t_) & same(16)
    rwkv_masks = np.concatenate([incl, strict, incl] + [u16] * 3 + [rest] * 3 + [l16] * 3, axis=1).astype(f)
    mc = np.zeros((P, HA + QA + 1, P), f)
    wqk = np.zeros((P, 2, QA, P), f)
    for h in range(HA):
        q, e = divmod(h, 2)
        r = slice(e * HD, (e + 1) * HD)
        mc[h, h, :] = 1.0
        mc[h, HA + q, r] = 1.0
        wqk[r, 0, q, r] = a["mlstm_w_q"][0][h]
        wqk[r, 1, q, r] = a["mlstm_w_k"][0][h]
    mc[:, HA + QA:, :] = np.where(s_ > t_, f(BIG), f(0))[:, None, :]
    token = (np.arange(NT)[None, :] * P + np.arange(P)[:, None]).astype(np.int32)
    entries = np.stack([np.stack([token, token + k * S], axis=2) for k in range(2)], axis=1)
    empty = np.zeros((SLOTS, 2), np.int32)
    empty[:, 1] = 2 * S + np.arange(SLOTS) // MAXBLK
    route = np.zeros((P, 2 * P + NG + NE + NE * MAXBLK + MAXBLK // 2), f)
    route[:, 0:P] = s_ < t_
    route[:, P:2 * P] = 1.0
    route[:, 2 * P:2 * P + NG] = NG - np.arange(NG)
    route[:, 2 * P + NG:2 * P + NG + NE] = NE - np.arange(NE)
    c0 = 2 * P + NG + NE
    route[0, c0:c0 + NE * MAXBLK] = np.repeat(np.arange(MAXBLK), NE)
    route[0, c0 + NE * MAXBLK:] = 2 * np.arange(MAXBLK // 2)
    out = {
        "moe_w1": a["moe_w1"], "moe_w3": a["moe_w3"], "moe_w2": a["moe_w2"], "w_out": a["w_out"],
        "w_router": np.concatenate([a["moe_w_rg"][0], a["moe_w_re"][0]], axis=1),
        "rows_router": rows(a["moe_b_rg"], a["moe_b_re"]), "route_cst": route,
        "slot_entries": entries, "empty_slots": empty,
        "mlstm_cst": mc.reshape(P, -1), "wqk": wqk, "rows_mlstm": rows(a["mlstm_norm_w"]),
        "rwkv_masks": rwkv_masks, "rows_rwkv": rows(a["rwkv_ln_w"], a["rwkv_ln_b"]), "g_up": a["rwkv_g_up"][0],
        "lora": np.concatenate([a["rwkv_w_up"][0], a["rwkv_a_up"][0]]), "rwkv_cst": rwkv_cst,
        "glu_w": a["s5_glu_w"],
        "x": a["x"], "ada_w": a["ada_w"], "w_in": a["w_in"],
        "cols": cols, "ident": np.eye(P, dtype=f),
        "rows_mod": rows(a["ada_b"]), "rows_norm": rows(a["norm_mix"], a["norm_ffn"], a["norm_final"]),
        "s5_bc": s5,
    }
    return out


def kernel(**inputs):
    import concourse.bacc as bacc
    from concourse.bass_utils import run_bass_kernel_spmd

    nc = bacc.Bacc("TRN2", target_bir_lowering=False, num_devices=1)
    arrays, io = {}, {}
    for name, a in host_layout(inputs).items():
        a = np.ascontiguousarray(a)
        arrays[f"in_{name}"] = a
        io[name] = nc.dram_tensor(f"in_{name}", a.shape, mybir.dt.from_np(a.dtype), kind="ExternalInput").ap()
    io["out"] = nc.dram_tensor("out_y", (1, S, D), F32, kind="ExternalOutput").ap()
    build_program(nc, io)
    r = run_bass_kernel_spmd(nc, [arrays], core_ids=[0])
    return r.results[0]["out_y"]
```

```python
from contextlib import ExitStack, contextmanager

import numpy as np

import concourse.bass as bass
from concourse import mybir

F32 = mybir.dt.float32
I32 = mybir.dt.int32
ALU = mybir.AluOpType
ACT = mybir.ActivationFunctionType
AX = mybir.AxisListType

P = 128
D = 1024
S = 1024
KT = D // P
NT = S // P
HD = 64
DA, DB, DC = 384, 384, 256
HA, HB = DA // HD, DB // HD
QA = DA // P
QB = DB // P
CONV_K = 4
C_QK, C_VO, C_R, C_LORA, C_U = 0, DA, 3 * DA + 2 * HA, 3 * DA + 2 * HA + 3 * DB, 3 * DA + 2 * HA + 3 * DB + 256
VO = 2 * DA + 2 * HA
G5, P5, GC = 16, 64, 16
QS = G5 // 2
J5, M5 = 8, S // 8
NG, EPG, NE = 4, 8, 32
DE = 512
BT = 96
MAXBLK = 2 * -(-((2 * S + NE * (BT - 1)) // BT) // 2)
ROUTE_COLS = 2 * P + NG + NE + NE * MAXBLK + MAXBLK // 2 + BT + MAXBLK + 4 * NT + 1
BIG = 1.0e30
NORM_EPS, HEAD_EPS, GN_EPS = 1e-6, 1e-5, 64e-5
RWKV_DECAY = -0.5 * float(np.exp(-0.5))

COLS = {}
_n = 0
for _name, _w in (("c", KT), ("conv_w", QA * CONV_K), ("conv_b", QA), ("mu", 11), ("w0", QB), ("a0", QB),
                  ("k_k", QB), ("k_a", QB), ("r_k", QB), ("a_re", QS), ("a_im", QS), ("log_dt", QS),
                  ("d5", G5), ("glu_b", 2), ("b_i", 1), ("b_f", 1), ("ada_b", 6 * KT),
                  ("norm_mix", KT), ("norm_ffn", KT)):
    COLS[_name] = (_n, _n + _w)
    _n += _w
NCOLS = _n


class Chain:

    def __init__(self, eng, sem):
        self.eng, self.sem, self.n = eng, sem, 0

    def add(self, ins):
        ins.then_inc(self.sem, 1)
        self.n += 1

    def sync(self):
        if self.n:
            self.eng.wait_ge(self.sem, self.n)

    def link(self, ins):
        self.add(ins)
        self.sync()


@contextmanager
def phase_semaphores(nc):
    taken = []

    def sem(name):
        taken.append(nc.alloc_semaphore(name))
        return taken[-1]

    yield sem
    nc.clear_and_free_semaphores(taken)
    nc.all_engine_barrier()


def col(t, name, i=0, n=1):
    a = COLS[name][0] + i
    return t["cols"][:, a:a + n]


W_BLOCKS = [(C_U, 2 * P), (C_R, DB), (C_R + DB, DB), (C_R + 2 * DB, DB), (C_LORA, 2 * P),
            (C_QK, DA), (C_VO, VO // 2), (C_VO + VO // 2, VO // 2)]


def load_w_in(eng, io, t, b):
    c0, n = W_BLOCKS[b]
    w = io["w_in"].rearrange("o (k p) n -> p (o k) n", p=P)
    eng.dma_start(t["ring"][:, b % 2, :, 0:n], w[:, :, c0:c0 + n]).then_inc(t["ring_in"][b % 2], 16)


def wait_w_in(eng, t, b):
    eng.wait_ge(t["ring_in"][b % 2], 16 * (b // 2 + 1))


def phase_norm1(nc, t, io):
    ps, hT = t["ps"], t["hT"]
    with ExitStack() as ctx:
        sb = lambda n, s, d=F32: ctx.enter_context(nc.sbuf_tensor(n, s, d))
        sem = ctx.enter_context(phase_semaphores(nc))
        w = sb("n1_ada", [P, 4, KT, 512])
        xs = sb("n1_x", [P, NT, D])
        junk = sb("n1_junk", [P, D])
        row = sb("n1_row", [1, 2 * D])
        mod = sb("n1_mod", [P, 2, KT])
        ss = sb("n1_ss", [P, NT])
        rstd = sb("n1_rstd", [P, NT])
        const_in, x_in = sem("n1_const_in"), [sem(f"n1_x_in{i}") for i in range(4)]
        w_in = [sem(f"n1_ada_in{n}") for n in range(4)]
        cond_tanh, cond_ready = sem("n1_cond_tanh"), sem("n1_cond_ready")
        sums_ready, var_ready, root_ready = sem("n1_sums"), sem("n1_var"), sem("n1_root")
        h_ready, tr_done, tr_taken = sem("n1_h_ready"), sem("n1_tr_done"), sem("n1_tr_taken")
        row_done, row_taken = sem("n1_row_done"), sem("n1_row_taken")
        mod_done, mod_ready, dve_c = sem("n1_mod_done"), sem("n1_mod_ready"), sem("n1_dve")
        ada = io["ada_w"].rearrange("o (k p) n -> p (o k) n", p=P)
        x = io["x"].rearrange("b (i p) d -> p (b i) d", p=P)
        BY_ACT = 3
        with nc.Block() as block:
            @block.sync
            def _(sp):
                sp.dma_start(t["cols"][:, :], io["cols"]).then_inc(const_in, 16)
                sp.dma_start(t["ident"][:, :], io["ident"]).then_inc(const_in, 16)
                for n in range(4):
                    sp.dma_start(xs[:, 2 * n:2 * n + 2, :], x[:, 2 * n:2 * n + 2, :]).then_inc(x_in[n], 16)
                for n in range(4):
                    sp.dma_start(w[:, n, :, :], ada[:, :, n * 512:(n + 1) * 512]).then_inc(w_in[n], 16)
                for b in range(2):
                    load_w_in(sp, io, t, b)

            @block.scalar
            def _(act):
                A = nc.scalar.activation
                act.wait_ge(const_in, 32)
                A(t["cond"][:, :], col(t, "c", 0, KT), ACT.Tanh, scale=0.5).then_inc(cond_tanh, 1)

                def take(i):
                    for half in range(2):
                        g = 2 * i + half
                        act.wait_ge(tr_done, g + 1)
                        A(hT[:, 4 * half:4 * half + 4, i * P:(i + 1) * P],
                          ps[4 + g % 4][:, :].rearrange("p (k n) -> p k n", k=4), ACT.Copy).then_inc(tr_taken, 1)

                for n in range(4):
                    act.wait_ge(x_in[n], 16)
                    for i in (2 * n, 2 * n + 1):
                        if i:
                            act.wait_ge(sums_ready, i)
                        A(junk[:, :], xs[:, i, :], ACT.Square, accum_out=ss[:, i:i + 1]).then_inc(sums_ready, 1)
                    act.wait_ge(var_ready, n + 1)
                    A(rstd[:, 2 * n:2 * n + 2], ss[:, 2 * n:2 * n + 2], ACT.Sqrt).then_inc(root_ready, 1)
                    if n:
                        take(2 * n - 2)
                        take(2 * n - 1)
                take(NT - 2)
                take(NT - 1)
                act.wait_ge(tr_taken, 2 * NT)
                act.wait_ge(mod_ready, 1)
                for k in range(KT - BY_ACT, KT):
                    A(hT[:, k, :], hT[:, k, :], ACT.Identity, bias=mod[:, 0, k:k + 1], scale=mod[:, 1, k:k + 1])

            @block.vector
            def _(dve):
                ch = Chain(dve, dve_c)
                V = nc.vector
                dve.wait_ge(cond_tanh, 1)
                V.scalar_tensor_tensor(t["cond"][:, :], t["cond"][:, :], 1.0, col(t, "c", 0, KT), ALU.add, ALU.mult
                                       ).then_inc(cond_ready, 1)
                for n in range(4):
                    pair = slice(2 * n, 2 * n + 2)
                    dve.wait_ge(sums_ready, 2 * n + 2)
                    V.tensor_scalar(ss[:, pair], ss[:, pair], 1.0 / D, NORM_EPS, ALU.mult, ALU.add).then_inc(var_ready, 1)
                    dve.wait_ge(root_ready, n + 1)
                    ch.link(V.reciprocal(rstd[:, pair], rstd[:, pair]))
                    for i in (2 * n, 2 * n + 1):
                        V.tensor_scalar(xs[:, i, :], xs[:, i, :], rstd[:, i:i + 1], None, ALU.mult).then_inc(h_ready, 1)
                for n in range(4):
                    dve.wait_ge(row_done, n + 1)
                    V.tensor_copy(row[:, n * 512:(n + 1) * 512], ps[n][0:1, :]).then_inc(row_taken, 1)
                dve.wait_ge(mod_done, 1)
                ch.link(V.scalar_tensor_tensor(mod[:, :, :], ps[4][:, 0:2 * KT].rearrange("p (a k) -> p a k", a=2), 0.5,
                                               col(t, "ada_b", 0, 2 * KT).rearrange("p (a k) -> p a k", a=2),
                                               ALU.mult, ALU.add))
                V.scalar_tensor_tensor(mod[:, 1, :], mod[:, 1, :], 1.0, col(t, "norm_mix", 0, KT), ALU.add, ALU.mult
                                       ).then_inc(mod_ready, 1)
                dve.wait_ge(mod_ready, 1)
                dve.wait_ge(tr_taken, 2 * NT)
                for k in range(KT - BY_ACT):
                    V.tensor_scalar(hT[:, k, :], hT[:, k, :], mod[:, 1, k:k + 1], mod[:, 0, k:k + 1], ALU.mult, ALU.add)

            @block.tensor
            def _(pe):
                pe.wait_ge(const_in, 32)
                for g in range(2 * NT):
                    i, half = divmod(g, 2)
                    pe.wait_ge(h_ready, i + 1)
                    if g >= 4:
                        pe.wait_ge(tr_taken, g - 3)
                    for k in range(4):
                        a = (4 * half + k) * P
                        last = nc.tensor.transpose(ps[4 + g % 4][:, k * P:(k + 1) * P], xs[:, i, a:a + P],
                                                   t["ident"][:, :])
                    last.then_inc(tr_done, 1)
                pe.wait_ge(cond_ready, 1)
                for n in range(4):
                    pe.wait_ge(w_in[n], 16)
                    for k in range(KT):
                        last = nc.tensor.matmul(ps[n][0:1, :], t["cond"][:, k:k + 1], w[:, n, k, :],
                                                start=(k == 0), stop=(k == KT - 1))
                    last.then_inc(row_done, 1)
                pe.wait_ge(tr_taken, 2 * NT - 3)
                for m in range(2 * KT):
                    if m % 4 == 0:
                        pe.wait_ge(row_taken, m // 4 + 1)
                    last = nc.tensor.matmul(ps[4][:, m:m + 1], row[0:1, m * P:(m + 1) * P], t["ident"][0:1, 0:1],
                                            start=True, stop=True)
                last.then_inc(mod_done, 1)


def phase_a(nc, t, io):
    ps = t["ps"]
    with ExitStack() as ctx:
        sb = lambda n, s, d=F32: ctx.enter_context(nc.sbuf_tensor(n, s, d))
        sem = ctx.enter_context(phase_semaphores(nc))
        ring = t["ring"]
        chunks = sb("pa_chunks", [P, J5 * DC])
        um = chunks[:, :].rearrange("p (g j c) -> p g j c", g=G5, j=J5)
        ym = chunks[:, :].rearrange("p (j n) -> p j n", j=J5)
        us = sb("pa_us", [P, G5, M5])
        braw = sb("pa_b", [P, 4, QS, GC])
        bb = sb("pa_bb", [P, 2, QS, GC])
        co = sb("pa_co", [P, 16, QS])
        coi = sb("pa_coi", [P, QS], I32)
        pw = sb("pa_pw", [P, 2, QS, J5 + 1])
        pr = sb("pa_pr", [P, 2, QS, J5])
        ws = sb("pa_ws", [P, 2, QS, P])
        wt = sb("pa_wt", [P, QS, 2, P])
        cl = sb("pa_cl", [P, 2, QS, J5 + 1, GC])
        turn = sb("pa_turn", [P, 2, QS, M5])
        tmp = sb("pa_tmp", [P, 2, QS * (J5 + 1) * GC])
        kt = sb("pa_kt", [GC, G5, P])
        tz = sb("pa_tz", [P, G5, P])
        xb = sb("pa_xb", [P, 2, QS, 1 + M5])
        gluw = sb("pa_glu", [P, 2, DC])
        hglu = sb("pa_hglu", [P, 2])
        gate = ws[:, :, :, :].rearrange("p c q m -> p c (q m)")
        glu = tmp[:, :, 0:S]
        small_in, pads = sem("pa_small_in"), sem("pa_pads")
        u_done, u_taken, us_done, us_taken = sem("pa_u_done"), sem("pa_u_taken"), sem("pa_us_done"), sem("pa_us_taken")
        proj_done, proj_taken = sem("pa_proj_done"), sem("pa_proj_taken")
        dt_ready, act_dt, ang_ready, act_sin = sem("pa_dt"), sem("pa_actdt"), sem("pa_ang"), sem("pa_sin")
        ws_ready, wt_done, wt_taken, e_done = sem("pa_ws_ready"), sem("pa_wt_done"), sem("pa_wt_taken"), sem("pa_e_done")
        cl_ready, k_done, k_taken, k_ready, tz_in = (sem("pa_cl_ready"), sem("pa_k_done"), sem("pa_k_taken"),
                                                     sem("pa_k_ready"), sem("pa_tz_in"))
        x_ready, y_done, y_taken = sem("pa_x_ready"), sem("pa_y_done"), sem("pa_y_taken")
        yt_done, yt_taken, dve_c = sem("pa_yt_done"), sem("pa_yt_taken"), sem("pa_dve")
        g_sq, g_in, g_tanh, z2_ready = sem("pa_gsq"), sem("pa_gin"), sem("pa_gtanh"), sem("pa_z2")
        glu_done, glu_tanh = sem("pa_glu_done"), sem("pa_glu_tanh")
        tiles = [(b, m) for b in range(1, 5) for m in range(W_BLOCKS[b][1] // P)]
        tiles_to = lambda b: sum(1 for x, _ in tiles if x <= b)
        WT_AT, E_AT, Y_AT, YT_AT, GLU_AT = 1, 2, 6, 7, 9

        with nc.Block() as block:
            @block.sync
            def _(sp):
                sp.dma_start(braw[:, :, :, :], io["s5_bc"]).then_inc(small_in, 16)
                sp.dma_start(gluw[:, :, :], io["glu_w"].rearrange("o (k p) n -> p (o k) n", p=P)).then_inc(small_in, 16)
                sp.wait_ge(u_done, J5)
                load_w_in(sp, io, t, 2)
                sp.wait_ge(proj_done, 2 * tiles_to(1))
                load_w_in(sp, io, t, 3)
                sp.wait_ge(k_ready, 1)
                sp.wait_ge(pads, 3)
                for j in range(J5):
                    sp.dma_start(tz[j * GC:(j + 1) * GC, :, j * GC:], kt[:, :, 0:P - j * GC]).then_inc(tz_in, 16)
                for b in (4, 5):
                    sp.wait_ge(proj_done, 2 * tiles_to(b - 2))
                    load_w_in(sp, io, t, b)

            @block.gpsimd
            def _(pool):
                nc.gpsimd.memset(t["pB"][:, :, 0:1], 0.0).then_inc(pads, 1)
                nc.gpsimd.memset(xb[:, :, :, 0:1], 0.0).then_inc(pads, 1)
                nc.gpsimd.memset(tz[:, :, :], 0.0).then_inc(pads, 1)

            @block.scalar
            def _(act):
                A = nc.scalar.activation
                A(co[:, 0, :], col(t, "log_dt", 0, QS), ACT.Exp).then_inc(act_dt, 1)
                act.wait_ge(dt_ready, 1)
                A(co[:, 2, :], co[:, 1, :], ACT.Exp).then_inc(act_dt, 1)
                act.wait_ge(ang_ready, 1)
                A(co[:, 5, :], co[:, 5, :], ACT.Sin).then_inc(act_sin, 1)
                A(co[:, 6, :], co[:, 6, :], ACT.Sin).then_inc(act_sin, 1)
                for j in range(J5):
                    act.wait_ge(u_done, j + 1)
                    A(um[:, :, j, :], ps[j % 2][:, 0:DC].rearrange("p (g c) -> p g c", g=G5), ACT.Copy).then_inc(u_taken, 1)
                for b in range(4):
                    act.wait_ge(us_done, b + 1)
                    A(us[:, 4 * b:4 * b + 4, :].rearrange("p g m -> p (g m)"), ps[2 + b][:, :], ACT.Copy).then_inc(us_taken, 1)
                for mt in range(len(tiles)):
                    for half in range(2):
                        g = 2 * mt + half
                        act.wait_ge(proj_done, g + 1)
                        A(t["pB"][:, mt, 1 + half * 512:1 + (half + 1) * 512], ps[g % 2][:, :], ACT.Copy).then_inc(proj_taken, 1)
                    if mt == WT_AT:
                        for b in range(4):
                            act.wait_ge(wt_done, b + 1)
                            A(wt[:, 2 * b:2 * b + 2, :, :].rearrange("p q c n -> p (q c n)"), ps[2 + b][:, :], ACT.Copy
                              ).then_inc(wt_taken, 1)
                    if mt == E_AT:
                        for i in range(4):
                            act.wait_ge(k_done, i + 1)
                            A(kt[:, 8 * (i // 2) + i % 2:8 * (i // 2) + 8:2, :],
                              ps[6 + i % 2][0:GC, :].rearrange("p (q n) -> p q n", q=4), ACT.Copy).then_inc(k_taken, 1)
                    if mt == Y_AT:
                        for i in range(4):
                            act.wait_ge(y_done, i + 1)
                            for q in range(4):
                                g = 8 * (i // 2) + 2 * q + i % 2
                                last = A(ym[:, :, g * GC:(g + 1) * GC],
                                         ps[6 + i % 2][:, q * P:(q + 1) * P].rearrange("p (j c) -> p j c", j=J5), ACT.Copy)
                            last.then_inc(y_taken, 1)
                    if mt == YT_AT:
                        for b in range(4):
                            act.wait_ge(yt_done, b + 1)
                            out = t["ycT"][:, b // 2, :].rearrange("p (m j) -> p j m", j=J5)
                            A(out[:, 4 * (b % 2):4 * (b % 2) + 4, :], ps[2 + b][:, :].rearrange("p (j m) -> p j m", j=4),
                              ACT.Copy).then_inc(yt_taken, 1)
                        act.wait_ge(yt_taken, 4)
                        for a in range(2):
                            A(gate[:, a, :], t["ycT"][:, a, :], ACT.Square).then_inc(g_sq, 1)
                    if mt == YT_AT + 1:
                        for a in range(2):
                            act.wait_ge(g_in, a + 1)
                            A(gate[:, a, :], gate[:, a, :], ACT.Tanh, scale=float(np.sqrt(2 / np.pi))).then_inc(g_tanh, 1)
                    if mt == GLU_AT:
                        for g in range(4):
                            a, hf = divmod(g, 2)
                            act.wait_ge(glu_done, g + 1)
                            A(glu[:, a, hf * 512:hf * 512 + 512], ps[4 + g][:, :], ACT.Tanh, bias=hglu[:, a:a + 1],
                              scale=0.25).then_inc(glu_tanh, 1)

            @block.vector
            def _(dve):
                ch = Chain(dve, dve_c)
                V = nc.vector
                tt = lambda o, a, b, op: ch.add(V.tensor_tensor(o, a, b, op))
                LT = lambda o, a, b, op: ch.link(V.tensor_tensor(o, a, b, op))
                are, aim = col(t, "a_re", 0, QS), col(t, "a_im", 0, QS)
                dve.wait_ge(act_dt, 1)
                V.tensor_tensor(co[:, 1, :], are, co[:, 0, :], ALU.mult).then_inc(dt_ready, 1)
                LT(co[:, 3, :], aim, co[:, 0, :], ALU.mult)
                ch.link(V.tensor_scalar(co[:, 4, :], co[:, 3, :], float(1 / (2 * np.pi)), None, ALU.mult))
                ch.link(V.tensor_copy(coi[:, :], co[:, 4, :]))
                ch.link(V.tensor_copy(co[:, 4, :], coi[:, :]))
                ch.link(V.scalar_tensor_tensor(co[:, 3, :], co[:, 4, :], -6.28125, co[:, 3, :], ALU.mult, ALU.add))
                ch.link(V.scalar_tensor_tensor(co[:, 3, :], co[:, 4, :], -float(2 * np.pi - 6.28125), co[:, 3, :],
                                               ALU.mult, ALU.add))

                def wrap(x, tmp):
                    ch.link(V.tensor_scalar(tmp, x, float(np.pi), -float(2 * np.pi), ALU.is_gt, ALU.mult))
                    LT(x, x, tmp, ALU.add)
                    ch.link(V.tensor_scalar(tmp, x, -float(np.pi), float(2 * np.pi), ALU.is_lt, ALU.mult))
                    LT(x, x, tmp, ALU.add)

                wrap(co[:, 3, :], co[:, 4, :])
                ch.link(V.tensor_scalar(co[:, 6, :], co[:, 3, :], float(np.pi / 2), None, ALU.add))
                wrap(co[:, 6, :], co[:, 4, :])
                lim = 3.1415925
                ch.link(V.tensor_scalar(co[:, 5, :], co[:, 3, :], lim, -lim, ALU.min, ALU.max))
                V.tensor_scalar(co[:, 6, :], co[:, 6, :], lim, -lim, ALU.min, ALU.max).then_inc(ang_ready, 1)
                dve.wait_ge(act_dt, 2)
                dve.wait_ge(act_sin, 2)
                ch.add(V.memset(pw[:, 0, :, 0], 1.0))
                ch.add(V.memset(pw[:, 1, :, 0], 0.0))
                tt(pw[:, 0, :, 1], co[:, 2, :], co[:, 6, :], ALU.mult)
                LT(pw[:, 1, :, 1], co[:, 2, :], co[:, 5, :], ALU.mult)
                tt(co[:, 7, :], are, are, ALU.mult)
                LT(co[:, 8, :], aim, aim, ALU.mult)
                LT(co[:, 7, :], co[:, 7, :], co[:, 8, :], ALU.add)
                ch.link(V.reciprocal(co[:, 7, :], co[:, 7, :]))
                ch.link(V.tensor_scalar(co[:, 8, :], pw[:, 0, :, 1], -1.0, None, ALU.add))
                tt(co[:, 9, :], co[:, 8, :], are, ALU.mult)
                tt(co[:, 10, :], pw[:, 1, :, 1], aim, ALU.mult)
                tt(co[:, 11, :], pw[:, 1, :, 1], are, ALU.mult)
                LT(co[:, 12, :], co[:, 8, :], aim, ALU.mult)
                tt(co[:, 9, :], co[:, 9, :], co[:, 10, :], ALU.add)
                LT(co[:, 11, :], co[:, 11, :], co[:, 12, :], ALU.subtract)
                tt(co[:, 9, :], co[:, 9, :], co[:, 7, :], ALU.mult)
                LT(co[:, 11, :], co[:, 11, :], co[:, 7, :], ALU.mult)
                dve.wait_ge(small_in, 32)

                def cmul(ore, oim, xre, xim, yre, yim, t0, t1, sign=1):
                    minus, plus = (ALU.subtract, ALU.add) if sign > 0 else (ALU.add, ALU.subtract)
                    tt(t0, xim, yim, ALU.mult)
                    LT(t1, xre, yim, ALU.mult)
                    tt(ore, xre, yre, ALU.mult)
                    LT(oim, xim, yre, ALU.mult)
                    tt(ore, ore, t0, minus)
                    LT(oim, oim, t1, plus)

                def scratch(*dims):
                    n = int(np.prod(dims))
                    names = "qab"[:len(dims)]
                    spec = f"p ({' '.join(names)}) -> p {' '.join(names)}"
                    sizes = dict(zip(names, dims))
                    return [tmp[:, c, 0:n].rearrange(spec, **sizes) for c in range(2)]

                over = lambda a, n: a.unsqueeze(2).broadcast_to([P, QS, n])
                over_c = lambda a, n: a.unsqueeze(3).broadcast_to([P, QS, n, GC])
                over_j = lambda a, n: a.unsqueeze(2).broadcast_to([P, QS, n, GC])
                cmul(bb[:, 0, :, :], bb[:, 1, :, :], braw[:, 0, :, :], braw[:, 1, :, :],
                     over(co[:, 9, :], GC), over(co[:, 11, :], GC), *scratch(QS, GC))
                for n in (1, 2, 4):
                    cmul(pw[:, 0, :, n + 1:2 * n + 1], pw[:, 1, :, n + 1:2 * n + 1], pw[:, 0, :, 1:n + 1],
                         pw[:, 1, :, 1:n + 1], over(pw[:, 0, :, n], n), over(pw[:, 1, :, n], n), *scratch(QS, n))
                for j in range(J5):
                    ch.add(V.tensor_copy(pr[:, :, :, j], pw[:, :, :, J5 - 1 - j]))
                ch.sync()
                W4 = lambda c: ws[:, c, :, :].rearrange("p q (j c) -> p q j c", j=J5)
                cmul(W4(0), W4(1), over_c(pr[:, 0, :, :], J5), over_c(pr[:, 1, :, :], J5),
                     over_j(bb[:, 0, :, :], J5), over_j(bb[:, 1, :, :], J5), *scratch(QS, J5, GC))
                dve.sem_inc(ws_ready, 1)
                n = J5 + 1
                cmul(cl[:, 0, :, :, :], cl[:, 1, :, :, :], over_c(pw[:, 0, :, :], n), over_c(pw[:, 1, :, :], n),
                     over_j(braw[:, 2, :, :], n), over_j(braw[:, 3, :, :], n), *scratch(QS, n, GC))
                V.tensor_scalar(cl[:, 1, :, :, :], cl[:, 1, :, :, :], -1.0, None, ALU.mult).then_inc(cl_ready, 1)
                ch.add(V.tensor_copy(co[:, 13, :], co[:, 6, :]))
                ch.add(V.tensor_copy(co[:, 14, :], co[:, 5, :]))
                ch.link(V.tensor_copy(co[:, 15, :], co[:, 2, :]))
                unit = co[:, 13, :], co[:, 14, :]
                for _ in range(3):
                    ch.add(V.tensor_tensor(co[:, 15, :], co[:, 15, :], co[:, 15, :], ALU.mult))
                    cmul(co[:, 3, :], co[:, 4, :], *unit, *unit, co[:, 0, :], co[:, 1, :])
                    ch.add(V.tensor_copy(unit[0], co[:, 3, :]))
                    ch.link(V.tensor_copy(unit[1], co[:, 4, :]))
                ch.add(V.memset(turn[:, 0, :, 0], 1.0))
                ch.add(V.memset(turn[:, 1, :, 0], 0.0))
                ch.sync()
                n = 1
                while n < M5:
                    cmul(turn[:, 0, :, n:2 * n], turn[:, 1, :, n:2 * n], turn[:, 0, :, 0:n], turn[:, 1, :, 0:n],
                         over(unit[0], n), over(unit[1], n), *scratch(QS, n))
                    n *= 2
                    if n < M5:
                        cmul(co[:, 3, :], co[:, 4, :], *unit, *unit, co[:, 0, :], co[:, 1, :])
                        ch.add(V.tensor_copy(unit[0], co[:, 3, :]))
                        ch.link(V.tensor_copy(unit[1], co[:, 4, :]))
                dve.wait_ge(k_taken, 4)
                eye = t["ident"][0:GC, 0:GC].unsqueeze(1).broadcast_to([GC, G5, GC])
                d5 = col(t, "d5", 0, G5)[0:GC, :].unsqueeze(2).broadcast_to([GC, G5, GC])
                diag = tmp[0:GC, 0, 0:G5 * GC].rearrange("p (g c) -> p g c", g=G5)
                LT(diag, eye, d5, ALU.mult)
                V.tensor_tensor(kt[:, :, 0:GC], kt[:, :, 0:GC], diag, ALU.add).then_inc(k_ready, 1)
                dve.wait_ge(k_ready, 1)
                dve.wait_ge(e_done, 1)
                for h in range(2):
                    q4 = slice(4 * h, 4 * h + 4)
                    E = lambda c: ps[2 + 2 * c + h][:, :].rearrange("p (q m) -> p q m", q=4)
                    s0, s1 = (tmp[:, c, 512 * h:512 * h + 512].rearrange("p (q m) -> p q m", q=4) for c in range(2))
                    cmul(ws[:, 0, q4, :], ws[:, 1, q4, :], E(0), E(1), turn[:, 0, q4, :], turn[:, 1, q4, :], s0, s1, -1)
                for q in range(QS):
                    for c in range(2):
                        ch.add(V.tensor_tensor_scan(ws[:, c, q, :], co[:, 15, q:q + 1].broadcast_to([P, M5]),
                                                    ws[:, c, q, :], 0.0, ALU.mult, ALU.add))
                ch.sync()
                dve.wait_ge(pads, 3)
                cmul(xb[:, 0, :, 1:], xb[:, 1, :, 1:], ws[:, 0, :, :], ws[:, 1, :, :], turn[:, 0, :, :], turn[:, 1, :, :],
                     *scratch(QS, M5))
                dve.sem_inc(x_ready, 1)
                y = t["ycT"]
                ch.add(V.tensor_scalar(hglu[:, :], col(t, "glu_b", 0, 2), 0.5, None, ALU.mult))
                for a in range(2):
                    dve.wait_ge(g_sq, a + 1)
                    ch.link(V.tensor_scalar(gate[:, a, :], gate[:, a, :], 0.044715, 1.0, ALU.mult, ALU.add))
                    V.tensor_tensor(gate[:, a, :], gate[:, a, :], y[:, a, :], ALU.mult).then_inc(g_in, 1)
                for a in range(2):
                    dve.wait_ge(g_tanh, a + 1)
                    V.scalar_tensor_tensor(y[:, a, :], gate[:, a, :], 1.0, y[:, a, :], ALU.add, ALU.mult).then_inc(z2_ready, 1)
                dve.wait_ge(z2_ready, 2)
                dve.wait_ge(glu_done, 4)
                for a in range(2):
                    dve.wait_ge(glu_tanh, 2 * (a + 1))
                    ch.link(V.scalar_tensor_tensor(glu[:, a, :], glu[:, a, :], 1.0, y[:, a, :], ALU.add, ALU.mult))
                    ch.link(V.tensor_scalar(y[:, a, :], glu[:, a, :], 0.25, None, ALU.mult))

            @block.tensor
            def _(pe):
                mm, tr, ident = nc.tensor.matmul, nc.tensor.transpose, t["ident"][:, :]
                wait_w_in(pe, t, 0)
                for j in range(J5):
                    if j >= 2:
                        pe.wait_ge(u_taken, j - 1)
                    for k in range(KT):
                        last = mm(ps[j % 2][:, 0:DC], t["hT"][:, k, j::J5], ring[:, 0, k, 0:DC],
                                  start=(k == 0), stop=(k == KT - 1))
                    last.then_inc(u_done, 1)
                pe.wait_ge(u_taken, J5)
                for g in range(G5):
                    last = tr(ps[2 + g // 4][:, (g % 4) * P:(g % 4 + 1) * P], um[:, g, :, :].rearrange("p j c -> p (j c)"), ident)
                    if g % 4 == 3:
                        last.then_inc(us_done, 1)
                for mt, (b, m) in enumerate(tiles):
                    if m == 0:
                        wait_w_in(pe, t, b)
                    for half in range(2):
                        g = 2 * mt + half
                        if g >= 2:
                            pe.wait_ge(proj_taken, g - 1)
                        for k in range(KT):
                            last = mm(ps[g % 2][:, :], ring[:, b % 2, k, m * P:(m + 1) * P],
                                      t["hT"][:, k, half * 512:half * 512 + 512], start=(k == 0), stop=(k == KT - 1))
                        last.then_inc(proj_done, 1)
                    if mt == WT_AT:
                        pe.wait_ge(ws_ready, 1)
                        for i in range(2 * QS):
                            q, c = divmod(i, 2)
                            if i % 4 == 0:
                                pe.wait_ge(us_taken, i // 4 + 1)
                            last = tr(ps[2 + i // 4][:, (i % 4) * P:(i % 4 + 1) * P], ws[:, c, q, :], ident)
                            if i % 4 == 3:
                                last.then_inc(wt_done, 1)
                    if mt == E_AT:
                        pe.wait_ge(wt_taken, 4)
                        for q in range(QS):
                            for c in range(2):
                                for e in range(2):
                                    last = mm(ps[2 + 2 * c + q // 4][e * P5:(e + 1) * P5, (q % 4) * P:(q % 4 + 1) * P],
                                              wt[:, q, c, e * P5:(e + 1) * P5], us[:, 2 * q + e, :], start=True, stop=True)
                        last.then_inc(e_done, 1)
                        pe.wait_ge(cl_ready, 1)
                        for i in range(4):
                            h, e = divmod(i, 2)
                            r = slice(e * P5, (e + 1) * P5)
                            if h:
                                pe.wait_ge(k_taken, e + 1)
                            for q in range(4 * h, 4 * h + 4):
                                for c in range(2):
                                    last = mm(ps[6 + e][0:GC, (q % 4) * P:(q % 4 + 1) * P], bb[r, c, q, :],
                                              cl[r, c, q, 0:J5, :].rearrange("p l c -> p (l c)"),
                                              start=(c == 0), stop=(c == 1))
                            last.then_inc(k_done, 1)
                    if mt == Y_AT:
                        pe.wait_ge(k_taken, 4)
                        pe.wait_ge(tz_in, 16 * J5)
                        pe.wait_ge(x_ready, 1)
                        for i in range(4):
                            h, e = divmod(i, 2)
                            r = slice(e * P5, (e + 1) * P5)
                            if h:
                                pe.wait_ge(y_taken, e + 1)
                            for q in range(4 * h, 4 * h + 4):
                                o = ps[6 + e][:, (q % 4) * P:(q % 4 + 1) * P]
                                mm(o, us[:, 2 * q + e, :], tz[:, 2 * q + e, :], start=True, stop=False)
                                for c in range(2):
                                    last = mm(o, xb[r, c, q, 0:M5], cl[r, c, q, 1:, :].rearrange("p l c -> p (l c)"),
                                              start=False, stop=(c == 1))
                            last.then_inc(y_done, 1)
                    if mt == YT_AT:
                        pe.wait_ge(y_taken, 4)
                        for i in range(16):
                            last = tr(ps[2 + i // 4][:, (i % 4) * P:(i % 4 + 1) * P],
                                      ym[:, i % J5, (i // J5) * P:(i // J5 + 1) * P], ident)
                            if i % 4 == 3:
                                last.then_inc(yt_done, 1)
                    if mt == GLU_AT:
                        pe.wait_ge(small_in, 32)
                        pe.wait_ge(yt_taken, 4)
                        pe.wait_ge(z2_ready, 2)
                        for g in range(4):
                            a, hf = divmod(g, 2)
                            for k in range(2):
                                last = mm(ps[4 + g][:, :], gluw[:, k, a * P:(a + 1) * P],
                                          t["ycT"][:, k, hf * 512:hf * 512 + 512], start=(k == 0), stop=(k == 1))
                            last.then_inc(glu_done, 1)


def phase_b(nc, t, io):
    ps = t["ps"]
    pB, at, bt, bonus, ec = t["pB"], t["a_til"], t["b_hat"], t["bonus"], t["chunk_decay"]
    with ExitStack() as ctx:
        sb = lambda n, s, d=F32: ctx.enter_context(nc.sbuf_tensor(n, s, d, side="right"))
        sem = ctx.enter_context(phase_semaphores(nc))
        ring = t["ring"]
        lora = sb("pb_lora", [P, DB])
        cst = sb("pb_cst", [P, P + 2])
        hcol = sb("pb_hcol", [P, 2, QB])
        T = sb("pb_t", [P, 5, S])
        small_in = sem("pb_small_in")
        proj_done, proj_taken = sem("pb_proj_done"), sem("pb_proj_taken")
        seg_ready, lora_ready, lora_tanh = sem("pb_seg"), sem("pb_lora_ready"), sem("pb_lora_tanh")
        z_done, z_taken = sem("pb_z_done"), sem("pb_z_taken")
        ell_ready, exps = sem("pb_ell_ready"), sem("pb_exps")
        kk_ready, sq_ready, ss_done, ss_taken, root = (sem("pb_kk"), sem("pb_sq"), sem("pb_ss_done"),
                                                       sem("pb_ss_taken"), sem("pb_root"))
        rk_ready, bon_done, bon_taken, q_free = sem("pb_rk"), sem("pb_bon_done"), sem("pb_bon_taken"), sem("pb_q_free")
        dve_c = sem("pb_dve")
        H = VO // 2
        n_cm = 2 * QA
        tok_groups = [(i, hf) for hf in range(2) for i in range(NT)]

        with nc.Block() as block:
            @block.sync
            def _(sp):
                load_w_in(sp, io, t, 6)
                sp.dma_start(lora[:, :], io["lora"]).then_inc(small_in, 16)
                sp.dma_start(cst[:, :], io["rwkv_cst"]).then_inc(small_in, 16)
                sp.wait_ge(proj_done, n_cm)
                load_w_in(sp, io, t, 7)

            @block.gpsimd
            def _(pool):
                nc.gpsimd.memset(t["qk"][:, :, 0:CONV_K - 1], 0.0)
                nc.gpsimd.memset(t["seg64"][:, :], 1.0).then_inc(seg_ready, 1)
                pool.wait_ge(seg_ready, 1)
                nc.gpsimd.memset(t["seg64"][:, 0::HD], 0.0).then_inc(seg_ready, 1)

            @block.scalar
            def _(act):
                A = nc.scalar.activation

                def take_proj(g):
                    act.wait_ge(proj_done, g + 1)
                    if g < n_cm:
                        m, hf = divmod(g, 2)
                        dst = t["qk"][:, m, CONV_K - 1 + hf * 512:CONV_K - 1 + hf * 512 + 512]
                        src = ps[g % 2][:, :]
                    else:
                        i, hf = tok_groups[g - n_cm]
                        dst, src = t["vo"][:, i, hf * H:(hf + 1) * H], ps[g % 2][:, 0:H]
                    A(dst, src, ACT.Copy).then_inc(proj_taken, 1)

                def elementwise(q):
                    if q:
                        act.wait_ge(q_free, q)
                    for part in range(4):
                        c, hf = divmod(part, 2)
                        act.wait_ge(z_done, 4 * q + part + 1)
                        A(T[:, c, hf * 512:hf * 512 + 512], ps[2 + part][:, :], ACT.Tanh,
                          bias=hcol[:, c, q:q + 1], scale=0.5).then_inc(z_taken, 1)
                    act.wait_ge(kk_ready, q + 1)
                    A(T[:, 4, :], T[:, 3, :], ACT.Square).then_inc(sq_ready, 1)
                    act.wait_ge(ell_ready, q + 1)
                    A(T[:, 0, :], T[:, 0, :], ACT.Exp).then_inc(exps, 1)
                    A(T[:, 2, :], T[:, 2, :], ACT.Exp).then_inc(exps, 1)
                    act.wait_ge(ss_taken, 2 * (q + 1))
                    A(T[:, 4, :], T[:, 4, :], ACT.Sqrt).then_inc(root, 1)

                for g in range(n_cm):
                    take_proj(g)
                    if g == 1:
                        act.wait_ge(lora_ready, 2)
                        A(pB[0:HD, 9, 1:], pB[0:HD, 9, 1:], ACT.Tanh).then_inc(lora_tanh, 1)
                        A(pB[:, 10, 1:], pB[:, 10, 1:], ACT.Tanh, scale=0.5).then_inc(lora_tanh, 1)
                for n in range(2 * NT):
                    if n in (0, 4, 8):
                        elementwise(n // 4)
                    take_proj(n_cm + n)
                    if n in (3, 7, 11):
                        q = n // 4
                        act.wait_ge(bon_done, q + 1)
                        A(bonus[:, :, 2 * q:2 * q + 2], ps[2][:, 0:2 * NT].rearrange("p (i e) -> p i e", e=2),
                          ACT.Copy).then_inc(bon_taken, 1)

            @block.vector
            def _(dve):
                ch = Chain(dve, dve_c)
                V = nc.vector

                def shift(i):
                    ch.link(V.tensor_tensor(T[:, 4, :], pB[:, i, 0:S], pB[:, i, 1:1 + S], ALU.subtract))
                    return V.scalar_tensor_tensor(pB[:, i, 1:1 + S], T[:, 4, :], col(t, "mu", i), pB[:, i, 1:1 + S],
                                                  ALU.mult, ALU.add)

                ch.add(V.tensor_scalar(hcol[:, 0, :], col(t, "w0", 0, QB), 0.5, None, ALU.mult))
                ch.link(V.tensor_scalar(hcol[:, 1, :], col(t, "a0", 0, QB), 0.5, None, ALU.mult))
                for i in (9, 10):
                    shift(i).then_inc(lora_ready, 1)
                    dve.wait_ge(lora_ready, i - 8)
                for i in range(9):
                    ch.link(shift(i))
                dve.wait_ge(lora_tanh, 2)
                ch.link(V.tensor_scalar(pB[:, 10, 1:], pB[:, 10, 1:], 1.0, 0.5, ALU.add, ALU.mult))
                dve.wait_ge(seg_ready, 2)
                for q in range(QB):
                    r, k = pB[:, q, 1:], pB[:, 3 + q, 1:]
                    V.tensor_scalar(T[:, 3, :], k, col(t, "k_k", q), None, ALU.mult).then_inc(kk_ready, 1)
                    dve.wait_ge(z_taken, 4 * (q + 1))
                    ch.add(V.tensor_scalar(T[:, 1, :], T[:, 1, :], 1.0, 0.5, ALU.add, ALU.mult))
                    ch.link(V.tensor_scalar(T[:, 0, :], T[:, 0, :], 1.0, RWKV_DECAY, ALU.add, ALU.mult))
                    ch.link(V.tensor_tensor_scan(T[:, 2, :], t["seg64"][:, :], T[:, 0, :], 0.0, ALU.mult, ALU.add))
                    V.tensor_tensor(T[:, 0, :], T[:, 2, :], T[:, 0, :], ALU.subtract).then_inc(ell_ready, 1)
                    for hf in range(2):
                        dve.wait_ge(ss_done, 2 * q + hf + 1)
                        V.tensor_scalar(T[:, 4, hf * 512:hf * 512 + 512], ps[6 + hf][:, :], 1e-24, None,
                                        ALU.max).then_inc(ss_taken, 1)
                    f = at[:, q, :]
                    ch.link(V.tensor_scalar(f, T[:, 1, :], -1.0, col(t, "k_a", q), ALU.add, ALU.mult))
                    ch.link(V.scalar_tensor_tensor(k, f, 1.0, k, ALU.add, ALU.mult))
                    ch.link(V.tensor_scalar(f, r, col(t, "r_k", q), None, ALU.mult))
                    dve.wait_ge(root, q + 1)
                    ch.link(V.reciprocal(T[:, 4, :], T[:, 4, :]))
                    ch.link(V.tensor_tensor(T[:, 3, :], T[:, 3, :], T[:, 4, :], ALU.mult))
                    V.tensor_tensor(T[:, 4, :], f, k, ALU.mult).then_inc(rk_ready, 1)
                    ch.add(V.tensor_tensor(T[:, 1, :], T[:, 3, :], T[:, 1, :], ALU.mult))
                    dve.wait_ge(exps, 2 * (q + 1))
                    ch.add(V.tensor_tensor(r, r, T[:, 2, :], ALU.mult))
                    ch.add(V.tensor_copy(ec[:, q, :], T[:, 2, 63::64]))
                    dve.wait_ge(rk_ready, q + 1)
                    ch.link(V.scalar_tensor_tensor(f, T[:, 3, :], -1.0, T[:, 0, :], ALU.mult, ALU.mult))
                    ch.link(V.reciprocal(T[:, 0, :], T[:, 2, :]))
                    ch.add(V.tensor_tensor(k, k, T[:, 0, :], ALU.mult))
                    ch.link(V.tensor_tensor(bt[:, q, :], T[:, 1, :], T[:, 0, :], ALU.mult))
                    dve.wait_ge(bon_done, q + 1)
                    dve.sem_inc(q_free, 1)

            @block.tensor
            def _(pe):
                def proj(g):
                    if g < n_cm:
                        if g == 0:
                            wait_w_in(pe, t, 5)
                        m, hf = divmod(g, 2)
                        ops = [(ring[:, 1, k, m * P:(m + 1) * P], t["hT"][:, k, hf * 512:hf * 512 + 512])
                               for k in range(KT)]
                        out = ps[g % 2][:, :]
                    else:
                        i, hf = tok_groups[g - n_cm]
                        wait_w_in(pe, t, 6 + hf)
                        ops = [(t["hT"][:, k, i * P:(i + 1) * P], ring[:, hf, k, :]) for k in range(KT)]
                        out = ps[g % 2][:, 0:H]
                    if g >= 2:
                        pe.wait_ge(proj_taken, g - 1)
                    for k, (a, b) in enumerate(ops):
                        last = nc.tensor.matmul(out, a, b, start=(k == 0), stop=(k == KT - 1))
                    last.then_inc(proj_done, 1)

                def z(q):
                    if q == 0:
                        pe.wait_ge(small_in, 32)
                        pe.wait_ge(lora_tanh, 1)
                        pe.wait_ge(lora_ready, 1)
                    for part in range(4):
                        c, hf = divmod(part, 2)
                        if q:
                            pe.wait_ge(z_taken, 4 * (q - 1) + part + 1)
                            pe.wait_ge(bon_taken, q)
                        rows = slice(c * HD, (c + 1) * HD)
                        nc.tensor.matmul(ps[2 + part][:, :], lora[rows, q * P:(q + 1) * P],
                                         pB[rows, 9, 1 + hf * 512:1 + hf * 512 + 512], start=True, stop=True
                                         ).then_inc(z_done, 1)

                def ss(q):
                    pe.wait_ge(sq_ready, q + 1)
                    for hf in range(2):
                        if q:
                            pe.wait_ge(ss_taken, 2 * (q - 1) + hf + 1)
                        nc.tensor.matmul(ps[6 + hf][:, :], cst[:, 0:P], T[:, 4, hf * 512:hf * 512 + 512],
                                         start=True, stop=True).then_inc(ss_done, 1)

                def bon(q):
                    pe.wait_ge(rk_ready, q + 1)
                    pe.wait_ge(z_taken, 4 * (q + 1))
                    for i in range(NT):
                        last = nc.tensor.matmul(ps[2][:, 2 * i:2 * i + 2], T[:, 4, i * P:(i + 1) * P],
                                                cst[:, P:P + 2], start=True, stop=True)
                    last.then_inc(bon_done, 1)

                for g in range(n_cm):
                    proj(g)
                for n in range(2 * NT):
                    if n in (0, 4, 8):
                        z(n // 4)
                        ss(n // 4)
                    proj(n_cm + n)
                    if n in (3, 7, 11):
                        bon(n // 4)


def phase_c(nc, t, io):
    ps = t["ps"]
    pB, at, bt = t["pB"], t["a_til"], t["b_hat"]
    with ExitStack() as ctx:
        sb = lambda n, s, d=F32: ctx.enter_context(nc.sbuf_tensor(n, s, d, side="right"))
        sem = ctx.enter_context(phase_semaphores(nc))
        msk = sb("pc_msk", [P, 384 + 3 * 384])
        rows = sb("pc_rows", [P, 2, DB])
        gup = sb("pc_gup", [P, DB])
        tok = sb("pc_tok", [P, 2, DB])
        v = sb("pc_v", [P, 2, DB])
        gm = sb("pc_gm", [P, HB, 3 * P])
        ad, adT, aoT = sb("pc_ad", [P, HB, P]), sb("pc_adT", [P, HB, P]), sb("pc_aoT", [P, HB, P])
        p2, p2T, p4, p4T = (sb(f"pc_{n}", [P, HB, P]) for n in ("p2", "p2T", "p4", "p4T"))
        X = sb("pc_X", [P, HB, P])
        av = sb("pc_av", [P, DB])
        ra = sb("pc_ra", [P, DB])
        sa = sb("pc_sa", [P, DB])
        st = sb("pc_state", [P, QB, P])
        sd = sb("pc_sdec", [P, QB, P])
        y = sb("pc_y", [P, 2, DB])
        g = sb("pc_g", [P, DB])
        o = sb("pc_o", [P, 2, DB])
        m = sb("pc_m", [P, 4, HB])
        ada = sb("pc_ada", [P, 2, KT, 256])
        ada_row = sb("pc_ada_row", [1, 512])
        CB = 128
        cv = sb("pc_conv", [P, 2, CB])
        small_in, zeroed = sem("pc_small_in"), sem("pc_zeroed")
        tr_done, tr_taken = sem("pc_tr_done"), sem("pc_tr_taken")
        gate_done, gate_taken = sem("pc_gate_done"), sem("pc_gate_taken")
        gram_done, gram_taken = sem("pc_gram_done"), sem("pc_gram_taken")
        a_done, a_taken = sem("pc_a_done"), sem("pc_a_taken")
        av_done, av_taken = sem("pc_av_done"), sem("pc_av_taken")
        st_done = [sem(f"pc_stage_done{h}") for h in range(2)]
        copied = [sem(f"pc_copied{h}") for h in range(2)]
        added = [sem(f"pc_added{h}") for h in range(2)]
        ra_done, ra_taken, sa_done, sa_taken = sem("pc_ra_done"), sem("pc_ra_taken"), sem("pc_sa_done"), sem("pc_sa_taken")
        sn_done, s_ready = sem("pc_sn_done"), sem("pc_s_ready")
        y1_taken, y2_done, y_ready = sem("pc_y1_taken"), sem("pc_y2_done"), sem("pc_y_ready")
        var_ready, root = sem("pc_var"), sem("pc_root")
        o_ready, ot_done, ot_taken = sem("pc_o_ready"), sem("pc_ot_done"), sem("pc_ot_taken")
        ada_in, ada_used, mod_taken = [sem("pc_ada_in0"), sem("pc_ada_in1")], sem("pc_ada_used"), sem("pc_mod_taken")
        row_ready, cols_done = sem("pc_ada_row_ready"), sem("pc_ada_cols")
        dve_c, pool_c = sem("pc_dve"), sem("pc_pool")
        CP = [0, 2, 4, 5, 5, 6, 8, 9, 9]
        AD = [0, 0, 1, 2, 3, 3, 3, 4, 5]
        NST, NCP, NAD = 8, CP[-1], AD[-1]
        bank = lambda h, b: ps[3 * h + b]
        ORDER = [0, 2, 4, 1, 3, 5]
        cols3 = lambda a: a[:, 0:384].rearrange("p (h n) -> p h n", h=3)

        with nc.Block() as block:
            @block.sync
            def _(sp):
                sp.dma_start(msk[:, :], io["rwkv_masks"]).then_inc(small_in, 16)
                sp.dma_start(rows[:, :, :], io["rows_rwkv"].rearrange("p (a n) -> p a n", a=2)).then_inc(small_in, 16)
                sp.dma_start(gup[:, :], io["g_up"]).then_inc(small_in, 16)
                weights = io["ada_w"].rearrange("o (k p) n -> p (o k) n", p=P)
                for b in range(2 * NT):
                    if b >= 2:
                        sp.wait_ge(ada_used, b - 1)
                    c0 = 2 * D + b * 256
                    sp.dma_start(ada[:, b % 2, :, :], weights[:, :, c0:c0 + 256]).then_inc(ada_in[b % 2], 16)

            @block.gpsimd
            def _(pool):
                nc.gpsimd.memset(st[:, :, :], 0.0).then_inc(zeroed, 1)
                ch = Chain(pool, pool_c)
                G = nc.gpsimd
                qk = t["qk"]
                for q in range(QA):
                    for b in reversed(range(S // CB)):
                        x = lambda j: qk[:, q, b * CB + j:b * CB + j + CB]
                        cw = lambda j: col(t, "conv_w", q * CONV_K + j)
                        ch.link(G.tensor_scalar(cv[:, 0, :], x(0), cw(0), col(t, "conv_b", q), ALU.mult, ALU.add))
                        for j in range(1, CONV_K):
                            ch.link(G.tensor_scalar(cv[:, 1, :], x(j), cw(j), None, ALU.mult))
                            o_ = x(CONV_K - 1) if j == CONV_K - 1 else cv[:, 0, :]
                            ch.link(G.tensor_tensor(o_, cv[:, 0, :], cv[:, 1, :], ALU.add))

            @block.scalar
            def _(act):
                cp = lambda d, s: nc.scalar.activation(d, s, ACT.Copy)

                def take_ot(i):
                    act.wait_ge(ot_done, i + 1)
                    cp(pB[:, 0:QB, 1 + i * P:1 + (i + 1) * P], cols3(ps[4])).then_inc(ot_taken, 1)

                def take_gate(i):
                    act.wait_ge(gate_done, i + 1)
                    if i:
                        act.wait_ge(o_ready, i)
                    cp(g[:, :], ps[3][:, 0:DB]).then_inc(gate_taken, 1)

                def roots(i):
                    act.wait_ge(var_ready, i + 1)
                    nc.scalar.activation(m[:, 2, :], m[:, 1, :], ACT.Sqrt).then_inc(root, 1)

                for i in range(NT):
                    for b, dst in enumerate((tok[:, 0, :], tok[:, 1, :], v[:, i % 2, :])):
                        act.wait_ge(tr_done, 3 * i + b + 1)
                        if b == 2 and i >= 2:
                            act.wait_ge(o_ready, i - 1)
                        cp(dst, ps[b][:, 0:DB]).then_inc(tr_taken, 1)
                    if i:
                        take_gate(i - 1)
                    copies = [[(p2, 1), (p2T, 2)], [(p4, 1), (p4T, 2)], [(p2, 1)], [], [(p4, 1)],
                              [(p2, 0), (p2T, 2)], [(p4, 1)], []]
                    for s in range(NST):
                        for h in range(2):
                            if copies[s]:
                                act.wait_ge(st_done[h], NST * i + s + 1)
                            for dst, b in copies[s]:
                                cp(dst[:, 3 * h:3 * h + 3, :], cols3(bank(h, b))).then_inc(copied[h], 1)
                        if s == 0 and i:
                            roots(i - 1)
                    if i:
                        take_ot(i - 1)
                    for c in range(2):
                        R = slice(64 * c, 64 * c + 64)
                        act.wait_ge(sa_done, 2 * i + c + 1)
                        cp(sa[R, :], ps[4][R, 0:DB]).then_inc(sa_taken, 1)
                    act.wait_ge(sn_done, 2 * (i + 1))
                    if i >= 2:
                        act.wait_ge(o_ready, i - 1)
                    cp(y[:, i % 2, :], ps[6][:, 0:DB]).then_inc(y1_taken, 1)
                take_gate(NT - 1)
                roots(NT - 1)
                take_ot(NT - 1)

            @block.vector
            def _(dve):
                ch = Chain(dve, dve_c)
                V = nc.vector
                L = lambda *a: ch.link(V.tensor_tensor(*a))
                M3 = lambda k: msk[:, 384 * (k + 1):384 * (k + 2)].rearrange("p (h n) -> p h n", h=3)

                def out(i):
                    yi = y[:, i % 2, :].rearrange("p (h n) -> p h n", h=HB)
                    ov = [o[:, k, :].rearrange("p (h n) -> p h n", h=HB) for k in range(2)]
                    vv = v[:, i % 2, :].rearrange("p (h n) -> p h n", h=HB)
                    bc = lambda a: a.unsqueeze(2).broadcast_to([P, HB, HD])
                    if i:
                        dve.wait_ge(ot_done, i)
                    dve.wait_ge(y_ready, i + 1)
                    ch.link(V.tensor_reduce(m[:, 0, :], yi, AX.X, ALU.add))
                    ch.link(V.tensor_scalar(m[:, 0, :], m[:, 0, :], 1.0 / HD, None, ALU.mult))
                    L(ov[0], yi, bc(m[:, 0, :]), ALU.subtract)
                    L(ov[1], ov[0], ov[0], ALU.mult)
                    ch.link(V.tensor_reduce(m[:, 1, :], ov[1], AX.X, ALU.add))
                    V.tensor_scalar(m[:, 1, :], m[:, 1, :], 1.0 / HD, GN_EPS, ALU.mult, ALU.add).then_inc(var_ready, 1)
                    L(ov[1], vv, bc(t["bonus"][:, i, :]), ALU.mult)
                    L(o[:, 1, :], o[:, 1, :], rows[:, 1, :], ALU.add)
                    dve.wait_ge(root, i + 1)
                    ch.link(V.reciprocal(m[:, 3, :], m[:, 2, :]))
                    L(ov[0], ov[0], bc(m[:, 3, :]), ALU.mult)
                    L(o[:, 0, :], o[:, 0, :], rows[:, 0, :], ALU.mult)
                    L(o[:, 0, :], o[:, 0, :], o[:, 1, :], ALU.add)
                    dve.wait_ge(gate_taken, i + 1)
                    V.tensor_tensor(o[:, 0, :], o[:, 0, :], g[:, :], ALU.mult).then_inc(o_ready, 1)

                def take_cols(i):
                    dve.wait_ge(cols_done, i + 1)
                    V.scalar_tensor_tensor(t["mod_cols"][:, 4 * i:4 * i + 4], ps[7][:, 0:4], 0.5,
                                           col(t, "ada_b", 2 * KT + 4 * i, 4), ALU.mult, ALU.add).then_inc(mod_taken, 1)

                dve.wait_ge(small_in, 48)
                dve.wait_ge(zeroed, 1)
                for i in range(NT):
                    for h in range(HB):
                        dve.wait_ge(gram_done, HB * i + h + 1)
                        G = ps[6 + h % 2]
                        ch.add(V.tensor_tensor(gm[:, h, :], G[:, P:512], msk[:, 0:384], ALU.mult))
                        ch.add(V.tensor_tensor(adT[:, h, :], G[:, 0:P], msk[:, 384:384 + P], ALU.mult))
                        V.tensor_tensor(aoT[:, h, :], G[:, 0:P], msk[:, 768:768 + P], ALU.mult).then_inc(gram_taken, 1)
                        if h % 3 == 2:
                            half = h // 3
                            hs = slice(3 * half, 3 * half + 3)
                            dve.wait_ge(a_done, 2 * i + half + 1)
                            ch.add(V.tensor_tensor(ad[:, hs, :], cols3(bank(half, 0)), M3(2), ALU.mult))
                            ch.sync()
                            V.tensor_tensor(X[:, hs, :], adT[:, hs, :],
                                            t["ident"][:, :].unsqueeze(1).broadcast_to([P, 3, P]),
                                            ALU.add).then_inc(a_taken, 1)
                    dve.wait_ge(av_done, i + 1)
                    V.tensor_copy(av[:, :], ps[6][:, 0:DB]).then_inc(av_taken, 1)
                    if i:
                        out(i - 1)
                    for s in (1, 2, 3, 6, 7):
                        for h in range(2):
                            hs = slice(3 * h, 3 * h + 3)
                            dve.wait_ge(st_done[h], NST * i + s + 1)
                            V.tensor_tensor(X[:, hs, :], X[:, hs, :], cols3(bank(h, 0)), ALU.add).then_inc(added[h], 1)
                    if i:
                        take_cols(i - 1)
                    for c in range(2):
                        n = 2 * i + c
                        R = slice(64 * c, 64 * c + 64)
                        dve.wait_ge(ra_done, n + 1)
                        V.tensor_tensor(ra[R, :], ps[7][R, 0:DB], av[R, :], ALU.add).then_inc(ra_taken, 1)
                        for q in range(QB):
                            ch.add(V.tensor_scalar(sd[:, q, :], st[:, q, :], t["chunk_decay"][:, q, n:n + 1], None,
                                                   ALU.mult))
                        ch.sync()
                        dve.wait_ge(sn_done, n + 1)
                        for q in range(QB):
                            for e in range(2):
                                r = slice(64 * e, 64 * e + 64)
                                last = V.scalar_tensor_tensor(
                                    st[r, q, 64 * e:64 * e + 64], ps[5][r, q * P + 64 * e:q * P + 64 * e + 64],
                                    t["chunk_decay"][r, q, n:n + 1], sd[r, q, 64 * e:64 * e + 64], ALU.mult, ALU.add)
                                ch.add(last)
                        ch.sync()
                        dve.sem_inc(s_ready, 1)
                    dve.wait_ge(ada_used, 2 * (i + 1))
                    V.tensor_copy(ada_row[:, :], ps[1][0:1, :]).then_inc(row_ready, 1)
                    dve.wait_ge(y2_done, i + 1)
                    dve.wait_ge(y1_taken, i + 1)
                    V.tensor_tensor(y[:, i % 2, :], y[:, i % 2, :], ps[3][:, 0:DB], ALU.add).then_inc(y_ready, 1)
                take_cols(NT - 1)
                out(NT - 1)

            @block.tensor
            def _(pe):
                mm = nc.tensor.matmul

                def gate(i):
                    mm(ps[3][:, 0:DB], pB[:, 10, 1 + i * P:1 + (i + 1) * P], gup[:, :], start=True, stop=True
                       ).then_inc(gate_done, 1)

                def out_t(i):
                    pe.wait_ge(o_ready, i + 1)
                    for q in range(QB):
                        last = nc.tensor.transpose(ps[4][:, q * P:(q + 1) * P], o[:, 0, q * P:(q + 1) * P],
                                                   t["ident"][:, :])
                    last.then_inc(ot_done, 1)

                def adaln(i, c, ks):
                    b = 2 * i + c
                    if ks[0] == 0:
                        pe.wait_ge(ada_in[b % 2], 16 * (b // 2 + 1))
                    for k in ks:
                        last = mm(ps[1][0:1, c * 256:(c + 1) * 256], t["cond"][:, k:k + 1], ada[:, b % 2, k, :],
                                  start=(k == 0), stop=(k == KT - 1))
                    if ks[-1] == KT - 1:
                        last.then_inc(ada_used, 1)

                def ada_cols(i):
                    pe.wait_ge(row_ready, i + 1)
                    for v_ in range(4):
                        last = mm(ps[7][:, v_:v_ + 1], ada_row[0:1, v_ * P:(v_ + 1) * P], t["ident"][0:1, 0:1],
                                  start=True, stop=True)
                    last.then_inc(cols_done, 1)

                for i in range(NT):
                    T0, T1 = i * P, (i + 1) * P
                    if i:
                        pe.wait_ge(row_ready, i)
                    vi = v[:, i % 2, :]
                    if i:
                        pe.wait_ge(added[0], NAD * i)
                        pe.wait_ge(copied[0], NCP * i)
                    for b in range(3):
                        for q in range(QB):
                            src = (bt[:, q, T0:T1], pB[:, 3 + q, 1 + T0:1 + T1], pB[:, 6 + q, 1 + T0:1 + T1])[b]
                            last = nc.tensor.transpose(ps[b][:, q * P:(q + 1) * P], src, t["ident"][:, :])
                        last.then_inc(tr_done, 1)
                    if i:
                        pe.wait_ge(y_ready, i)
                        gate(i - 1)
                    else:
                        pe.wait_ge(small_in, 48)
                        pe.wait_ge(zeroed, 1)
                    for h, head in enumerate(ORDER):
                        q, e = divmod(head, 2)
                        r = slice(64 * e, 64 * e + 64)
                        A_, R_ = at[r, q, T0:T1], pB[r, q, 1 + T0:1 + T1]
                        B_, K_ = bt[r, q, T0:T1], pB[r, 3 + q, 1 + T0:1 + T1]
                        if HB * i + h >= 2:
                            pe.wait_ge(gram_taken, HB * i + h - 1)
                        if h < 2 and i:
                            pe.wait_ge(y1_taken, i)
                            pe.wait_ge(ra_taken, 2 * i)
                        G = ps[6 + h % 2]
                        mm(G[:, 0:P], B_, A_, start=True, stop=True)
                        mm(G[:, P:2 * P], B_, R_, start=True, stop=True)
                        mm(G[:, 2 * P:3 * P], K_, A_, start=True, stop=True)
                        mm(G[:, 3 * P:], K_, R_, start=True, stop=True).then_inc(gram_done, 1)
                        half = h // 3
                        if h % 3 == 0:
                            if half == 0:
                                pe.wait_ge(tr_taken, 3 * i + 1)
                            elif i:
                                pe.wait_ge(gate_taken, i)
                        last = mm(bank(half, 0)[:, (h % 3) * P:(h % 3 + 1) * P], A_, B_, start=True, stop=True)
                        if h % 3 == 2:
                            last.then_inc(a_done, 1)
                    pe.wait_ge(gram_taken, HB * (i + 1))
                    pe.wait_ge(tr_taken, 3 * (i + 1))
                    for h, head in enumerate(ORDER):
                        last = mm(ps[6][:, head * HD:(head + 1) * HD], gm[:, h, P:2 * P], vi[:, head * HD:(head + 1) * HD],
                                  start=True, stop=True)
                    last.then_inc(av_done, 1)
                    if i:
                        ada_cols(i - 1)
                    stages = [[(1, adT, ad), (2, ad, adT)], [(0, p2, X), (1, p2T, p2), (2, p2, p2T)],
                              [(0, p4, X), (1, p4T, p4)], [(0, p2, X)], None, [(0, aoT, p4), (2, p4, aoT)],
                              [(0, p2, X), (1, p2T, p2)], [(0, p4, X)]]
                    for s, prods in enumerate(stages):
                        for h in range(2):
                            if s == 0:
                                pe.wait_ge(a_taken, 2 * i + h + 1)
                                if h and i:
                                    pe.wait_ge(added[1], NAD * i)
                                    pe.wait_ge(copied[1], NCP * i)
                                    pe.wait_ge(s_ready, 2 * i)
                                    pe.wait_ge(sa_taken, 2 * i)
                            else:
                                if NCP * i + CP[s]:
                                    pe.wait_ge(copied[h], NCP * i + CP[s])
                                if NAD * i + AD[s]:
                                    pe.wait_ge(added[h], NAD * i + AD[s])
                            for j in range(3):
                                n = 3 * h + j
                                if prods is None:
                                    last = nc.tensor.transpose(bank(h, 1)[:, j * P:(j + 1) * P], X[:, n, :],
                                                               t["ident"][:, :])
                                    continue
                                for b, lhs, rhs in prods:
                                    last = mm(bank(h, b)[:, j * P:(j + 1) * P], lhs[:, n, :], rhs[:, n, :],
                                              start=True, stop=True)
                            last.then_inc(st_done[h], 1)
                    pe.wait_ge(added[1], NAD * (i + 1))
                    pe.wait_ge(added[0], NAD * (i + 1))
                    pe.wait_ge(copied[1], NCP * (i + 1))
                    if i:
                        out_t(i - 1)
                    pe.wait_ge(av_taken, i + 1)
                    if i:
                        pe.wait_ge(mod_taken, i)
                    for c in range(2):
                        n = 2 * i + c
                        R = slice(64 * c, 64 * c + 64)
                        if n:
                            pe.wait_ge(s_ready, n)
                        for q in range(QB):
                            last = mm(ps[7][R, q * P:(q + 1) * P], at[:, q, T0 + 64 * c:T0 + 64 * c + 64],
                                      st[:, q, :], start=True, stop=True)
                        last.then_inc(ra_done, 1)
                        adaln(i, c, (0, 1))
                        for q in range(QB):
                            mm(ps[6][R, q * P:(q + 1) * P], pB[:, q, 1 + T0 + 64 * c:1 + T0 + 64 * c + 64],
                               st[:, q, :], start=True, stop=True)
                        pe.wait_ge(ra_taken, n + 1)
                        if c == 0 and i:
                            pe.wait_ge(ot_taken, i)
                        for h, head in enumerate(ORDER):
                            last = mm(ps[4][R, head * HD:(head + 1) * HD], X[R, h, 64 * c:64 * c + 64],
                                      ra[R, head * HD:(head + 1) * HD], start=True, stop=True)
                        last.then_inc(sa_done, 1)
                        adaln(i, c, (2, 3))
                        pe.wait_ge(sa_taken, n + 1)
                        for q in range(QB):
                            o_ = ps[5][:, q * P:(q + 1) * P]
                            mm(o_, tok[R, 1, q * P:(q + 1) * P], vi[R, q * P:(q + 1) * P], start=True, stop=False)
                            last = mm(o_, tok[R, 0, q * P:(q + 1) * P], sa[R, q * P:(q + 1) * P], start=False, stop=True)
                        last.then_inc(sn_done, 1)
                        adaln(i, c, (4, 5, 6, 7))
                    for h, head in enumerate(ORDER):
                        hc = slice(head * HD, (head + 1) * HD)
                        o_ = ps[3][:, hc]
                        mm(o_, gm[:, h, 2 * P:], vi[:, hc], start=True, stop=False)
                        last = mm(o_, gm[:, h, 0:P], sa[:, hc], start=False, stop=True)
                    last.then_inc(y2_done, 1)
                pe.wait_ge(y_ready, NT)
                gate(NT - 1)
                ada_cols(NT - 1)
                out_t(NT - 1)


def phase_d(nc, t, io):
    ps = t["ps"]
    pB, vo, qk = t["pB"], t["vo"], t["qk"]
    qT, kT = t["a_til"], t["b_hat"]
    W65 = HD + 1
    with ExitStack() as ctx:
        sb = lambda n, s, d=F32: ctx.enter_context(nc.sbuf_tensor(n, s, d, side="right"))
        sem = ctx.enter_context(phase_semaphores(nc))
        cst = sb("pd_cst", [P, (HA + QA + 1) * P])
        wqk = sb("pd_wqk", [P, 2, QA, P])
        nw = sb("pd_nw", [P, DA])
        vaug = sb("pd_vaug", [P, NT, HA, W65])
        M = sb("pd_M", [P, S])
        R4 = sb("pd_R4", [HA, 4, S])
        fz, bc_ = sb("pd_fz", [HA, S]), sb("pd_b", [HA, S])
        mp = sb("pd_mp", [HA, NT + 1])
        gcol = sb("pd_gcol", [P, NT, 4, HA])
        dec = sb("pd_dec", [P, QA, NT])
        E = sb("pd_E", [P, HA, P])
        Pm = sb("pd_P", [P, HA, P])
        kw = sb("pd_kw", [P, 2, DA])
        C = sb("pd_C", [P, QA, 2, W65])
        hb = sb("pd_h", [P, 2, HA, W65])
        scr = sb("pd_scr", [P, HA, HD])
        mom = sb("pd_mom", [P, 5, HA])
        small_in, prep = sem("pd_small_in"), sem("pd_prep")
        gt_done, f_ready, f_exp, f_ln = sem("pd_gt_done"), sem("pd_f_ready"), sem("pd_f_exp"), sem("pd_f_ln")
        arg_ready, exps = sem("pd_arg_ready"), sem("pd_exps")
        gc_done, gc_taken, m_ready = sem("pd_gc_done"), sem("pd_gc_taken"), sem("pd_m_ready")
        cv_tanh, cx_ready = sem("pd_cv_tanh"), sem("pd_cx_ready")
        qk_done, qk_taken = sem("pd_qk_done"), sem("pd_qk_taken")
        e_done, e_taken, sc_done, p_ready = sem("pd_e_done"), sem("pd_e_taken"), sem("pd_sc_done"), sem("pd_p_ready")
        kt_done, kt_taken, kw_ready = sem("pd_kt_done"), sem("pd_kt_taken"), sem("pd_kw_ready")
        it_done, ia_done, h_taken = sem("pd_it_done"), sem("pd_ia_done"), sem("pd_h_taken")
        c_done, c_ready = sem("pd_c_done"), sem("pd_c_ready")
        o_tanh, var_ready, root = sem("pd_o_tanh"), sem("pd_var"), sem("pd_root")
        y_ready, yt_done, yt_taken = sem("pd_y_ready"), sem("pd_yt_done"), sem("pd_yt_taken")
        mean_ready, sq_ready, factor_ready = sem("pd_mean"), sem("pd_sq"), sem("pd_factor")
        dve_c, pool_c = sem("pd_dve"), sem("pd_pool")
        sel = lambda h: cst[:, h * P:(h + 1) * P]
        pair_sel = lambda q: cst[0:HA, (HA + q) * P:(HA + q + 1) * P]
        causal = cst[:, (HA + QA) * P:(HA + QA + 1) * P]
        ORDER = [0, 2, 4, 1, 3, 5]
        cx = pB[:, 3:6, 1:]
        ov = vo[:, :, DA:2 * DA]

        with nc.Block() as block:
            @block.sync
            def _(sp):
                sp.dma_start(cst[:, :], io["mlstm_cst"]).then_inc(small_in, 16)
                sp.dma_start(wqk[:, :, :, :], io["wqk"]).then_inc(small_in, 16)
                sp.dma_start(nw[:, :], io["rows_mlstm"]).then_inc(small_in, 16)

            @block.gpsimd
            def _(pool):
                nc.gpsimd.memset(M[:, :], 0.0).then_inc(prep, 1)
                nc.gpsimd.memset(t["seg64"][:, HD::2 * HD], 1.0).then_inc(prep, 1)
                nc.gpsimd.memset(C[:, :, :, :], 0.0).then_inc(prep, 1)
                nc.gpsimd.memset(mp[:, 0:1], 0.0).then_inc(prep, 1)
                nc.gpsimd.memset(vaug[:, :, :, HD:W65], 1.0).then_inc(prep, 1)
                for i in range(NT):
                    nc.gpsimd.tensor_copy(vaug[:, i, :, 0:HD],
                                          vo[:, i, 0:DA].rearrange("p (h n) -> p h n", h=HA)).then_inc(prep, 1)
                ch = Chain(pool, pool_c)
                bu = lambda a: a.unsqueeze(2).broadcast_to([P, HA, HD])
                for i in range(NT):
                    num = hb[:, i % 2, :, 0:HD]
                    o_ = ov[:, i, :].rearrange("p (h n) -> p h n", h=HA)
                    pool.wait_ge(mean_ready, i + 1)
                    ch.link(nc.gpsimd.tensor_tensor(num, num, bu(mom[:, 1, :]), ALU.subtract))
                    nc.gpsimd.tensor_tensor(scr[:, :, :], num, num, ALU.mult).then_inc(sq_ready, 1)
                    pool.wait_ge(sq_ready, i + 1)
                    pool.wait_ge(factor_ready, i + 1)
                    ch.link(nc.gpsimd.tensor_tensor(num, num, bu(mom[:, 3, :]), ALU.mult))
                    nc.gpsimd.tensor_tensor(o_, o_, num, ALU.mult).then_inc(y_ready, 1)

            @block.scalar
            def _(act):
                A = nc.scalar.activation
                for q in range(QA):
                    A(kT[:, q, :], qk[:, q, CONV_K - 1:], ACT.Tanh, scale=0.5).then_inc(cv_tanh, 1)
                act.wait_ge(f_ready, 2)
                A(fz[:, :], fz[:, :], ACT.Exp, scale=-1.0).then_inc(f_exp, 1)
                act.wait_ge(f_exp, 1)
                A(fz[:, :], fz[:, :], ACT.Ln, bias=1.0).then_inc(f_ln, 1)
                for g in range(4 * QA):
                    which, rem = divmod(g, 2 * QA)
                    q, hf = divmod(rem, 2)
                    act.wait_ge(qk_done, g + 1)
                    A((qT, kT)[which][:, q, hf * 512:hf * 512 + 512], ps[4 + g % 2][:, :], ACT.Copy,
                      scale=(0.5, 0.0625)[which]).then_inc(qk_taken, 1)
                A(ov, ov, ACT.Tanh, scale=0.5).then_inc(o_tanh, 1)
                for k in range(3):
                    act.wait_ge(arg_ready, k + 1)
                    A(R4[:, k + 1, :], R4[:, k + 1, :], ACT.Exp).then_inc(exps, 1)
                def roots(i):
                    act.wait_ge(var_ready, i + 1)
                    A(mom[:, 2, :], mom[:, 2, :], ACT.Sqrt).then_inc(root, 1)

                act.wait_ge(gc_done, 2)
                A(gcol[:, :, :, :].rearrange("p i k h -> p (i k h)"), ps[6][:, 0:4 * HA * NT], ACT.Copy).then_inc(gc_taken, 1)
                A(dec[:, :, :].rearrange("p q i -> p (q i)"), ps[7][:, 0:QA * NT], ACT.Copy).then_inc(gc_taken, 1)
                act.wait_ge(gc_taken, 2)
                for i in range(NT):
                    act.wait_ge(kt_done, i + 1)
                    if i >= 2:
                        act.wait_ge(c_done, i - 1)
                    A(kw[:, i % 2, :], ps[7][:, 0:DA], ACT.Copy, scale=0.0625).then_inc(kt_taken, 1)
                    for n, h in enumerate(ORDER):
                        act.wait_ge(e_done, 2 * i + n // 3 + 1)
                        if i and n == 0:
                            act.wait_ge(p_ready, 2 * i)
                        A(E[:, n, :], ps[n // 3][:, (n % 3) * P:(n % 3 + 1) * P], ACT.Exp,
                          bias=gcol[:, i, 0, h:h + 1], scale=-1.0).then_inc(e_taken, 1)
                    if i:
                        roots(i - 1)
                roots(NT - 1)
                for g in range(2 * QA):
                    act.wait_ge(yt_done, g + 1)
                    q, hf = divmod(g, 2)
                    A(qk[:, q, hf * 512:hf * 512 + 512], ps[g % 4][:, :], ACT.Copy).then_inc(yt_taken, 1)

            @block.vector
            def _(dve):
                ch = Chain(dve, dve_c)
                V = nc.vector
                L = lambda *a: ch.link(V.tensor_tensor(*a))
                m0, m1, m2, m3 = (mom[:, k, :] for k in range(4))

                def mean(i):
                    hv = hb[:, i % 2, :, :]
                    if i:
                        dve.wait_ge(y_ready, i)
                    dve.wait_ge(h_taken, i + 1)
                    ch.add(V.tensor_reduce(m1, hv[:, :, 0:HD], AX.X, ALU.add))
                    ch.link(V.scalar_tensor_tensor(m0, hv[:, :, HD], -1.0, hv[:, :, HD], ALU.mult, ALU.max))
                    V.tensor_scalar(m1, m1, 1.0 / HD, None, ALU.mult).then_inc(mean_ready, 1)
                    L(m0, m0, gcol[:, i, 2, :], ALU.max)
                    ch.link(V.reciprocal(m0, m0))
                    L(mom[:, 4, :], m0, m0, ALU.mult)

                def variance(i):
                    dve.wait_ge(sq_ready, i + 1)
                    ch.link(V.tensor_reduce(m2, scr[:, :, :], AX.X, ALU.add))
                    L(m2, m2, mom[:, 4, :], ALU.mult)
                    V.tensor_scalar(m2, m2, 1.0 / HD, HEAD_EPS, ALU.mult, ALU.add).then_inc(var_ready, 1)
                    ch.link(V.scalar_tensor_tensor(ov[:, i, :], ov[:, i, :], 1.0, nw[:, :], ALU.add, ALU.mult))

                def factor(i):
                    dve.wait_ge(root, i + 1)
                    ch.link(V.reciprocal(m3, m2))
                    V.scalar_tensor_tensor(m3, m3, 0.5, m0, ALU.mult, ALU.mult).then_inc(factor_ready, 1)

                dve.wait_ge(gt_done, 1)
                for hf in range(2):
                    n = slice(hf * 512, hf * 512 + 512)
                    ch.add(V.tensor_scalar(R4[:, 0, n], ps[hf][0:HA, :], col(t, "b_i")[0:HA, :], None, ALU.add))
                    ch.add(V.tensor_scalar(bc_[:, n], ps[2 + hf][0:HA, :], col(t, "b_f")[0:HA, :], None, ALU.add))
                    ch.sync()
                    V.scalar_tensor_tensor(fz[:, n], bc_[:, n], -1.0, bc_[:, n], ALU.mult, ALU.max).then_inc(f_ready, 1)
                for q in range(QA):
                    dve.wait_ge(cv_tanh, q + 1)
                    V.scalar_tensor_tensor(cx[:, q, :], kT[:, q, :], 1.0, qk[:, q, CONV_K - 1:], ALU.add, ALU.mult
                                           ).then_inc(cx_ready, 1)
                dve.wait_ge(f_ln, 1)
                dve.wait_ge(prep, 4)
                ch.link(V.scalar_tensor_tensor(fz[:, :], bc_[:, :], 0.0, fz[:, :], ALU.min, ALU.subtract))
                ch.link(V.tensor_tensor_scan(bc_[:, :], t["seg64"][0:HA, :], fz[:, :], 0.0, ALU.mult, ALU.add))
                L(R4[:, 0, :], R4[:, 0, :], bc_[:, :], ALU.subtract)
                for i in range(NT):
                    n = slice(i * P, (i + 1) * P)
                    ch.link(V.tensor_tensor_scan(M[0:HA, n], R4[:, 0, n], R4[:, 0, n], mp[:, i:i + 1], ALU.max, ALU.max))
                    L(mp[:, i + 1:i + 2], bc_[:, (i + 1) * P - 1:(i + 1) * P], M[0:HA, (i + 1) * P - 1:(i + 1) * P], ALU.add)
                dve.sem_inc(m_ready, 1)
                c3 = lambda a: a.rearrange("p (i n) -> p i n", i=NT)
                V.tensor_tensor(c3(R4[:, 1, :]), mp[:, 0:NT].unsqueeze(2).broadcast_to([HA, NT, P]), c3(M[0:HA, :]),
                                ALU.subtract).then_inc(arg_ready, 1)
                L(R4[:, 2, :], bc_[:, :], M[0:HA, :], ALU.add)
                V.tensor_scalar(R4[:, 2, :], R4[:, 2, :], -1.0, 80.0, ALU.mult, ALU.min).then_inc(arg_ready, 1)
                V.tensor_tensor(c3(R4[:, 3, :]), c3(R4[:, 0, :]), M[0:HA, P - 1::P].unsqueeze(2).broadcast_to([HA, NT, P]),
                                ALU.subtract).then_inc(arg_ready, 1)
                dve.wait_ge(gc_taken, 2)
                dve.wait_ge(prep, 5 + NT)
                dve.wait_ge(o_tanh, 1)
                h6 = lambda a: a.rearrange("p (h n) -> p h n", h=HA)
                bcast = lambda a, n: a.unsqueeze(2).broadcast_to([P, HA, n])
                for i in range(NT):
                    dve.wait_ge(kt_taken, i + 1)
                    V.tensor_tensor(h6(kw[:, i % 2, :]), h6(kw[:, i % 2, :]), bcast(gcol[:, i, 3, :], HD), ALU.mult
                                    ).then_inc(kw_ready, 1)
                    if i:
                        mean(i - 1)
                    for b in range(2):
                        dve.wait_ge(e_taken, 6 * i + 3 * b + 3)
                        dve.wait_ge(sc_done, 2 * i + b + 1)
                        if i:
                            dve.wait_ge(ia_done, i)
                        V.tensor_tensor(Pm[:, 3 * b:3 * b + 3, :], ps[2 + b][:, 0:384].rearrange("p (h n) -> p h n", h=3),
                                        E[:, 3 * b:3 * b + 3, :], ALU.mult).then_inc(p_ready, 1)
                    if i:
                        variance(i - 1)
                    dve.wait_ge(it_done, i + 1)
                    if i >= 2:
                        dve.wait_ge(y_ready, i - 1)
                    L(hb[:, i % 2, :, :], h6(ps[5][:, 0:HA * W65]), bcast(gcol[:, i, 1, :], W65), ALU.mult)
                    dve.wait_ge(ia_done, i + 1)
                    V.tensor_tensor(hb[:, i % 2, :, :], hb[:, i % 2, :, :], h6(ps[4][:, 0:HA * W65]), ALU.add).then_inc(h_taken, 1)
                    dve.wait_ge(c_done, i + 1)
                    for q in range(QA):
                        for e in range(2):
                            r = slice(64 * e, 64 * e + 64)
                            a = q * 2 * W65 + e * W65
                            ch.add(V.scalar_tensor_tensor(C[r, q, e, :], C[r, q, e, :], dec[r, q, i:i + 1],
                                                          ps[6][r, a:a + W65], ALU.mult, ALU.add))
                    ch.sync()
                    dve.sem_inc(c_ready, 1)
                    if i:
                        factor(i - 1)
                mean(NT - 1)
                variance(NT - 1)
                factor(NT - 1)

            @block.tensor
            def _(pe):
                mm, tr = nc.tensor.matmul, nc.tensor.transpose
                ident = t["ident"]
                for k in range(2):
                    for i in range(NT):
                        last = tr(ps[2 * k + i // 4][0:HA, (i % 4) * P:(i % 4 + 1) * P],
                                  vo[:, i, 2 * DA + k * HA:2 * DA + (k + 1) * HA], ident[:, :])
                last.then_inc(gt_done, 1)
                pe.wait_ge(small_in, 48)
                for g in range(4 * QA):
                    which, rem = divmod(g, 2 * QA)
                    q, hf = divmod(rem, 2)
                    pe.wait_ge(cx_ready, q + 1)
                    if g >= 2:
                        pe.wait_ge(qk_taken, g - 1)
                    mm(ps[4 + g % 2][:, :], wqk[:, which, q, :], cx[:, q, hf * 512:hf * 512 + 512],
                       start=True, stop=True).then_inc(qk_done, 1)
                pe.wait_ge(exps, 3)
                for i in range(NT):
                    for k in range(4):
                        a = (i * 4 + k) * HA
                        last = tr(ps[6][:, a:a + HA], R4[:, k, i * P:(i + 1) * P], ident[0:HA, 0:HA])
                last.then_inc(gc_done, 1)
                for q in range(QA):
                    last = mm(ps[7][:, q * NT:(q + 1) * NT], pair_sel(q), R4[:, 1, P - 1::P], start=True, stop=True)
                last.then_inc(gc_done, 1)
                pe.wait_ge(m_ready, 1)
                pe.wait_ge(qk_taken, 4 * QA)
                pe.wait_ge(prep, 5 + NT)
                pe.wait_ge(gc_taken, 2)
                for i in range(NT):
                    n = slice(i * P, (i + 1) * P)
                    if i:
                        pe.wait_ge(kt_taken, i)
                    for q in range(QA):
                        last = mm(ps[7][:, q * P:(q + 1) * P], cx[:, q, n], wqk[:, 1, q, :], start=True, stop=True)
                    last.then_inc(kt_done, 1)
                    for b in range(2):
                        if i:
                            pe.wait_ge(e_taken, 6 * (i - 1) + 3 * b + 3)
                        for j in range(3):
                            mm(ps[b][:, j * P:(j + 1) * P], ident[:, :], causal, start=True, stop=False)
                            last = mm(ps[b][:, j * P:(j + 1) * P], sel(ORDER[3 * b + j]), M[:, n],
                                      start=False, stop=True)
                        last.then_inc(e_done, 1)
                    for b in range(2):
                        if i:
                            pe.wait_ge(p_ready, 2 * (i - 1) + b + 1)
                        for j in range(3):
                            h = ORDER[3 * b + j]
                            q, r = h // 2, slice(64 * (h % 2), 64 * (h % 2) + 64)
                            last = mm(ps[2 + b][:, j * P:(j + 1) * P], kT[r, q, n], qT[r, q, n], start=True, stop=True)
                        last.then_inc(sc_done, 1)
                    if i:
                        pe.wait_ge(c_ready, i)
                        pe.wait_ge(h_taken, i)
                    for q in range(QA):
                        last = mm(ps[5][:, q * 2 * W65:(q + 1) * 2 * W65], qT[:, q, n],
                                  C[:, q, :, :].rearrange("p e n -> p (e n)"), start=True, stop=True)
                    last.then_inc(it_done, 1)
                    pe.wait_ge(kw_ready, i + 1)
                    for q in range(QA):
                        last = mm(ps[6][:, q * 2 * W65:(q + 1) * 2 * W65], kw[:, i % 2, q * P:(q + 1) * P],
                                  vaug[:, i, 2 * q:2 * q + 2, :].rearrange("p e n -> p (e n)"), start=True, stop=True)
                    last.then_inc(c_done, 1)
                    for s, h in enumerate(ORDER):
                        pe.wait_ge(p_ready, 2 * i + s // 3 + 1)
                        last = mm(ps[4][:, h * W65:(h + 1) * W65], Pm[:, s, :], vaug[:, i, h, :], start=True, stop=True)
                    last.then_inc(ia_done, 1)
                for g in range(2 * QA):
                    q, hf = divmod(g, 2)
                    if g >= 4:
                        pe.wait_ge(yt_taken, g - 3)
                    for j in range(4):
                        i = 4 * hf + j
                        pe.wait_ge(y_ready, i + 1)
                        last = tr(ps[g % 4][:, j * P:(j + 1) * P], ov[:, i, q * P:(q + 1) * P], ident[:, :])
                    last.then_inc(yt_done, 1)


def first_w13(t):
    return t["wout"][:, :, :].rearrange("p (c k) n -> p c (k n)", c=2)


def load_w13(eng, io, t, expert, dst, sem):
    for c, name in enumerate(("moe_w1", "moe_w3")):
        w = io[name].rearrange("o e (p k) n -> p (o e) (k n)", p=P)
        eng.dma_start(dst[:, c, :], w[:, bass.ds(expert, 1), :].rearrange("p a n -> p (a n)")).then_inc(sem, 16)


def phase_e(nc, t, io):
    ps = t["ps"]
    mod, x1 = t["mod2"], t["x1"]
    with ExitStack() as ctx:
        sb = lambda n, s, d=F32: ctx.enter_context(nc.sbuf_tensor(n, s, d, side="right"))
        sem = ctx.enter_context(phase_semaphores(nc))
        wr = sb("pe_wr", [P, KT, NG + NE])
        br = sb("pe_br", [P, NG + NE])
        diag = sb("pe_diag", [P, 2, 512])
        cst = sb("pe_cst", [P, ROUTE_COLS])
        tmp = sb("pe_tmp", [P, 2, D])
        h2 = sb("pe_h2", [P, 2, D])
        hT = sb("pe_hT", [P, 2, KT, P])
        ss = sb("pe_ss", [P, 3, NT])
        lg = sb("pe_lg", [P, NT, NG + NE])
        R = sb("pe_R", [P, 8, NT])
        g4 = sb("pe_g4", [P, 3, NT, NG])
        e32 = sb("pe_e32", [P, 6, NT, NE])
        place = sb("pe_place", [P, 3, 2, NT])
        cum = sb("pe_cum", [P, NT + 1, NE])
        cb = sb("pe_cb", [P, 4, NE])
        ends_by = sb("pe_ends_by", [1, MAXBLK, NE])
        bf = sb("pe_bf", [1, 2, MAXBLK])
        wout_in, x_in = [sem(f"pe_wout{k}") for k in range(2)], [sem(f"pe_x_in{i}") for i in range(NT)]
        diag_ready, row_done, row_taken = sem("pe_diag_ready"), sem("pe_row_done"), sem("pe_row_taken")
        first_expert, first_ready = sb("pe_first", [1, 1], I32), sem("pe_first_ready")
        small_in, cst_in = sem("pe_small_in"), sem("pe_cst_in")
        hot_ready, tab_done = sem("pe_hot_ready"), sem("pe_tab_done")
        mix_done, x1_ready, mix_taken = sem("pe_mix_done"), sem("pe_x1_ready"), sem("pe_mix_taken")
        sq, var_ready, root, h2_ready = sem("pe_sq"), sem("pe_var"), sem("pe_root"), sem("pe_h2_ready")
        h2_out = [sem("pe_h2_out0"), sem("pe_h2_out1")]
        t_done, t_taken, lg_done = sem("pe_t_done"), sem("pe_t_taken"), sem("pe_lg_done")
        x_ready, x_done = sem("pe_x_ready"), sem("pe_x_done")
        cum_ready, rank_done, dve_c = sem("pe_cum"), sem("pe_rank"), sem("pe_dve")
        ltri, ones = cst[:, 0:P], cst[:, P:2 * P]
        w4, w32 = cst[:, 2 * P:2 * P + NG], cst[:, 2 * P + NG:2 * P + NG + NE]
        c0 = 2 * P + NG + NE
        c1 = c0 + NE * MAXBLK + MAXBLK // 2
        jrow = cst[0:1, c0:c0 + NE * MAXBLK].rearrange("p (j e) -> p j e", e=NE)
        prow = cst[0:1, c0 + NE * MAXBLK:c1]
        slot_no, block_no = cst[:, c1:c1 + BT], cst[:, c1 + BT:c1 + BT + MAXBLK]
        c2 = c1 + BT + MAXBLK
        token_no, row_no = cst[:, c2:c2 + 2 * NT], cst[:, c2 + 2 * NT:c2 + 4 * NT]
        spare_row = cst[0:BT, c2 + 4 * NT:c2 + 4 * NT + 1]
        flat = lambda a: a.rearrange("p a b -> p (a b)")
        hot_slot = flat(tmp[:, :, :])[:, 0:2 * NT * BT].rearrange("p (a n) -> p a n", n=BT)
        hot_block = flat(h2[:, :, :])[:, 0:4 * NT * MAXBLK].rearrange("p (a c n) -> p a c n", c=2, n=MAXBLK)

        def lhs(k, i):
            if k < 3:
                return t["qk"][:, k, i * P:(i + 1) * P]
            if k < 6:
                return t["pB"][:, k - 3, 1 + i * P:1 + (i + 1) * P]
            return t["ycT"][:, k - 6, i * P:(i + 1) * P]

        with nc.Block() as block:
            @block.sync
            def _(sp):
                wout = io["w_out"].rearrange("o (k p) n -> p (o k) n", p=P)
                x = io["x"].rearrange("b (i p) d -> p (b i) d", p=P)
                sp.dma_start(cst[:, :], io["route_cst"]).then_inc(cst_in, 16)
                for hf in range(2):
                    n = slice(hf * 512, hf * 512 + 512)
                    sp.dma_start(t["wout"][:, :, n], wout[:, :, n]).then_inc(wout_in[hf], 16)
                for i in range(NT):
                    sp.dma_start(x1[:, i, :], x[:, i, :]).then_inc(x_in[i], 16)
                sp.dma_start(wr[:, :, :], io["w_router"].rearrange("(k p) n -> p k n", p=P)).then_inc(small_in, 16)
                sp.dma_start(br[:, :], io["rows_router"]).then_inc(small_in, 16)
                for i in range(NT):
                    sp.wait_ge(h2_ready, i + 1)
                    sp.dma_start(io["h2"][i * P:(i + 1) * P, :], h2[:, i % 2, :]).then_inc(h2_out[i % 2], 16)
                for u in range(2):
                    sp.wait_ge(h2_out[u], 16 * (NT // 2))
                sp.wait_ge(first_ready, 1)
                sp.wait_ge(mix_done, 2 * NT)
                e = sp.value_load(first_expert[0:1, 0:1], min_val=0, max_val=NE - 1)
                load_w13(sp, io, t, e, first_w13(t), t["first_w13_in"])

            @block.scalar
            def _(act):
                A = nc.scalar.activation
                for n in range(8):
                    act.wait_ge(row_done, n + 1)
                    A(mod[:, n // 2, (n % 2) * 512:(n % 2) * 512 + 512], ps[2 + n % 2][:, :], ACT.Copy).then_inc(row_taken, 1)
                for i in range(NT + 1):
                    if i < NT:
                        act.wait_ge(x1_ready, i + 1)
                        if i:
                            act.wait_ge(sq, i)
                        A(tmp[:, 1, :], x1[:, i, :], ACT.Square, accum_out=ss[:, 0, i:i + 1]).then_inc(sq, 1)
                        act.wait_ge(var_ready, i + 1)
                        A(ss[:, 1, i:i + 1], ss[:, 1, i:i + 1], ACT.Sqrt).then_inc(root, 1)
                    if i:
                        for g in range(2):
                            act.wait_ge(t_done, 2 * (i - 1) + g + 1)
                            if i >= 3:
                                act.wait_ge(lg_done, i - 2)
                            A(hT[:, (i - 1) % 2, 4 * g:4 * g + 4, :], ps[4 + g][:, :].rearrange("p (k n) -> p k n", k=4),
                              ACT.Copy).then_inc(t_taken, 1)
                act.wait_ge(x_ready, 1)
                A(g4[:, 1, :, :], g4[:, 1, :, :], ACT.Exp).then_inc(x_done, 1)
                act.wait_ge(x_ready, 2)
                A(R[:, 5, :], R[:, 5, :], ACT.Exp).then_inc(x_done, 1)

            @block.vector
            def _(dve):
                ch = Chain(dve, dve_c)
                V = nc.vector
                L = lambda *a: ch.link(V.tensor_tensor(*a))
                mc = t["mod_cols"]
                for a in (0, 2, 3):
                    ch.add(V.tensor_scalar(mc[:, a * KT:(a + 1) * KT], mc[:, a * KT:(a + 1) * KT], 1.0, None, ALU.add))
                ch.sync()
                L(mc[:, 2 * KT:3 * KT], mc[:, 2 * KT:3 * KT], col(t, "norm_ffn", 0, KT), ALU.mult)
                for n in range(8):
                    if n >= 2:
                        dve.wait_ge(row_done, n - 1)
                    V.tensor_tensor(diag[:, n % 2, :].rearrange("p (k n) -> p k n", k=4),
                                    t["ident"][:, :].unsqueeze(1).broadcast_to([P, 4, P]),
                                    mc[:, 4 * n:4 * n + 4].unsqueeze(2).broadcast_to([P, 4, P]), ALU.mult
                                    ).then_inc(diag_ready, 1)
                dve.wait_ge(small_in, 32)
                dve.wait_ge(cst_in, 16)
                dve.wait_ge(row_taken, 8)
                for i in range(NT):
                    for hf in range(2):
                        n = slice(hf * 512, hf * 512 + 512)
                        dve.wait_ge(mix_done, 2 * i + hf + 1)
                        V.tensor_tensor(tmp[:, 0, n], ps[hf][:, :], mod[:, 0, n], ALU.mult).then_inc(mix_taken, 1)
                        dve.wait_ge(mix_taken, 2 * i + hf + 1)
                        if hf == 0:
                            dve.wait_ge(x_in[i], 16)
                        ch.add(V.tensor_tensor(x1[:, i, n], x1[:, i, n], tmp[:, 0, n], ALU.add))
                    ch.sync()
                    dve.sem_inc(x1_ready, 1)
                    dve.wait_ge(sq, i + 1)
                    V.tensor_scalar(ss[:, 1, i:i + 1], ss[:, 0, i:i + 1], 1.0 / D, NORM_EPS, ALU.mult, ALU.add
                                    ).then_inc(var_ready, 1)
                    dve.wait_ge(root, i + 1)
                    ch.link(V.reciprocal(ss[:, 2, i:i + 1], ss[:, 1, i:i + 1]))
                    if i >= 2:
                        dve.wait_ge(h2_out[i % 2], 16 * (i // 2))
                        dve.wait_ge(t_done, 2 * (i - 1))
                    ch.link(V.scalar_tensor_tensor(h2[:, i % 2, :], x1[:, i, :], ss[:, 2, i:i + 1], mod[:, 2, :],
                                                   ALU.mult, ALU.mult))
                    V.tensor_tensor(h2[:, i % 2, :], h2[:, i % 2, :], mod[:, 1, :], ALU.add).then_inc(h2_ready, 1)
                    if i:
                        dve.wait_ge(lg_done, i)
                        ch.add(V.tensor_tensor(lg[:, i - 1, :], ps[6 + (i - 1) % 2][:, 0:NG + NE], br[:, :], ALU.add))
                dve.wait_ge(lg_done, NT)
                ch.link(V.tensor_tensor(lg[:, NT - 1, :], ps[6 + (NT - 1) % 2][:, 0:NG + NE], br[:, :], ALU.add))
                lg4, lg32 = lg[:, :, 0:NG], lg[:, :, NG:]
                b3 = lambda a, n: a.unsqueeze(2).broadcast_to([P, NT, n])
                r3 = lambda a, n: a.unsqueeze(1).broadcast_to([P, NT, n])
                ch.link(V.tensor_reduce(R[:, 0, :], lg4, AX.X, ALU.max))
                V.tensor_tensor(g4[:, 1, :, :], lg4, b3(R[:, 0, :], NG), ALU.subtract).then_inc(x_ready, 1)
                L(g4[:, 0, :, :], lg4, b3(R[:, 0, :], NG), ALU.is_equal)
                L(g4[:, 0, :, :], g4[:, 0, :, :], r3(w4, NG), ALU.mult)
                ch.link(V.tensor_reduce(R[:, 0, :], g4[:, 0, :, :], AX.X, ALU.max))
                L(g4[:, 0, :, :], g4[:, 0, :, :], b3(R[:, 0, :], NG), ALU.is_equal)
                ch.link(V.tensor_scalar(g4[:, 2, :, :], g4[:, 0, :, :], -1.0, BIG, ALU.add, ALU.mult))
                dve.wait_ge(x_done, 1)
                ch.link(V.tensor_reduce(R[:, 1, :], g4[:, 1, :, :], AX.X, ALU.add))
                ch.link(V.reciprocal(R[:, 1, :], R[:, 1, :]))
                em = e32[:, 0, :, :]
                for i in range(NT):
                    ch.add(V.tensor_tensor(em[:, i, :].rearrange("p (g e) -> p g e", g=NG),
                                           lg32[:, i, :].rearrange("p (g e) -> p g e", g=NG),
                                           g4[:, 2, i, :].unsqueeze(2).broadcast_to([P, NG, EPG]), ALU.add))
                ch.sync()

                def first_largest(oh, src, m):
                    ch.link(V.tensor_reduce(m, src, AX.X, ALU.max))
                    L(oh, src, b3(m, NE), ALU.is_equal)
                    L(oh, oh, r3(w32, NE), ALU.mult)
                    ch.link(V.tensor_reduce(R[:, 7, :], oh, AX.X, ALU.max))
                    L(oh, oh, b3(R[:, 7, :], NE), ALU.is_equal)

                oh1, oh2 = e32[:, 1, :, :], e32[:, 2, :, :]
                first_largest(oh1, em, R[:, 2, :])
                ch.link(V.scalar_tensor_tensor(em, oh1, -3 * BIG, em, ALU.mult, ALU.add))
                first_largest(oh2, em, R[:, 3, :])
                V.tensor_tensor(R[:, 5, :], R[:, 3, :], R[:, 2, :], ALU.subtract).then_inc(x_ready, 1)
                L(e32[:, 3, :, :], oh1, oh2, ALU.add)
                ch.add(V.memset(cum[:, 0, :], 0.0))
                ch.sync()
                for i in range(NT):
                    L(cum[:, i + 1, :], cum[:, i, :], e32[:, 3, i, :], ALU.add)
                dve.sem_inc(cum_ready, 1)
                dve.wait_ge(x_done, 2)
                ch.link(V.tensor_scalar(R[:, 4, :], R[:, 5, :], 1.0, None, ALU.add))
                ch.link(V.reciprocal(R[:, 4, :], R[:, 4, :]))
                L(t["wts"][:, 0, :], R[:, 1, :], R[:, 4, :], ALU.mult)
                L(t["wts"][:, 1, :], t["wts"][:, 0, :], R[:, 5, :], ALU.mult)
                dve.wait_ge(rank_done, 1)
                cnt, nb, end, base = (cb[:, k, :] for k in range(4))
                ch.add(V.tensor_copy(cnt, ps[1][:, 0:NE]))
                ch.link(V.memset(nb, 0.0))
                for k in range(-(-S // BT)):
                    ch.link(V.scalar_tensor_tensor(nb, cnt, float(BT * k), nb, ALU.is_gt, ALU.add))
                ch.link(V.tensor_tensor_scan(end, ones[:, 0:NE], nb, 0.0, ALU.mult, ALU.add))
                ch.link(V.tensor_scalar(bf[:, 1, 0:NE], end[0:1, :], 0.0, None, ALU.is_le))
                ch.link(V.tensor_reduce(bf[:, 0, 0:1], bf[:, 1, 0:NE], AX.X, ALU.add))
                V.tensor_copy(first_expert[:, :], bf[:, 0, 0:1]).then_inc(first_ready, 1)
                L(base, end, nb, ALU.subtract)
                ranks = ps[0][:, 0:NT * NE].rearrange("p (i e) -> p i e", e=NE)
                for k, oh in enumerate((oh1, oh2)):
                    L(e32[:, 5, :, :], oh, ranks, ALU.mult)
                    ch.link(V.tensor_reduce(place[:, 0, k, :], e32[:, 5, :, :], AX.X, ALU.add))
                    L(e32[:, 4, :, :], oh, r3(base, NE), ALU.mult)
                    ch.link(V.tensor_reduce(place[:, 1, k, :], e32[:, 4, :, :], AX.X, ALU.add))
                rank, first_block, b_in = (place[:, k, :, :] for k in range(3))
                ch.link(V.tensor_scalar(b_in, rank, float(BT), None, ALU.is_ge))
                for k in range(2, -(-S // BT)):
                    ch.link(V.scalar_tensor_tensor(b_in, rank, float(BT * k), b_in, ALU.is_ge, ALU.add))
                ch.link(V.scalar_tensor_tensor(rank, b_in, -float(BT), rank, ALU.mult, ALU.add))
                L(first_block, first_block, b_in, ALU.add)
                for u in range(2):
                    dve.wait_ge(h2_out[u], 16 * (NT // 2))
                slot, blk_ = flat(rank), flat(first_block)
                over = lambda a, n: a.unsqueeze(2).broadcast_to([P, 2 * NT, n])
                row = flat(b_in)
                L(row, row_no, slot, ALU.subtract)
                ch.add(V.tensor_tensor(hot_slot, slot_no.unsqueeze(1).broadcast_to([P, 2 * NT, BT]), over(slot, BT),
                                       ALU.is_equal))
                L(hot_block[:, :, 0, :], block_no.unsqueeze(1).broadcast_to([P, 2 * NT, MAXBLK]), over(blk_, MAXBLK),
                  ALU.is_equal)
                L(hot_block[:, :, 1, :], hot_block[:, :, 0, :], over(row, MAXBLK), ALU.mult)
                L(hot_block[:, :, 0, :], hot_block[:, :, 0, :], over(token_no, MAXBLK), ALU.mult)
                dve.sem_inc(hot_ready, 1)
                L(ends_by[:, :, :], end[0:1, :].unsqueeze(1).broadcast_to([1, MAXBLK, NE]), jrow, ALU.is_le)
                ch.link(V.tensor_reduce(bf[:, 0, :], ends_by[:, :, :], AX.X, ALU.add))
                ch.link(V.tensor_scalar(bf[:, 0, :], bf[:, 0, :], float(NE - 1), None, ALU.min))
                ch.link(V.tensor_copy(t["blk"][:, 0:MAXBLK], bf[:, 0, :]))
                ch.link(V.tensor_scalar(bf[:, 1, 0:MAXBLK // 2], prow, end[0:1, NE - 1:NE], None, ALU.is_lt))
                ch.link(V.tensor_reduce(bf[:, 0, 0:1], bf[:, 1, 0:MAXBLK // 2], AX.X, ALU.add))
                for k in range(1, 4):
                    ch.link(V.tensor_scalar(bf[:, 0, k:k + 1], bf[:, 0, 0:1], -float(k), None, ALU.add))
                ch.add(V.tensor_copy(t["blk"][:, MAXBLK:MAXBLK + 4], bf[:, 0, 0:4]))
                dve.wait_ge(tab_done, 1)
                V.tensor_copy(t["tab"][:, :, 0], ps[2][0:BT, 0:MAXBLK])
                V.tensor_scalar(t["tab"][:, :, 1], ps[2][0:BT, MAXBLK:2 * MAXBLK], spare_row, None, ALU.add)

            @block.tensor
            def _(pe):
                def turn(i):
                    pe.wait_ge(h2_ready, i + 1)
                    for g in range(2):
                        if i:
                            pe.wait_ge(t_taken, 2 * (i - 1) + g + 1)
                        for k in range(4):
                            last = nc.tensor.transpose(ps[4 + g][:, k * P:(k + 1) * P],
                                                       h2[:, i % 2, (4 * g + k) * P:(4 * g + k + 1) * P], t["ident"][:, :])
                        last.then_inc(t_done, 1)

                def logits(i):
                    pe.wait_ge(t_taken, 2 * (i + 1))
                    for k in range(KT):
                        last = nc.tensor.matmul(ps[6 + i % 2][:, 0:NG + NE], hT[:, i % 2, k, :], wr[:, k, :],
                                                start=(k == 0), stop=(k == KT - 1))
                    last.then_inc(lg_done, 1)

                def mix(i, hf):
                    if i == 0:
                        pe.wait_ge(wout_in[hf], 16)
                    if i:
                        pe.wait_ge(mix_taken, 2 * (i - 1) + hf + 1)
                    for k in range(KT):
                        last = nc.tensor.matmul(ps[hf][:, :], lhs(k, i), t["wout"][:, k, hf * 512:hf * 512 + 512],
                                                start=(k == 0), stop=(k == KT - 1))
                    last.then_inc(mix_done, 1)

                pe.wait_ge(cst_in, 16)
                for n in range(8):
                    pe.wait_ge(diag_ready, n + 1)
                    if n >= 2:
                        pe.wait_ge(row_taken, n - 1)
                    nc.tensor.matmul(ps[2 + n % 2][:, :], ones, diag[:, n % 2, :], start=True, stop=True
                                     ).then_inc(row_done, 1)
                for i in range(NT):
                    mix(i, 0)
                    if i >= 2:
                        logits(i - 2)
                    mix(i, 1)
                    if i == 1:
                        pe.wait_ge(small_in, 32)
                    if i:
                        turn(i - 1)
                logits(NT - 2)
                turn(NT - 1)
                logits(NT - 1)
                pe.wait_ge(cum_ready, 1)
                ranks = ps[0][:, 0:NT * NE]
                nc.tensor.matmul(ranks, ltri, flat(e32[:, 3, :, :]), start=True, stop=False)
                nc.tensor.matmul(ranks, ones, flat(cum[:, 0:NT, :]), start=False, stop=True)
                nc.tensor.matmul(ps[1][:, 0:NE], ones, cum[:, NT, :], start=True, stop=True).then_inc(rank_done, 1)
                pe.wait_ge(hot_ready, 1)
                for a in range(2 * NT):
                    last = nc.tensor.matmul(ps[2][0:BT, 0:2 * MAXBLK], hot_slot[:, a, :],
                                            hot_block[:, a, :, :].rearrange("p c n -> p (c n)"),
                                            start=(a == 0), stop=(a == 2 * NT - 1))
                last.then_inc(tab_done, 1)


def phase_moe(nc, t, io):
    ps = t["ps"]
    KF = DE // P
    with ExitStack() as ctx:
        sb = lambda n, s, d=F32: ctx.enter_context(nc.sbuf_tensor(n, s, d))
        sem = ctx.enter_context(phase_semaphores(nc))
        w13 = first_w13(t), sb("mo_w13", [P, 2, KT * DE])
        w2 = sb("mo_w2", [P, 2, KF, D])
        token_id = sb("mo_token", [BT, 2], I32)
        row_id = sb("mo_row", [BT, 2], I32)
        xg = sb("mo_xg", [BT, 2, D])
        xT = sb("mo_xT", [P, 2, KT, BT])
        th = sb("mo_th", [P, 2, KF * BT])
        hh = sb("mo_hh", [P, 2, KF * BT])
        yb = sb("mo_y", [BT, 2, D])
        w13_in = t["first_w13_in"], sem("mo_w13_in1")
        w2_in = [sem(f"mo_w2_in{u}") for u in range(2)]
        x_in = [sem(f"mo_x_in{u}") for u in range(2)]
        y_out = [sem(f"mo_y_out{u}") for u in range(2)]
        token_ready, row_ready, held = sem("mo_token"), sem("mo_row"), sem("mo_held")
        t_done, t_taken = sem("mo_t_done"), sem("mo_t_taken")
        a_done, h_done, tanh_done, hh_ready = sem("mo_a_done"), sem("mo_h_done"), sem("mo_tanh"), sem("mo_hh")
        y_done, y_taken, dve_c = sem("mo_y_done"), sem("mo_y_taken"), sem("mo_dve")
        ident, blk, tab = t["ident"], t["blk"], t["tab"]
        x_banks, h_banks, y_banks = (ps[0], ps[1]), ((ps[2], ps[3]), (ps[4], ps[7])), (ps[5], ps[6])
        W2 = io["moe_w2"].rearrange("o e (k p) n -> p (o e) k n", p=P)

        def rounds_less(eng, k):
            return eng.value_load(blk[0:1, MAXBLK + k:MAXBLK + k + 1], min_val=1, max_val=MAXBLK // 2 - k)

        def at(r, u):
            return 2 * r + u

        def expert(eng, r, u):
            return eng.value_load(blk[0:1, bass.ds(at(r, u), 1)], min_val=0, max_val=NE - 1)

        with nc.Block() as block:
            @block.sync
            def _(sp):
                def load(r, u, before=None):
                    e = expert(sp, r, u)
                    if before is not None:
                        sp.wait_ge(h_done, at(before, u) + 1)
                    load_w13(sp, io, t, e, w13[u], w13_in[u])

                n = rounds_less(sp, 1)
                sp.wait_ge(x_in[0], 16)
                load(0, 1)
                with sp.Fori(0, n) as r:
                    load(r + 1, 0, r)
                    load(r + 1, 1, r)

            @block.gpsimd
            def _(pool):
                def gather(r, u, before=None):
                    if before is not None:
                        pool.wait_ge(t_done, 2 * at(before, u) + 2)
                    nc.gpsimd.tensor_copy(token_id[:, u:u + 1], tab[:, bass.ds(at(r, u), 1), 0]).then_inc(token_ready, 1)
                    pool.wait_ge(token_ready, at(r, u) + 1)
                    pool.sem_inc(held, 1)
                    nc.gpsimd.indirect_dma_start(
                        out=xg[:, u, :], out_offset=None, in_=io["h2"],
                        in_offset=bass.IndirectOffsetOnAxis(ap=token_id[:, u:u + 1], axis=0)).then_inc(x_in[u], 16)

                def scatter(r, u, before=None):
                    pool.wait_ge(y_taken, 2 * at(r, u) + 2)
                    nc.gpsimd.tensor_copy(row_id[:, u:u + 1], tab[:, bass.ds(at(r, u), 1), 1]).then_inc(row_ready, 1)
                    pool.wait_ge(row_ready, at(r, u) + 1)
                    if before is not None:
                        pool.wait_ge(y_out[1 - u], 16 * before + 16)
                    pool.sem_inc(held, 1)
                    nc.gpsimd.indirect_dma_start(
                        out=io["y_rows"], out_offset=bass.IndirectOffsetOnAxis(ap=row_id[:, u:u + 1], axis=0),
                        in_=yb[:, u, :], in_offset=None).then_inc(y_out[u], 16)

                n, n2 = rounds_less(pool, 1), rounds_less(pool, 2)
                gather(0, 0)
                gather(0, 1)
                gather(1, 0, 0)
                scatter(0, 0)
                gather(1, 1, 0)
                scatter(0, 1, 0)
                with pool.Fori(0, n2) as r:
                    gather(r + 2, 0, r + 1)
                    scatter(r + 1, 0, r)
                    gather(r + 2, 1, r + 1)
                    scatter(r + 1, 1, r + 1)
                scatter(n, 0, n2)
                scatter(n, 1, n)
                for u in range(2):
                    pool.wait_ge(y_out[u], 16 * n + 16)

            @block.scalar
            def _(act):
                A = nc.scalar.activation

                def load_w2(r, u, before=None):
                    e = expert(act, r, u)
                    if before is not None:
                        act.wait_ge(y_done, 2 * at(before, u) + 2)
                    act.dma_start(w2[:, u, :, :], W2[:, bass.ds(e, 1), :, :].rearrange("p a k n -> p (a k) n")
                                  ).then_inc(w2_in[u], 16)

                def tokens(r, u):
                    for g in range(2):
                        act.wait_ge(t_done, 2 * at(r, u) + g + 1)
                        A(xT[:, u, 4 * g:4 * g + 4, :], x_banks[g][:, 0:4 * BT].rearrange("p (k n) -> p k n", k=4), ACT.Copy
                          ).then_inc(t_taken, 1)

                def tanh(r, u):
                    act.wait_ge(a_done, at(r, u) + 1)
                    A(th[:, u, :], h_banks[u][0][:, 0:KF * BT], ACT.Tanh, scale=0.5).then_inc(tanh_done, 1)

                n, n2 = rounds_less(act, 1), rounds_less(act, 2)
                tokens(0, 0)
                load_w2(0, 0)
                load_w2(0, 1)
                tanh(0, 0)
                tokens(0, 1)
                tanh(0, 1)
                tokens(1, 0)
                load_w2(1, 0, 0)
                with act.Fori(0, n2) as r:
                    tanh(r + 1, 0)
                    tokens(r + 1, 1)
                    load_w2(r + 1, 1, r)
                    tanh(r + 1, 1)
                    tokens(r + 2, 0)
                    load_w2(r + 2, 0, r + 1)
                tanh(n, 0)
                tokens(n, 1)
                load_w2(n, 1, n2)
                tanh(n, 1)

            @block.vector
            def _(dve):
                V = nc.vector

                def swiglu(r, u):
                    a, b = (bank[:, 0:KF * BT] for bank in h_banks[u])
                    dve.wait_ge(tanh_done, at(r, u) + 1)
                    V.scalar_tensor_tensor(hh[:, u, :], th[:, u, :], 1.0, a, ALU.add, ALU.mult).then_inc(dve_c, 1)
                    dve.wait_ge(dve_c, at(r, u) + 1)
                    dve.wait_ge(h_done, at(r, u) + 1)
                    V.tensor_tensor(hh[:, u, :], hh[:, u, :], b, ALU.mult).then_inc(hh_ready, 1)

                def result(r, u, before=None):
                    if before is not None:
                        dve.wait_ge(y_out[u], 16 * before + 16)
                    for g in range(2):
                        n = slice(g * 512, g * 512 + 512)
                        dve.wait_ge(y_done, 2 * at(r, u) + g + 1)
                        V.scalar_tensor_tensor(yb[:, u, n], y_banks[g][0:BT, :], 0.5, t["mod2"][0:BT, 3, n],
                                               ALU.mult, ALU.mult).then_inc(y_taken, 1)

                n, n2, n3 = (rounds_less(dve, k) for k in range(1, 4))
                swiglu(0, 0)
                swiglu(0, 1)
                result(0, 0)
                swiglu(1, 0)
                result(0, 1)
                swiglu(1, 1)
                result(1, 0, 0)
                with dve.Fori(0, n3) as r:
                    swiglu(r + 2, 0)
                    result(r + 1, 1, r)
                    swiglu(r + 2, 1)
                    result(r + 2, 0, r + 1)
                swiglu(n, 0)
                result(n2, 1, n3)
                swiglu(n, 1)
                result(n, 0, n2)
                result(n, 1, n2)

            @block.tensor
            def _(pe):
                mm, tr = nc.tensor.matmul, nc.tensor.transpose

                def tokens(r, u, before=None):
                    pe.wait_ge(x_in[u], 16 * r + 16)
                    for g in range(2):
                        if before is not None:
                            pe.wait_ge(t_taken, 2 * before + 1 + g)
                        for k in range(4):
                            last = tr(x_banks[g][:, k * BT:(k + 1) * BT], xg[:, u, 4 * g + k::KT], ident[0:BT, 0:BT])
                        last.then_inc(t_done, 1)

                def first(r, u, before=None):
                    pe.wait_ge(t_taken, 2 * at(r, u) + 2)
                    pe.wait_ge(w13_in[u], 32 * r + 32)
                    if before is not None:
                        pe.wait_ge(hh_ready, at(before, u) + 1)
                    for c, done in enumerate((a_done, h_done)):
                        for m in range(KF):
                            for k in range(KT):
                                last = mm(h_banks[u][c][:, m * BT:(m + 1) * BT],
                                          w13[u][:, c, k * DE + m * P:k * DE + (m + 1) * P], xT[:, u, k, :],
                                          start=(k == 0), stop=(k == KT - 1))
                        last.then_inc(done, 1)

                def second(r, u, before=None):
                    pe.wait_ge(hh_ready, at(r, u) + 1)
                    pe.wait_ge(w2_in[u], 16 * r + 16)
                    for g in range(2):
                        if before is not None:
                            pe.wait_ge(y_taken, 2 * before + 1 + g)
                        for k in range(KF):
                            last = mm(y_banks[g][0:BT, :], hh[:, u, k * BT:(k + 1) * BT], w2[:, u, k, g * 512:g * 512 + 512],
                                      start=(k == 0), stop=(k == KF - 1))
                        last.then_inc(y_done, 1)

                n, n2 = rounds_less(pe, 1), rounds_less(pe, 2)
                tokens(0, 0)
                first(0, 0)
                tokens(0, 1, 0)
                first(0, 1)
                tokens(1, 0, 1)
                second(0, 0)
                with pe.Fori(0, n2) as r:
                    first(r + 1, 0, r)
                    tokens(r + 1, 1, at(r + 1, 0))
                    second(r, 1, at(r, 0))
                    first(r + 1, 1, r)
                    tokens(r + 2, 0, at(r + 1, 1))
                    second(r + 1, 0, at(r, 1))
                first(n, 0, n2)
                tokens(n, 1, at(n, 0))
                second(n2, 1, at(n2, 0))
                first(n, 1, n2)
                second(n, 0, at(n2, 1))
                second(n, 1, at(n, 0))


def phase_out(nc, t, io):
    x1 = t["x1"]
    with ExitStack() as ctx:
        sb = lambda n, s, d=F32: ctx.enter_context(nc.sbuf_tensor(n, s, d))
        sem = ctx.enter_context(phase_semaphores(nc))
        nf = sb("po_nf", [P, D])
        yg = sb("po_y", [P, NT, 2, D])
        sq_out = sb("po_sq", [P, D])
        ss = sb("po_ss", [P, 3, NT])
        nf_in, y_in = sem("po_nf_in"), [sem(f"po_y_in{i}") for i in range(NT)]
        x2_ready, sq, var_ready, root, o_ready, out_done = (sem("po_x2"), sem("po_sqs"), sem("po_var"), sem("po_root"),
                                                            sem("po_o"), sem("po_out"))
        inv_ready, scaled, dve_c = sem("po_inv"), sem("po_scaled"), sem("po_dve")
        out = io["out"].rearrange("b (i p) d -> p (b i) d", p=P)
        with nc.Block() as block:
            @block.sync
            def _(sp):
                sp.dma_start(nf[:, :], io["rows_norm"]).then_inc(nf_in, 16)
                for i in range(NT):
                    for k in range(2):
                        sp.dma_start(yg[:, i, k, :], io["y_rows"][k * S + i * P:k * S + (i + 1) * P, :]
                                     ).then_inc(y_in[i], 16)
                for i in range(NT):
                    sp.wait_ge(o_ready, i + 1)
                    sp.dma_start(out[:, i, :], x1[:, i, :]).then_inc(out_done, 16)
                sp.wait_ge(out_done, 16 * NT)

            @block.gpsimd
            def _(pool):
                pool.wait_ge(nf_in, 16)
                for i in range(NT):
                    pool.wait_ge(scaled, i + 1)
                    nc.gpsimd.tensor_tensor(x1[:, i, :], x1[:, i, :], nf[:, :], ALU.mult).then_inc(o_ready, 1)

            @block.scalar
            def _(act):
                def scale(i):
                    act.wait_ge(inv_ready, i + 1)
                    nc.scalar.activation(x1[:, i, :], x1[:, i, :], ACT.Copy, scale=ss[:, 2, i:i + 1]).then_inc(scaled, 1)

                for i in range(NT):
                    act.wait_ge(x2_ready, i + 1)
                    if i:
                        act.wait_ge(sq, i)
                    nc.scalar.activation(sq_out[:, :], x1[:, i, :], ACT.Square, accum_out=ss[:, 0, i:i + 1]).then_inc(sq, 1)
                    act.wait_ge(var_ready, i + 1)
                    nc.scalar.activation(ss[:, 1, i:i + 1], ss[:, 1, i:i + 1], ACT.Sqrt).then_inc(root, 1)
                    if i:
                        scale(i - 1)
                scale(NT - 1)

            @block.vector
            def _(dve):
                ch = Chain(dve, dve_c)
                V = nc.vector

                def finish(i):
                    dve.wait_ge(sq, i + 1)
                    V.tensor_scalar(ss[:, 1, i:i + 1], ss[:, 0, i:i + 1], 1.0 / D, NORM_EPS, ALU.mult, ALU.add
                                    ).then_inc(var_ready, 1)
                    dve.wait_ge(root, i + 1)
                    V.reciprocal(ss[:, 2, i:i + 1], ss[:, 1, i:i + 1]).then_inc(inv_ready, 1)

                for i in range(NT):
                    dve.wait_ge(y_in[i], 32)
                    a, b = yg[:, i, 0, :], yg[:, i, 1, :]
                    ch.link(V.scalar_tensor_tensor(x1[:, i, :], a, t["wts"][:, 0, i:i + 1], x1[:, i, :], ALU.mult, ALU.add))
                    V.scalar_tensor_tensor(x1[:, i, :], b, t["wts"][:, 1, i:i + 1], x1[:, i, :], ALU.mult, ALU.add
                                           ).then_inc(x2_ready, 1)
                    if i:
                        finish(i - 1)
                finish(NT - 1)


def build_program(nc, io):
    io["h2"] = nc.dram_tensor("h2_rows", (S, D), F32, kind="Internal").ap()
    io["y_rows"] = nc.dram_tensor("y_rows", (2 * S + BT, D), F32, kind="Internal").ap()
    with ExitStack() as ctx:
        def put(stack, name, shape, dtype=F32, side="left"):
            t[name] = stack.enter_context(nc.sbuf_tensor(name, shape, dtype, side=side))

        t = {"ps": [ctx.enter_context(nc.psum_tensor(f"bank{i}", [P, 512], F32)) for i in range(8)]}
        put(ctx, "ident", [P, P])
        with ExitStack() as late, ExitStack() as mix:
            put(mix, "cols", [P, NCOLS])
            put(mix, "cond", [P, KT])
            put(mix, "mod_cols", [P, 4 * KT])
            put(mix, "ycT", [P, 2, S])
            with ExitStack() as heads:
                with ExitStack() as norm, phase_semaphores(nc) as sem:
                    t["ring_in"] = [sem("ring_in0"), sem("ring_in1")]
                    put(norm, "hT", [P, KT, S], side="right")
                    put(norm, "ring", [P, 2, KT, VO // 2], side="right")
                    phase_norm1(nc, t, io)
                    put(mix, "pB", [P, 11, 1 + S])
                    phase_a(nc, t, io)
                    put(mix, "qk", [P, QA, CONV_K - 1 + S])
                    put(heads, "a_til", [P, QB, S])
                    put(heads, "b_hat", [P, QB, S])
                    put(heads, "bonus", [P, NT, HB])
                    put(heads, "chunk_decay", [P, QB, S // HD])
                    put(heads, "vo", [P, NT, VO])
                    put(heads, "seg64", [P, S])
                    phase_b(nc, t, io)
                phase_c(nc, t, io)
                phase_d(nc, t, io)
            put(late, "x1", [P, NT, D], side="right")
            put(late, "mod2", [P, 4, D], side="right")
            put(late, "wts", [P, 2, NT], side="right")
            put(late, "blk", [1, MAXBLK + 4], I32, side="right")
            put(late, "tab", [BT, MAXBLK, 2], I32, side="right")
            put(late, "wout", [P, KT, D], side="right")
            with phase_semaphores(nc) as sem:
                t["first_w13_in"] = sem("first_w13_in")
                phase_e(nc, t, io)
                mix.close()
                phase_moe(nc, t, io)
            phase_out(nc, t, io)


def host_layout(inp):
    f = np.float32
    a = {k: np.asarray(v) for k, v in inp.items()}
    tile_cols = lambda v: v.reshape(-1, P).T
    cols = np.zeros((P, NCOLS), f)

    def put(name, v):
        lo, hi = COLS[name]
        cols[:v.shape[0], lo:hi] = v

    put("c", tile_cols(a["c"][0]))
    put("conv_w", a["mlstm_conv_w"][0].reshape(CONV_K, QA, P).transpose(2, 1, 0).reshape(P, -1))
    put("conv_b", tile_cols(a["mlstm_conv_b"][0]))
    put("mu", tile_cols(a["rwkv_mu"][0]))
    for name, key in (("w0", "rwkv_w0"), ("a0", "rwkv_a0"), ("k_k", "rwkv_k_k"), ("k_a", "rwkv_k_a"),
                      ("r_k", "rwkv_r_k")):
        put(name, tile_cols(a[key][0].reshape(-1)))
    put("a_re", tile_cols(a["s5_a_re"][0].reshape(-1)))
    put("a_im", tile_cols(a["s5_a_im"][0].reshape(-1)))
    put("log_dt", tile_cols(np.repeat(a["s5_log_dt"][0], P5)))
    put("d5", a["s5_d"][0].reshape(G5, GC).T)
    put("glu_b", tile_cols(a["s5_glu_b"][0]))
    put("ada_b", tile_cols(a["ada_b"].reshape(-1)))
    put("norm_mix", tile_cols(a["norm_mix"].reshape(-1)))
    put("norm_ffn", tile_cols(a["norm_ffn"].reshape(-1)))
    put("b_i", a["mlstm_b_i"][0][:, None])
    put("b_f", a["mlstm_b_f"][0][:, None])
    s5 = np.zeros((P, 4, QS, GC), f)
    for e in range(2):
        r = slice(e * P5, (e + 1) * P5)
        s5[r, 0] = a["s5_b_re"][0][e::2].transpose(1, 0, 2)
        s5[r, 1] = a["s5_b_im"][0][e::2].transpose(1, 0, 2)
        s5[r, 2] = a["s5_c_re"][0][e::2].transpose(2, 0, 1)
        s5[r, 3] = a["s5_c_im"][0][e::2].transpose(2, 0, 1)
    rows = lambda *v: np.ascontiguousarray(np.broadcast_to(np.concatenate([x.reshape(-1) for x in v]), (P, sum(x.size for x in v))))
    rwkv_cst = np.zeros((P, P + 2), f)
    for e in range(2):
        rwkv_cst[e * HD:(e + 1) * HD, e * HD:(e + 1) * HD] = 1.0
        rwkv_cst[e * HD:(e + 1) * HD, P + e] = 1.0
    s_, t_ = np.arange(P)[:, None], np.arange(P)[None, :]
    same = lambda n: s_ // n == t_ // n
    strict, incl = ((s_ < t_) & same(HD)), ((s_ <= t_) & same(HD))
    u16, rest, l16 = (s_ < t_) & same(16), strict & ~same(16), (s_ > t_) & same(16)
    rwkv_masks = np.concatenate([incl, strict, incl] + [u16] * 3 + [rest] * 3 + [l16] * 3, axis=1).astype(f)
    mc = np.zeros((P, HA + QA + 1, P), f)
    wqk = np.zeros((P, 2, QA, P), f)
    for h in range(HA):
        q, e = divmod(h, 2)
        r = slice(e * HD, (e + 1) * HD)
        mc[h, h, :] = 1.0
        mc[h, HA + q, r] = 1.0
        wqk[r, 0, q, r] = a["mlstm_w_q"][0][h]
        wqk[r, 1, q, r] = a["mlstm_w_k"][0][h]
    mc[:, HA + QA:, :] = np.where(s_ > t_, f(BIG), f(0))[:, None, :]
    route = np.zeros((P, ROUTE_COLS), f)
    route[:, 0:P] = s_ < t_
    route[:, P:2 * P] = 1.0
    route[:, 2 * P:2 * P + NG] = NG - np.arange(NG)
    route[:, 2 * P + NG:2 * P + NG + NE] = NE - np.arange(NE)
    c0 = 2 * P + NG + NE
    route[0, c0:c0 + NE * MAXBLK] = np.repeat(np.arange(MAXBLK), NE)
    c1 = c0 + NE * MAXBLK + MAXBLK // 2
    route[0, c0 + NE * MAXBLK:c1] = 2 * np.arange(MAXBLK // 2)
    token = np.arange(NT)[None, :] * P + np.arange(P)[:, None]
    ends = np.cumsum([c1, BT, MAXBLK, 2 * NT, 2 * NT, 1])
    for lo, hi, v in zip(ends[:-1], ends[1:], (np.arange(BT), np.arange(MAXBLK), np.concatenate([token, token], axis=1),
                                               np.concatenate([token - 2 * S, token - S], axis=1),
                                               2 * S + np.arange(P)[:, None])):
        route[:, lo:hi] = v
    out = {
        "moe_w1": a["moe_w1"], "moe_w3": a["moe_w3"], "moe_w2": a["moe_w2"], "w_out": a["w_out"],
        "w_router": np.concatenate([a["moe_w_rg"][0], a["moe_w_re"][0]], axis=1),
        "rows_router": rows(a["moe_b_rg"], a["moe_b_re"]), "route_cst": route,
        "mlstm_cst": mc.reshape(P, -1), "wqk": wqk, "rows_mlstm": rows(a["mlstm_norm_w"]),
        "rwkv_masks": rwkv_masks, "rows_rwkv": rows(a["rwkv_ln_w"], a["rwkv_ln_b"]), "g_up": a["rwkv_g_up"][0],
        "lora": np.concatenate([a["rwkv_w_up"][0], a["rwkv_a_up"][0]]), "rwkv_cst": rwkv_cst,
        "glu_w": a["s5_glu_w"],
        "x": a["x"], "ada_w": a["ada_w"], "w_in": a["w_in"],
        "cols": cols, "ident": np.eye(P, dtype=f),
        "rows_norm": rows(a["norm_final"]),
        "s5_bc": s5,
    }
    return out


def kernel(**inputs):
    import concourse.bacc as bacc
    from concourse.bass_utils import run_bass_kernel_spmd

    nc = bacc.Bacc("TRN2", target_bir_lowering=False, num_devices=1)
    arrays, io = {}, {}
    for name, a in host_layout(inputs).items():
        a = np.ascontiguousarray(a)
        arrays[f"in_{name}"] = a
        io[name] = nc.dram_tensor(f"in_{name}", a.shape, mybir.dt.from_np(a.dtype), kind="ExternalInput").ap()
    io["out"] = nc.dram_tensor("out_y", (1, S, D), F32, kind="ExternalOutput").ap()
    build_program(nc, io)
    r = run_bass_kernel_spmd(nc, [arrays], core_ids=[0])
    return r.results[0]["out_y"]
```
